# Optimizing a Trainium2 kernel written in Bass

```python
import math
import jax, jax.numpy as jnp
from jax import lax
import numpy as np

D_MODEL = 1024
BATCH = 1
SEQ = 256
DEPTH = 1

N_META = 16
HEAD_DIM = 64
SWA_Q_HEADS = D_MODEL // (2 * HEAD_DIM)
SWA_KV_HEADS = max(SWA_Q_HEADS // 4, 1)
SWA_GROUP = SWA_Q_HEADS // SWA_KV_HEADS
FOX_HEADS = D_MODEL // (2 * HEAD_DIM)
SWA_Q_W = SWA_Q_HEADS * HEAD_DIM
SWA_KV_W = SWA_KV_HEADS * HEAD_DIM
FOX_W = FOX_HEADS * HEAD_DIM
D_MIX = SWA_Q_W + FOX_W
OFF_QA = SWA_Q_W
OFF_KA = OFF_QA + SWA_KV_W
OFF_VA = OFF_KA + SWA_KV_W
OFF_QB = OFF_VA + FOX_W
OFF_KB = OFF_QB + FOX_W
OFF_VB = OFF_KB + FOX_W
D_PROJ = OFF_VB + FOX_HEADS
WINDOW = 128
BLOCK = 128
N_BUCKETS = 32
MAX_DISTANCE = 128
D_FF = -(-8 * D_MODEL // (3 * 256)) * 256
EPS = 1e-6
NEG_INF = -1e30


def rms_norm(x, g):
    xf = x.astype(jnp.float32)
    y = xf * lax.rsqrt(jnp.mean(xf * xf, axis=-1, keepdims=True) + EPS)
    return (y * g.astype(jnp.float32)).astype(x.dtype)

def t5_bucket(dist):
    n = jnp.maximum(dist, 0).astype(jnp.int32)
    max_exact = N_BUCKETS // 2
    nf = jnp.maximum(n, 1).astype(jnp.float32)
    large = max_exact + (jnp.log(nf / max_exact) / math.log(MAX_DISTANCE / max_exact)
                         * (N_BUCKETS - max_exact)).astype(jnp.int32)
    large = jnp.minimum(large, N_BUCKETS - 1)
    return jnp.where(n < max_exact, n, large)

def softmax_with_sink(s, sink):
    sink_r = sink.reshape((1,) + sink.shape + (1,) * (s.ndim - 3))
    col = jnp.broadcast_to(sink_r, s.shape[:-1] + (1,))
    p = jax.nn.softmax(jnp.concatenate([s, col], axis=-1), axis=-1)
    return p[..., :-1]

def swa_sink_attention(q, k, v, sinks, rel_bias):
    B, L = q.shape[0], q.shape[1]
    n_blk = (L - N_META) // BLOCK
    scale = HEAD_DIM ** -0.5
    sink = sinks.astype(jnp.float32).reshape(SWA_KV_HEADS, SWA_GROUP)
    tab = rel_bias.astype(jnp.float32)
    mi = jnp.arange(N_META)
    km, vm = k[:, :N_META], v[:, :N_META]

    qm = q[:, :N_META].reshape(B, N_META, SWA_KV_HEADS, SWA_GROUP, HEAD_DIM)
    d_mm = mi[:, None] - mi[None, :]
    b_mm = tab[t5_bucket(d_mm)].transpose(2, 0, 1).reshape(SWA_KV_HEADS, SWA_GROUP, N_META, N_META)
    s_mm = jnp.einsum('bqhgd,bkhd->bhgqk', qm, km, preferred_element_type=jnp.float32) * scale + b_mm
    s_mm = jnp.where(d_mm >= 0, s_mm, NEG_INF)
    p_mm = softmax_with_sink(s_mm, sink).astype(v.dtype)
    o_meta = jnp.einsum('bhgqk,bkhd->bqhgd', p_mm, vm).reshape(B, N_META, SWA_Q_HEADS, HEAD_DIM)

    qr = q[:, N_META:].reshape(B, n_blk, BLOCK, SWA_KV_HEADS, SWA_GROUP, HEAD_DIM)
    kr = k[:, N_META:].reshape(B, n_blk, BLOCK, SWA_KV_HEADS, HEAD_DIM)
    vr = v[:, N_META:].reshape(B, n_blk, BLOCK, SWA_KV_HEADS, HEAD_DIM)

    def with_prev(t):
        prev = jnp.pad(t, ((0, 0), (1, 0), (0, 0), (0, 0), (0, 0)))[:, :-1]
        return jnp.concatenate([prev, t], axis=2)

    kw, vw = with_prev(kr), with_prev(vr)
    qi = jnp.arange(BLOCK)[:, None]
    ki = jnp.arange(2 * BLOCK)[None, :]
    d_w = qi + BLOCK - ki
    b_w = tab[t5_bucket(d_w)].transpose(2, 0, 1).reshape(SWA_KV_HEADS, SWA_GROUP, 1, BLOCK, 2 * BLOCK)
    blk = jnp.arange(n_blk)[:, None, None]
    valid_w = ((d_w >= 0) & (d_w < WINDOW))[None] & ((blk > 0) | (ki >= BLOCK)[None])
    s_w = jnp.einsum('bnqhgd,bnkhd->bhgnqk', qr, kw, preferred_element_type=jnp.float32) * scale + b_w
    s_w = jnp.where(valid_w, s_w, NEG_INF)
    d_m = N_META + blk * BLOCK + qi[None] - mi[None, None, :]
    b_m = tab[t5_bucket(d_m)].transpose(3, 0, 1, 2).reshape(SWA_KV_HEADS, SWA_GROUP, n_blk, BLOCK, N_META)
    s_m = jnp.einsum('bnqhgd,bmhd->bhgnqm', qr, km, preferred_element_type=jnp.float32) * scale + b_m
    p = softmax_with_sink(jnp.concatenate([s_m, s_w], axis=-1), sink).astype(v.dtype)
    o = (jnp.einsum('bhgnqm,bmhd->bnqhgd', p[..., :N_META], vm)
         + jnp.einsum('bhgnqk,bnkhd->bnqhgd', p[..., N_META:], vw))
    o_real = o.reshape(B, n_blk * BLOCK, SWA_Q_HEADS, HEAD_DIM)
    return jnp.concatenate([o_meta, o_real], axis=1)

def forgetting_attention(q, k, v, f_logit):
    B, L = q.shape[0], q.shape[1]
    n_blk = (L - N_META) // BLOCK
    scale = HEAD_DIM ** -0.5
    cum = jnp.cumsum(jax.nn.log_sigmoid(f_logit.astype(jnp.float32)), axis=1).transpose(0, 2, 1)

    mi = jnp.arange(N_META)
    s = jnp.einsum('bqhd,bkhd->bhqk', q[:, :N_META], k[:, :N_META], preferred_element_type=jnp.float32) * scale
    s = s + cum[:, :, :N_META, None] - cum[:, :, None, :N_META]
    s = jnp.where(mi[:, None] >= mi[None, :], s, NEG_INF)
    p = jax.nn.softmax(s, axis=-1).astype(v.dtype)
    o_meta = jnp.einsum('bhqk,bkhd->bqhd', p, v[:, :N_META])

    qb = q[:, N_META:].reshape(B, n_blk, BLOCK, FOX_HEADS, HEAD_DIM).transpose(1, 0, 2, 3, 4)
    cb = cum[:, :, N_META:].reshape(B, FOX_HEADS, n_blk, BLOCK).transpose(2, 0, 1, 3)
    k_pos = jnp.arange(L)

    def one_block(args):
        q_blk, c_blk, b = args
        q_pos = N_META + b * BLOCK + jnp.arange(BLOCK)
        sb = jnp.einsum('bqhd,bkhd->bhqk', q_blk, k, preferred_element_type=jnp.float32) * scale
        sb = sb + c_blk[..., None] - cum[:, :, None, :]
        sb = jnp.where(k_pos[None, :] <= q_pos[:, None], sb, NEG_INF)
        pb = jax.nn.softmax(sb, axis=-1).astype(v.dtype)
        return jnp.einsum('bhqk,bkhd->bqhd', pb, v)

    o = lax.map(one_block, (qb, cb, jnp.arange(n_blk)))
    o_real = o.transpose(1, 0, 2, 3, 4).reshape(B, n_blk * BLOCK, FOX_HEADS, HEAD_DIM)
    return jnp.concatenate([o_meta, o_real], axis=1)

def first_inputs(seed: int = 0) -> dict:
    key = jax.random.key(seed)
    ks = jax.random.split(key, 14)
    f32 = jnp.float32
    gain = lambda k: 1.0 + 0.05 * jax.random.normal(k, (DEPTH, D_MODEL), f32)
    return {
        "x": jax.random.normal(ks[0], (BATCH, SEQ, D_MODEL), f32),
        "meta_tokens": jax.random.normal(ks[1], (N_META, D_MODEL), f32),
        "rel_bias": 0.5 * jax.random.normal(ks[2], (N_BUCKETS, SWA_Q_HEADS), f32),
        "ln_pre_mix": gain(ks[3]),
        "ln_post_mix": gain(ks[4]),
        "ln_pre_ffn": gain(ks[5]),
        "ln_post_ffn": gain(ks[6]),
        "w_in": jax.random.normal(ks[7], (DEPTH, D_MODEL, D_PROJ), f32) * D_MODEL ** -0.5,
        "b_forget": jax.random.uniform(ks[8], (DEPTH, FOX_HEADS), f32, minval=1.0, maxval=5.0),
        "sinks": 0.5 * jax.random.normal(ks[9], (DEPTH, SWA_Q_HEADS), f32),
        "w_out": jax.random.normal(ks[10], (DEPTH, D_MIX, D_MODEL), f32) * D_MIX ** -0.5,
        "w_gate_up": jax.random.normal(ks[11], (DEPTH, D_MODEL, 2 * D_FF), f32) * D_MODEL ** -0.5,
        "w_down": jax.random.normal(ks[12], (DEPTH, D_FF, D_MODEL), f32) * D_FF ** -0.5,
    }

def first_block(x, meta_tokens, rel_bias, ln_pre_mix, ln_post_mix, ln_pre_ffn, ln_post_ffn,
              w_in, b_forget, sinks, w_out, w_gate_up, w_down):
    B = x.shape[0]
    meta = jnp.broadcast_to(meta_tokens[None].astype(x.dtype), (B, N_META, D_MODEL))
    h = jnp.concatenate([meta, x], axis=1)
    L = h.shape[1]
    for layer in range(DEPTH):
        hn = rms_norm(h, ln_pre_mix[layer])
        proj = jnp.einsum('bld,dc->blc', hn, w_in[layer])
        q_a = proj[..., :OFF_QA].reshape(B, L, SWA_Q_HEADS, HEAD_DIM)
        k_a = proj[..., OFF_QA:OFF_KA].reshape(B, L, SWA_KV_HEADS, HEAD_DIM)
        v_a = proj[..., OFF_KA:OFF_VA].reshape(B, L, SWA_KV_HEADS, HEAD_DIM)
        q_b = proj[..., OFF_VA:OFF_QB].reshape(B, L, FOX_HEADS, HEAD_DIM)
        k_b = proj[..., OFF_QB:OFF_KB].reshape(B, L, FOX_HEADS, HEAD_DIM)
        v_b = proj[..., OFF_KB:OFF_VB].reshape(B, L, FOX_HEADS, HEAD_DIM)
        f_b = proj[..., OFF_VB:] + b_forget[layer].astype(proj.dtype)
        o_a = swa_sink_attention(q_a, k_a, v_a, sinks[layer], rel_bias)
        o_b = forgetting_attention(q_b, k_b, v_b, f_b)
        mix = jnp.concatenate([o_a.reshape(B, L, SWA_Q_W), o_b.reshape(B, L, FOX_W)], axis=-1)
        h = h + rms_norm(jnp.einsum('blc,cd->bld', mix, w_out[layer]), ln_post_mix[layer])
        hn = rms_norm(h, ln_pre_ffn[layer])
        gu = jnp.einsum('bld,df->blf', hn, w_gate_up[layer])
        ff = jnp.einsum('blf,fd->bld', jax.nn.silu(gu[..., :D_FF]) * gu[..., D_FF:], w_down[layer])
        h = h + rms_norm(ff, ln_post_ffn[layer])
    return h[:, N_META:]


ROPE_THETA = 10000.0
NEG_INF_2 = -1e30

SWA_HEADS = 8
SWA_KV_HEADS_2 = 2
SWA_GROUP_2 = SWA_HEADS // SWA_KV_HEADS_2
SWA_HEAD_DIM = 64
SWA_WINDOW = 128
SWA_BLOCK = 128

MLA_HEADS = 8
MLA_Q_RANK = 256
MLA_KV_RANK = 128
MLA_NOPE_DIM = 64
MLA_ROPE_DIM = 32
MLA_V_DIM = 64
MLA_QK_DIM = MLA_NOPE_DIM + MLA_ROPE_DIM
MLA_Q_BLOCK = 128

SWA_WIDTH = SWA_HEADS * SWA_HEAD_DIM
MLA_WIDTH = MLA_HEADS * MLA_V_DIM
MIX_WIDTH = SWA_WIDTH + MLA_WIDTH

IN_SIZES = (SWA_HEADS * SWA_HEAD_DIM,
            SWA_KV_HEADS_2 * SWA_HEAD_DIM,
            SWA_KV_HEADS_2 * SWA_HEAD_DIM,
            MLA_Q_RANK,
            MLA_KV_RANK,
            MLA_ROPE_DIM)
IN_WIDTH = int(sum(IN_SIZES))
IN_SPLITS = tuple(int(v) for v in np.cumsum(IN_SIZES)[:-1])

PEER_HEADS = 8
PEER_N_KEYS = 128
PEER_EXPERTS = PEER_N_KEYS * PEER_N_KEYS
PEER_QUERY_DIM = 256
PEER_HALF_DIM = PEER_QUERY_DIM // 2
PEER_TOPK = 16
PEER_TOKEN_BLOCK = 128

N_MOD = 6


def rmsnorm(x, gain=None):
    xf = x.astype(jnp.float32)
    y = xf * lax.rsqrt(jnp.mean(xf * xf, axis=-1, keepdims=True) + EPS)
    if gain is not None:
        y = y * gain.astype(jnp.float32)
    return y.astype(x.dtype)

def modulate(h, shift, scale):
    return h * (1.0 + scale[:, None, :]) + shift[:, None, :]

def rope_tables(seq, dim):
    inv = 1.0 / (ROPE_THETA ** (jnp.arange(0, dim, 2, dtype=jnp.float32) / dim))
    ang = jnp.arange(seq, dtype=jnp.float32)[:, None] * inv[None, :]
    return jnp.cos(ang), jnp.sin(ang)

def apply_rope(x, cos, sin):
    xf = x.astype(jnp.float32)
    half = xf.shape[-1] // 2
    x1, x2 = xf[..., :half], xf[..., half:]
    c = cos[None, :, None, :]
    s = sin[None, :, None, :]
    return jnp.concatenate([x1 * c - x2 * s, x2 * c + x1 * s], axis=-1).astype(x.dtype)

def windowed_gqa(q, k, v, sink):
    B, S = q.shape[0], q.shape[1]
    nb = S // SWA_BLOCK
    cos, sin = rope_tables(S, SWA_HEAD_DIM)
    q = apply_rope(q, cos, sin)
    k = apply_rope(k, cos, sin)
    qb = q.reshape(B, nb, SWA_BLOCK, SWA_KV_HEADS_2, SWA_GROUP_2, SWA_HEAD_DIM)
    pad = ((0, 0), (SWA_BLOCK, SWA_BLOCK), (0, 0), (0, 0))
    kp = jnp.pad(k, pad).reshape(B, nb + 2, SWA_BLOCK, SWA_KV_HEADS_2, SWA_HEAD_DIM)
    vp = jnp.pad(v, pad).reshape(B, nb + 2, SWA_BLOCK, SWA_KV_HEADS_2, SWA_HEAD_DIM)
    kb = jnp.concatenate([kp[:, :-2], kp[:, 1:-1], kp[:, 2:]], axis=2)
    vb = jnp.concatenate([vp[:, :-2], vp[:, 1:-1], vp[:, 2:]], axis=2)
    scores = jnp.einsum('bnqhgd,bnkhd->bnhgqk', qb, kb).astype(jnp.float32) * (SWA_HEAD_DIM ** -0.5)
    q_off = jnp.arange(SWA_BLOCK)[:, None]
    k_off = jnp.arange(3 * SWA_BLOCK)[None, :] - SWA_BLOCK
    band = jnp.abs(k_off - q_off) <= SWA_WINDOW
    k_pos = (jnp.arange(nb) * SWA_BLOCK)[:, None] + k_off
    valid = (k_pos >= 0) & (k_pos < S)
    mask = band[None, :, :] & valid[:, None, :]
    scores = jnp.where(mask[None, :, None, None], scores, NEG_INF_2)
    sink_l = jnp.broadcast_to(sink.astype(jnp.float32).reshape(1, 1, SWA_KV_HEADS_2, SWA_GROUP_2, 1, 1),
                              scores.shape[:-1] + (1,))
    probs = jax.nn.softmax(jnp.concatenate([scores, sink_l], axis=-1), axis=-1)[..., :-1]
    out = jnp.einsum('bnhgqk,bnkhd->bnqhgd', probs.astype(v.dtype), vb)
    return out.reshape(B, S, SWA_WIDTH)

def latent_attention(q_lat, kv_lat, k_rope_raw, q_norm, w_q_up, kv_norm, w_kv_up):
    B, S = q_lat.shape[0], q_lat.shape[1]
    nb = S // MLA_Q_BLOCK
    cos, sin = rope_tables(S, MLA_ROPE_DIM)
    q = (rmsnorm(q_lat, q_norm) @ w_q_up).reshape(B, S, MLA_HEADS, MLA_QK_DIM)
    q_nope = q[..., :MLA_NOPE_DIM]
    q_rope = apply_rope(q[..., MLA_NOPE_DIM:], cos, sin)
    kv = (rmsnorm(kv_lat, kv_norm) @ w_kv_up).reshape(B, S, MLA_HEADS, MLA_NOPE_DIM + MLA_V_DIM)
    k_nope = kv[..., :MLA_NOPE_DIM]
    v = kv[..., MLA_NOPE_DIM:]
    k_rope = apply_rope(k_rope_raw[:, :, None, :], cos, sin)[:, :, 0, :]
    scale = MLA_QK_DIM ** -0.5
    qn_blocks = q_nope.reshape(B, nb, MLA_Q_BLOCK, MLA_HEADS, MLA_NOPE_DIM).transpose(1, 0, 2, 3, 4)
    qr_blocks = q_rope.reshape(B, nb, MLA_Q_BLOCK, MLA_HEADS, MLA_ROPE_DIM).transpose(1, 0, 2, 3, 4)

    def attend(blk):
        qn, qr = blk
        s = (jnp.einsum('bqhd,bkhd->bhqk', qn, k_nope)
             + jnp.einsum('bqhd,bkd->bhqk', qr, k_rope)).astype(jnp.float32) * scale
        p = jax.nn.softmax(s, axis=-1).astype(v.dtype)
        return jnp.einsum('bhqk,bkhd->bqhd', p, v)

    out = lax.map(attend, (qn_blocks, qr_blocks))
    return out.transpose(1, 0, 2, 3, 4).reshape(B, S, MLA_WIDTH)

def peer(h, w_query, sub_keys, expert_u, expert_v):
    B, S, D = h.shape
    blocks = h.reshape((B * S) // PEER_TOKEN_BLOCK, PEER_TOKEN_BLOCK, D)

    def block(xb):
        q = (xb @ w_query).reshape(PEER_TOKEN_BLOCK, PEER_HEADS, 2, PEER_HALF_DIM)
        s = jnp.einsum('chpd,hpnd->chpn', q, sub_keys).astype(jnp.float32)
        top_s, top_i = lax.top_k(s, PEER_TOPK)
        cand_s = (top_s[:, :, 0, :, None] + top_s[:, :, 1, None, :]).reshape(
            PEER_TOKEN_BLOCK, PEER_HEADS, PEER_TOPK * PEER_TOPK)
        cand_i = (top_i[:, :, 0, :, None] * PEER_N_KEYS + top_i[:, :, 1, None, :]).reshape(
            PEER_TOKEN_BLOCK, PEER_HEADS, PEER_TOPK * PEER_TOPK)
        best_s, pos = lax.top_k(cand_s, PEER_TOPK)
        idx = jnp.take_along_axis(cand_i, pos, axis=-1)
        g = jax.nn.softmax(best_s, axis=-1)
        u = expert_u[idx]
        act = jax.nn.gelu(jnp.einsum('cd,chkd->chk', xb, u).astype(jnp.float32), approximate=False)
        w = (g * act).astype(xb.dtype)
        return jnp.einsum('chk,chkd->cd', w, expert_v[idx])

    return lax.map(block, blocks).reshape(B, S, D)

def second_inputs(seed: int = 0) -> dict:
    key = jax.random.key(seed)
    ks = jax.random.split(key, 20)
    f32 = jnp.float32
    nrm = lambda k, shape, s: jax.random.normal(k, shape, f32) * s
    L, D = DEPTH, D_MODEL
    return {
        "x": nrm(ks[0], (BATCH, SEQ, D), 1.0),
        "c": nrm(ks[1], (BATCH, D), 1.0),
        "w_ada": nrm(ks[2], (L, D, N_MOD * D), D ** -0.5),
        "b_ada": nrm(ks[3], (L, N_MOD * D), 0.01),
        "w_in": nrm(ks[4], (L, D, IN_WIDTH), D ** -0.5),
        "swa_sink": nrm(ks[5], (L, SWA_HEADS), 0.5),
        "mla_q_norm": 1.0 + nrm(ks[6], (L, MLA_Q_RANK), 0.02),
        "w_mla_q_up": nrm(ks[7], (L, MLA_Q_RANK, MLA_HEADS * MLA_QK_DIM), MLA_Q_RANK ** -0.5),
        "mla_kv_norm": 1.0 + nrm(ks[8], (L, MLA_KV_RANK), 0.02),
        "w_mla_kv_up": nrm(ks[9], (L, MLA_KV_RANK, MLA_HEADS * (MLA_NOPE_DIM + MLA_V_DIM)), MLA_KV_RANK ** -0.5),
        "out_norm_swa": 1.0 + nrm(ks[10], (L, SWA_WIDTH), 0.02),
        "out_norm_mla": 1.0 + nrm(ks[11], (L, MLA_WIDTH), 0.02),
        "w_out": nrm(ks[12], (L, MIX_WIDTH, D), MIX_WIDTH ** -0.5),
        "w_peer_query": nrm(ks[13], (L, D, PEER_HEADS * PEER_QUERY_DIM), D ** -0.5),
        "peer_sub_keys": nrm(ks[14], (L, PEER_HEADS, 2, PEER_N_KEYS, PEER_HALF_DIM), PEER_HALF_DIM ** -0.5),
        "peer_expert_u": nrm(ks[15], (L, PEER_EXPERTS, D), D ** -0.5),
        "peer_expert_v": nrm(ks[16], (L, PEER_EXPERTS, D), PEER_HEADS ** -0.5),
        "final_norm": 1.0 + nrm(ks[17], (D,), 0.02),
    }

def second_block(x, c, w_ada, b_ada, w_in, swa_sink, mla_q_norm, w_mla_q_up, mla_kv_norm, w_mla_kv_up,
              out_norm_swa, out_norm_mla, w_out, w_peer_query, peer_sub_keys, peer_expert_u,
              peer_expert_v, final_norm):
    B, S, D = x.shape
    c_act = jax.nn.silu(c)
    for l in range(DEPTH):
        mod = c_act @ w_ada[l] + b_ada[l]
        sh_a, sc_a, g_a, sh_f, sc_f, g_f = jnp.split(mod, N_MOD, axis=-1)

        h = modulate(rmsnorm(x), sh_a, sc_a)
        proj = h @ w_in[l]
        qa, ka, va, q_lat, kv_lat, k_rope_raw = jnp.split(proj, IN_SPLITS, axis=-1)
        o_a = windowed_gqa(qa.reshape(B, S, SWA_HEADS, SWA_HEAD_DIM),
                           ka.reshape(B, S, SWA_KV_HEADS_2, SWA_HEAD_DIM),
                           va.reshape(B, S, SWA_KV_HEADS_2, SWA_HEAD_DIM),
                           swa_sink[l])
        o_b = latent_attention(q_lat, kv_lat, k_rope_raw, mla_q_norm[l], w_mla_q_up[l],
                               mla_kv_norm[l], w_mla_kv_up[l])
        mixed = jnp.concatenate([rmsnorm(o_a, out_norm_swa[l]), rmsnorm(o_b, out_norm_mla[l])], axis=-1)
        x = x + g_a[:, None, :] * (mixed @ w_out[l])

        h = modulate(rmsnorm(x), sh_f, sc_f)
        x = x + g_f[:, None, :] * peer(h, w_peer_query[l], peer_sub_keys[l], peer_expert_u[l], peer_expert_v[l])
    return rmsnorm(x, final_norm)


def setup_inputs(seed=0):
    out = dict(first_inputs(seed))
    for name, value in second_inputs(seed + 1).items():
        if name != "x":
            out[name + "_2"] = value
    return out


def reference(
    x, meta_tokens, rel_bias, ln_pre_mix, ln_post_mix, ln_pre_ffn, ln_post_ffn, w_in, b_forget,
    sinks, w_out, w_gate_up, w_down, c_2, w_ada_2, b_ada_2, w_in_2, swa_sink_2, mla_q_norm_2,
    w_mla_q_up_2, mla_kv_norm_2, w_mla_kv_up_2, out_norm_swa_2, out_norm_mla_2, w_out_2,
    w_peer_query_2, peer_sub_keys_2, peer_expert_u_2, peer_expert_v_2, final_norm_2,
):
    x = first_block(
        x, meta_tokens, rel_bias, ln_pre_mix, ln_post_mix, ln_pre_ffn, ln_post_ffn, w_in,
        b_forget, sinks, w_out, w_gate_up, w_down,
    )
    return second_block(
        x, c_2, w_ada_2, b_ada_2, w_in_2, swa_sink_2, mla_q_norm_2, w_mla_q_up_2, mla_kv_norm_2,
        w_mla_kv_up_2, out_norm_swa_2, out_norm_mla_2, w_out_2, w_peer_query_2, peer_sub_keys_2,
        peer_expert_u_2, peer_expert_v_2, final_norm_2,
    )


_drawn_inputs = setup_inputs


def setup_inputs(seed=0):
    import zlib

    import numpy as np

    out = dict(_drawn_inputs(seed))
    spreads = {}
    factors = {'sinks': 8.0,
     'b_ada_2': 4.651,
     'swa_sink_2': 8.0,
     'mla_q_norm_2': 8.0,
     'mla_kv_norm_2': 8.0,
     'out_norm_swa_2': 102.644,
     'out_norm_mla_2': 106.204,
     'final_norm_2': 20.724,
     'w_peer_query_2': 5.998,
     'peer_sub_keys_2': 6.145,
     'peer_expert_u_2': 6.957,
     'peer_expert_v_2': 6.133}
    for name, (base, spread) in spreads.items():
        noise = np.random.default_rng([zlib.crc32(name.encode()), seed]).standard_normal(out[name].shape)
        drawn = base * np.exp(spread * noise) if base else spread * noise
        out[name] = __import__('jax').numpy.asarray(drawn.astype(out[name].dtype))
    for name, factor in factors.items():
        out[name] = (out[name] * factor).astype(out[name].dtype)
    return out
```

```python
from contextlib import ExitStack

import numpy as np

import concourse.bass as bass
from concourse import mybir

F32 = mybir.dt.float32
U32 = mybir.dt.uint32
ALU = mybir.AluOpType
ACT = mybir.ActivationFunctionType
AX_X = mybir.AxisListType.X

P = 128
D = 1024
DC = D // P
SEQ = 256
META = 16
N1 = SEQ + META
N2 = SEQ
HEADS = 8
DH = 64
FF = 2816
FC = FF // P
EPS = 1e-6
NEG = -1e30
LOWEST = -3.0e38
WINDOW = 128
BUCKETS = 32
MAX_DISTANCE = 128

NOPE = 64
ROPE = 32
QK = NOPE + ROPE
QR_C = 2
KEYS = 128
TOPK = 16
PAIRS = HEADS * TOPK

TILE_COLS = [(0, P), (P, P), (2 * P, META)]

RING = 8
N_QK1, N_V1, N_OUT, N_ADA, N_QK2, N_V2, N_QUERY, N_SUB = 13, 5, DC, 6 * DC, 9, 1, 16, 2
N_FFN, N_DOWN = 2 * FC, FC
T_QK1 = 0
T_V1 = T_QK1 + N_QK1
T_ADA = T_V1 + N_V1
T_OUT1 = T_ADA + N_ADA
T_FFN = T_OUT1 + N_OUT
T_DOWN = T_FFN + N_FFN
T_QK2 = T_DOWN + N_DOWN
T_V2 = T_QK2 + N_QK2
T_OUT2 = T_V2 + N_V2
T_QUERY = T_OUT2 + N_OUT
T_SUB = T_QUERY + N_QUERY
N_STREAM = T_SUB + N_SUB
assert N_STREAM % RING == 0

VEC = {}
_at = 0
for _name, _n in (("pre_mix", DC), ("post_mix", DC), ("pre_ffn", DC), ("post_ffn", DC), ("b_ada", 6 * DC),
                  ("q_norm", QR_C), ("kv_norm", 1), ("out_norm", DC), ("final", DC), ("cond", DC),
                  ("sinks1", HEADS), ("sinks2", HEADS)):
    VEC[_name] = (_at, _n)
    _at += _n
N_VEC = _at

SLOT_HEAD = [c + 4 * half for c in range(4) for half in range(2)]

BIAS_OWN = (0, 255, 0, -127)
BIAS_PREV = (255, 255, P, -127)
BIAS_META1 = (510, 143, META + P, -127)
BIAS_META0 = (653, 143, META, -127)
BIAS_MM = (796, 31, 0, -15)
N_BIAS = 827

CONST = {}
_at = 0
for _name, _n in (("ident", P), ("iota", P), ("flip", P), ("rot64", P), ("rot32", P), ("cos64", N2), ("sin64", N2),
                  ("cos32", N2), ("sin32", N2), ("causal1", N1), ("causal0", N1 - P), ("causalm", META),
                  ("band1", N2), ("band0", N2), ("select", HEADS * P), ("bucket", N_BIAS), ("bmask", N_BIAS)):
    CONST[_name] = (_at, _n)
    _at += _n
N_CONST = _at


def bucket_of(d):
    n = np.maximum(d, 0)
    exact = BUCKETS // 2
    nf = np.maximum(n, 1).astype(np.float32)
    large = exact + (np.log(nf / np.float32(exact)) / np.float32(np.log(MAX_DISTANCE / exact))
                     * np.float32(BUCKETS - exact)).astype(np.int32)
    return np.where(n < exact, n, np.minimum(large, BUCKETS - 1))


def shape_constants():
    out = np.zeros((P, N_CONST), np.float32)

    def put(name, a):
        at, n = CONST[name]
        assert a.shape[1] == n
        out[:a.shape[0], at:at + n] = a

    row = np.arange(P)
    put("ident", np.eye(P))
    put("iota", np.broadcast_to(row.astype(np.float32), (P, P)))
    put("flip", np.eye(P)[::-1])
    pos = np.concatenate([np.arange(P, 2 * P), np.arange(P)]).astype(np.float32)
    for dim in (64, 32):
        half = dim // 2
        inv = (1.0 / (np.float32(10000.0) ** (np.arange(0, dim, 2, dtype=np.float32) / np.float32(dim)))).astype(np.float32)
        ang = (inv[row % half][:, None] * pos[None, :]).astype(np.float32)
        put(f"cos{dim}", np.cos(ang))
        put(f"sin{dim}", np.sin(ang))
        rot = np.zeros((P, P), np.float32)
        for i in range(P):
            if i % dim < half:
                rot[i + half, i] = -1.0
            else:
                rot[i - half, i] = 1.0
        put(f"rot{dim}", rot)
    q = row[:, None]
    k = row[None, :]
    causal = np.where(k <= q, 0.0, NEG)
    put("causal1", np.concatenate([causal, np.zeros((P, P + META))], 1))
    put("causal0", np.concatenate([causal, np.zeros((P, META))], 1))
    put("causalm", causal[:META, :META])
    both = np.concatenate([k + P, k], 1)
    put("band1", np.where(np.abs(both - (q + P)) <= WINDOW, 0.0, NEG))
    put("band0", np.where(np.abs(both - q) <= WINDOW, 0.0, NEG))
    sel = np.zeros((HEADS, HEADS, P), np.float32)
    for h in range(HEADS):
        sel[h, h] = -1.0
    put("select", sel.reshape(HEADS, HEADS * P))
    hot = np.zeros((BUCKETS, N_BIAS), np.float32)
    mask = np.zeros((HEADS, N_BIAS), np.float32)
    for at, n, d0, u0 in (BIAS_OWN, BIAS_PREV, BIAS_META1, BIAS_META0, BIAS_MM):
        d = d0 - (np.arange(n) + u0)
        hot[bucket_of(d), at + np.arange(n)] = 1.0
        dead = d < 0
        if (at, n, d0, u0) in (BIAS_OWN, BIAS_PREV):
            dead |= d >= WINDOW
        hot[:, at:at + n][:, dead] = 0.0
        mask[:, at:at + n][:, dead] = NEG
    put("bucket", hot)
    put("bmask", mask)
    return out


def build(nc, x_t, weights, up_experts, down_experts, small, vectors, w_f, b_f, rel, const, scratch, out):
    ctx = ExitStack()
    with ctx:
        def sb(name, shape, dt=F32):
            return ctx.enter_context(nc.sbuf_tensor(name, shape, dt))

        ring = sb("ring", [P, RING, D])
        resid = sb("resid", [P, DC, N1])
        normed = sb("normed", [P, DC, N1])
        rstd = sb("rstd", [P, N1])
        log_ms = sb("log_ms", [P, N1])
        eps = sb("eps", [P, 1])
        vec = sb("vec", [P, N_VEC])
        modv = sb("modv", [P, 6 * DC])
        cond_act = sb("cond_act", [P, DC])
        ident = sb("ident", [P, P])
        iota = sb("iota", [P, P])
        ones = sb("ones", [P, P])
        idx1_t = sb("idx1_t", [P, N2])
        idx2_t = sb("idx2_t", [P, N2])
        gate_t = sb("gate_t", [P, N2])
        zeros = sb("zeros", [P, 512])
        hot1 = sb("hot1", [P, 8, P])
        hot2 = sb("hot2", [P, 8, P])
        act_sb = sb("act_sb", [P, 4, N2])
        picked = sb("picked", [P, 4, N2])
        arena = sb("arena", [P, KEYS * N2])
        gates = arena[:, :].rearrange("p (k n) -> p k n", n=N2)
        used = [0]

        def part(cols):
            at = used[0]
            used[0] += cols
            assert used[0] <= KEYS * N2
            return arena[:, at:at + cols]

        def part3(a, b):
            return part(a * b).rearrange("p (a b) -> p a b", b=b)

        consts = part(N_CONST)

        def cst(name, rows=P):
            at, n = CONST[name]
            return consts[0:rows, at:at + n]

        squares = part3(DC, N1)
        qk = part3(N_QK1, N1)
        k_mla = qk[:, 0:HEADS, 0:N2]
        v_nat = part3(3, N_V1 * P)
        small_sb = part(QR_C * HEADS * QK + HEADS * (NOPE + DH))
        w_f_sb = part3(DC, HEADS)
        bf_sb = part(1)
        rel_sb = part(HEADS)
        cum_q = part3(3, HEADS)
        stats = [part(16) for _ in range(2)]
        probs_t = [part3(3, 4 * P) for _ in range(2)]

        def overlay(at, *shapes):
            after, used[0] = used[0], at
            made = [part3(*n) for n in shapes]
            used[0] = max(used[0], after)
            return made

        here = used[0]
        score = [part3(4, N1 + 2) for _ in range(2)]
        silu_sb, = overlay(here, (4, N1))
        here = used[0]
        mixed = part3(DC, N1)
        f_work, = overlay(here, (6, N1))
        here = used[0]
        lin_out = part3(DC, N1)
        bias_vec = arena[:, here:here + N_BIAS]
        here = used[0]
        bias1, fox1 = part3(HEADS, N1), part3(HEADS, N1)
        bias0, fox0 = part3(HEADS, N1 - P), part3(HEADS, N1 - P)
        biasm, foxm = part3(HEADS, META), part3(HEADS, META)
        ffn_act, = overlay(here, (FC, N1))
        rope_tmp, rope_tmp2, q_mla = overlay(here, (DC, N2), (DC, N2), (HEADS, N2))
        used[0] = N_CONST
        query = part3(16, N2)
        keys_s = part3(16, P)
        keys_s2 = part3(16, P)
        top_v = part3(16, TOPK)
        top_i = part3(16, TOPK)
        top_if = part3(16, TOPK)
        cand = part3(HEADS, TOPK * TOPK)
        cand2 = part3(HEADS, TOPK * TOPK)
        hot16 = part3(HEADS, TOPK * TOPK)
        best_v = part3(HEADS, TOPK)
        best_i = part3(HEADS, TOPK)
        best_a = part3(HEADS, TOPK)
        best_f = part3(HEADS, TOPK)
        best_e = part3(HEADS, TOPK)
        choice = part3(3, PAIRS)
        gate_sum = part(HEADS)

        psum = ctx.enter_context(nc.psum_tensor("psum", [P, 8, 512], F32))
        bank = [psum[:, b, :] for b in range(8)]
        flat = psum[:, :, :].rearrange("p b n -> p (b n)")

        names = """
            inputs_landed consts_landed ones_set bias_summed bias_vec_set bias_vec_stored bias_tables_landed bias_flipped bias_taken
            squared norm_summed out_norm_half rstd_set normed_set
            forget_done proj_evacuated
            forget_set forget_exp cum_set cum_turned cum_q_set cum_spread fox_tables_set
            cond_set mod_set
            scores_done scores_read sink_put max_set exp_done probs_set probs_turned probs_t_set attended mixed_set
            mixed_scaled resid_set silu_set ffn_act_set down_done down_evacuated
            rot_done rope_set k_rope_set mla_up_done mla_up_set
            query_set keys_scored keys_evacuated topk_set choice_turned choice_t_set
            hot_set gates_done gates_set peer_act_done peer_gelu_set peer_picked peer_out_done
            final_set out_stored vector_step scalar_step act_used
            weight_used down_used
        """.split()
        s = {n: ctx.enter_context(nc.semaphore(n)) for n in names}
        weight_landed = [ctx.enter_context(nc.semaphore(f"weight_landed{i}")) for i in range(RING)]
        up_landed = [ctx.enter_context(nc.semaphore(f"up_landed{i}")) for i in range(4)]
        down_landed = [ctx.enter_context(nc.semaphore(f"down_landed{i}")) for i in range(4)]

        def vcol(name, j=0):
            at, n = VEC[name]
            assert j < n
            return vec[:, at + j:at + j + 1]

        R_F, R_QK1, R_V1 = 0, 1, 1 + N_QK1
        R_OUT1 = R_V1 + N_V1
        R_DOWN = R_OUT1 + DC
        R_QK2 = R_DOWN + DC
        R_V2 = R_QK2 + N_QK2
        R_OUT2 = R_V2 + N_V2
        R_QUERY = R_OUT2 + DC

        units1 = [(kind, g, qt) for kind in (0, 1) for g in (0, 1) for qt in (0, 1, 2)]
        units2 = [(kind, g, qt) for kind in (2, 3) for g in (0, 1) for qt in (0, 1)]
        units = units1 + units2

        def shape_of(u):
            kind, _, qt = units[u]
            q0, nq = TILE_COLS[qt]
            if kind >= 2:
                return 0, N2, q0, nq
            return q0, N1 - q0, q0, nq

        def key_blocks(u):
            kind, _, qt = units[u]
            k0 = shape_of(u)[0]
            last = 3 if kind < 2 else 2
            first = qt if kind < 2 else 0
            return [(t, TILE_COLS[t][0] - k0, TILE_COLS[t][1]) for t in range(first, last)]

        flips = []
        for src, dst, rows in ((fox1, bias1, P), (fox0, bias0, P), (foxm, biasm, META)):
            src, dst = (a.rearrange("p h k -> p (h k)") for a in (src, dst))
            for c in range(0, src.shape[1], 512):
                n = min(512, src.shape[1] - c)
                flips.append((src[0:rows, c:c + n], dst[0:rows, c:c + n], rows, n))

        def has_sink(u):
            return units[u][0] in (0, 2)

        block = ctx.enter_context(nc.Block())

        @block.sync
        def _(sp):
            for slot in range(RING):
                sp.dma_start(ring[:, slot, :], weights[slot]).then_inc(weight_landed[slot], 16)
            with sp.Fori(1, N_STREAM // RING) as i:
                for slot in range(RING):
                    sp.wait_ge(s["weight_used"], (i - 1) * RING + slot + 1)
                    sp.dma_start(ring[:, slot, :], weights[bass.ds(i * RING + slot, 1)].rearrange("a p n -> p (a n)")).then_inc(weight_landed[slot], 16)
            for e in range(4):
                sp.wait_ge(s["weight_used"], N_STREAM - RING + e + 1)
                sp.dma_start(ring[:, e, :], up_experts[e]).then_inc(up_landed[e], 16)
            for e in range(4):
                sp.wait_ge(s["weight_used"], N_STREAM - RING + 4 + e + 1)
                sp.dma_start(ring[:, 4 + e, :], down_experts[e]).then_inc(down_landed[e], 16)
            with sp.Fori(1, KEYS // 4) as i:
                for e in range(4):
                    sp.wait_ge(s["peer_act_done"], (i - 1) * 4 + e + 1)
                    sp.dma_start(ring[:, e, :], up_experts[bass.ds(i * 4 + e, 1)].rearrange("a p n -> p (a n)")).then_inc(up_landed[e], 16)
                    sp.wait_ge(s["down_used"], (i - 1) * 4 + e + 1)
                    sp.dma_start(ring[:, 4 + e, :], down_experts[bass.ds(i * 4 + e, 1)].rearrange("a p n -> p (a n)")).then_inc(down_landed[e], 16)
            sp.wait_ge(s["final_set"], 1)
            sp.dma_start(out, lin_out[:, :, 0:N2]).then_inc(s["out_stored"], 16)
            sp.wait_ge(s["out_stored"], 16)

        @block.gpsimd
        def _(pool):
            nc.gpsimd.memset(ones[:, :], 1.0).then_inc(s["ones_set"], 1)
            nc.gpsimd.memset(zeros[:, :], 0.0).then_inc(s["ones_set"], 1)
            nc.gpsimd.memset(eps[:, :], EPS).then_inc(s["ones_set"], 1)
            pool.wait_ge(s["bias_vec_set"], 2)
            pool.dma_start(scratch, bias_vec[0:HEADS, :]).then_inc(s["bias_vec_stored"], 16)
            pool.wait_ge(s["bias_vec_stored"], 16)

            def rows(section, nq, nk):
                at, _, _, u0 = section
                return bass.AP(scratch.tensor, scratch.offset + at - u0 - (nq - 1), [[1, nq], [N_BIAS, HEADS], [1, nk]])

            pool.dma_start(fox1[:, :, 0:P], rows(BIAS_OWN, P, P)).then_inc(s["bias_tables_landed"], 16)
            pool.dma_start(fox1[:, :, P:2 * P], rows(BIAS_PREV, P, P)).then_inc(s["bias_tables_landed"], 16)
            pool.dma_start(fox1[:, :, 2 * P:N1], rows(BIAS_META1, P, META)).then_inc(s["bias_tables_landed"], 16)
            pool.dma_start(fox0[:, :, 0:P], rows(BIAS_OWN, P, P)).then_inc(s["bias_tables_landed"], 16)
            pool.dma_start(fox0[:, :, P:N1 - P], rows(BIAS_META0, P, META)).then_inc(s["bias_tables_landed"], 16)
            pool.dma_start(foxm[0:META, :, :], rows(BIAS_MM, META, META)).then_inc(s["bias_tables_landed"], 16)
            pool.wait_ge(s["consts_landed"], 16 * 8)

            def put_sinks(u0, u1):
                for u in range(u0, u1):
                    if not has_sink(u):
                        continue
                    _, nk, _, nq = shape_of(u)
                    kind, g, _ = units[u]
                    at = VEC["sinks1" if kind == 0 else "sinks2"][0] + 4 * g
                    if u >= 2:
                        pool.wait_ge(s["probs_turned"], u - 1)
                    nc.gpsimd.tensor_copy(score[u % 2][0:nq, :, nk:nk + 1],
                                          vec[0:nq, at:at + 4].unsqueeze(2)).then_inc(s["sink_put"], 1)

            put_sinks(0, len(units1))
            pool.wait_ge(s["resid_set"], 2)
            put_sinks(len(units1), len(units))

        @block.scalar
        def _(act):
            steps = [0]

            def step(ins):
                steps[0] += 1
                ins.then_inc(s["scalar_step"], 1)

            def settle():
                act.wait_ge(s["scalar_step"], steps[0])

            act.dma_start(resid[:, :, :], x_t).then_inc(s["inputs_landed"], 16)
            act.dma_start(consts, const).then_inc(s["consts_landed"], 16)
            act.dma_start(vec[:, :], vectors).then_inc(s["consts_landed"], 16)
            act.dma_start(ident[:, :], const[:, 0:P]).then_inc(s["consts_landed"], 16)
            act.dma_start(iota[:, :], const[:, P:2 * P]).then_inc(s["consts_landed"], 16)
            act.dma_start(w_f_sb, w_f).then_inc(s["consts_landed"], 16)
            act.dma_start(bf_sb[0:HEADS, :], b_f).then_inc(s["consts_landed"], 16)
            act.dma_start(rel_sb[0:BUCKETS, :], rel).then_inc(s["consts_landed"], 16)
            act.dma_start(small_sb, small).then_inc(s["consts_landed"], 16)

            def norm(k, src, chunks, n):
                nc.scalar.activation(squares[:, 0:chunks, 0:n], src, ACT.Square).then_inc(s["squared"], 1)
                act.wait_ge(s["norm_summed"], k)
                step(nc.scalar.activation(log_ms[:, 0:n], bank[7][:, 0:n], ACT.Ln, bias=eps[:, 0:1], scale=1.0 / (chunks * P)))
                settle()
                nc.scalar.activation(rstd[:, 0:n], log_ms[:, 0:n], ACT.Exp, scale=-0.5).then_inc(s["rstd_set"], 1)

            def evacuate(r, t, dst, src, scale=1.0, more=()):
                act.wait_ge(s["weight_used"], t + 1)
                ins = nc.scalar.activation(dst, src, ACT.Copy, scale=scale)
                for d, f in more:
                    ins = nc.scalar.activation(d, f, ACT.Copy)
                ins.then_inc(s["proj_evacuated"], 1)

            act.wait_ge(s["inputs_landed"], 16)
            act.wait_ge(s["ones_set"], 3)
            norm(1, resid[:, :, :], DC, N1)
            act.wait_ge(s["consts_landed"], 16 * 8)
            c0 = VEC["cond"][0]
            nc.scalar.activation(cond_act[:, :], vec[:, c0:c0 + DC], ACT.Silu).then_inc(s["cond_set"], 1)
            act.wait_ge(s["forget_done"], 1)
            nc.scalar.activation(f_work[0:HEADS, 0, :], bank[R_F % 4][0:HEADS, 0:N1], ACT.Copy).then_inc(s["proj_evacuated"], 1)
            act.wait_ge(s["forget_set"], 1)
            step(nc.scalar.activation(f_work[0:HEADS, 1, :], f_work[0:HEADS, 0, :], ACT.Abs))
            settle()
            step(nc.scalar.activation(f_work[0:HEADS, 2, :], f_work[0:HEADS, 1, :], ACT.Exp, scale=-1.0))
            settle()
            nc.scalar.activation(f_work[0:HEADS, 1, :], f_work[0:HEADS, 2, :], ACT.Ln, bias=ones[0:HEADS, 0:1]).then_inc(s["forget_exp"], 1)
            for j in range(N_QK1):
                r = R_QK1 + j
                evacuate(r, T_QK1 + j, qk[:, j, :], bank[r % 4][:, 0:N1], scale=0.125 if j < 4 or 5 <= j < 9 else 1.0)
            for j in range(N_V1):
                r = R_V1 + j
                b = bank[r % 4][:, 0:3 * P].rearrange("p (t n) -> p t n", n=P)
                evacuate(r, T_V1 + j, v_nat[:, 0:2, j * P:(j + 1) * P], b[:, 0:2, :],
                         more=[(v_nat[0:META, 2, j * P:(j + 1) * P], b[0:META, 2, :])])

            for n, (_, dst, rows, cols) in enumerate(flips):
                act.wait_ge(s["bias_flipped"], n + 1)
                nc.scalar.activation(dst, bank[4 + n % 4][0:rows, 0:cols], ACT.Copy).then_inc(s["bias_taken"], 1)

            def exps(u):
                _, nk, _, nq = shape_of(u)
                n = nk + has_sink(u)
                act.wait_ge(s["max_set"], u + 1)
                for h in range(4):
                    ins = nc.scalar.activation(score[u % 2][0:nq, h, 0:n], score[u % 2][0:nq, h, 0:n], ACT.Exp,
                                               bias=stats[u % 2][0:nq, 4 + h:5 + h],
                                               accum_out=stats[u % 2][0:nq, 8 + h:9 + h])
                ins.then_inc(s["exp_done"], 1)

            def take_probs_t(u):
                nq = shape_of(u)[3]
                act.wait_ge(s["probs_turned"], u + 1)
                if u >= 2:
                    act.wait_ge(s["attended"], u - 1)
                for t, _, kn in key_blocks(u):
                    ins = nc.scalar.activation(
                        probs_t[u % 2][0:kn, t, :].rearrange("p (h q) -> p h q", q=P)[:, :, 0:nq],
                        bank[4 + t][0:kn, :].rearrange("p (h q) -> p h q", q=P)[:, :, 0:nq], ACT.Copy)
                ins.then_inc(s["probs_t_set"], 1)

            def attention(u0, u1):
                for u in range(u0, u1 + 1):
                    if u < u1:
                        exps(u)
                    if u > u0:
                        take_probs_t(u - 1)

            attention(0, len(units1))
            for j in range(DC):
                r = R_OUT1 + j
                evacuate(r, T_OUT1 + j, lin_out[:, j, :], bank[r % 4][:, 0:N1])
            act.wait_ge(s["proj_evacuated"], R_OUT1 + DC)
            norm(2, lin_out, DC, N1)
            act.wait_ge(s["resid_set"], 1)
            norm(3, resid[:, :, :], DC, N1)

            def silu(j, k):
                act.wait_ge(s["weight_used"], T_FFN + j * 2 + 2)
                nc.scalar.activation(silu_sb[:, k, :], bank[2 * k][:, 0:N1], ACT.Silu).then_inc(s["silu_set"], 1)

            for k in range(4):
                silu(k, k)
            with act.Fori(1, FC // 4) as i:
                for k in range(4):
                    act.wait_ge(s["ffn_act_set"], (i - 1) * 4 + k + 1)
                    silu(i * 4 + k, k)
            for k in range(FC % 4):
                act.wait_ge(s["ffn_act_set"], FC // 4 * 4 - 4 + k + 1)
                silu(FC // 4 * 4 + k, k)
            for j in range(DC):
                r = R_DOWN + j
                evacuate(r, T_DOWN + (j * FC + FC - 1) // DC, lin_out[:, j, :], bank[r % 4][:, 0:N1])
            act.wait_ge(s["proj_evacuated"], R_DOWN + DC)
            norm(4, lin_out, DC, N1)

            act.wait_ge(s["resid_set"], 2)
            norm(5, resid[:, :, 0:N2], DC, N2)

            def add_shift(n, at):
                for c in range(DC):
                    act.wait_ge(s["mixed_scaled"], n * DC + c + 1)
                    ins = nc.scalar.activation(normed[:, c, 0:N2], normed[:, c, 0:N2], ACT.Identity,
                                               bias=modv[:, at + c:at + c + 1])
                ins.then_inc(s["normed_set"], 1)

            add_shift(0, 0)
            for j in range(N_QK2):
                r = R_QK2 + j
                evacuate(r, T_QK2 + j, qk[:, j, 0:N2], bank[r % 4][:, 0:N2], scale=0.125 if j < 4 else 1.0)
            b = bank[R_V2 % 4][:, 0:2 * P].rearrange("p (t n) -> p t n", n=P)
            evacuate(R_V2, T_V2, v_nat[:, 0:2, 0:P], b)
            act.wait_ge(s["proj_evacuated"], R_QK2 + N_QK2)
            norm(6, qk[:, 5:7, 0:N2], QR_C, N2)
            act.wait_ge(s["normed_set"], 4)
            norm(7, qk[:, 7:8, 0:N2], 1, N2)
            act.wait_ge(s["mla_up_done"], 1)
            nc.scalar.activation(q_mla[0:QK, :, :], flat[0:QK, 0:HEADS * N2].rearrange("p (h n) -> p h n", n=N2),
                                 ACT.Copy, scale=float(QK) ** -0.5).then_inc(s["mla_up_set"], 1)
            act.wait_ge(s["mla_up_done"], 2)
            nc.scalar.activation(v_nat[:, 0:2, P:P + HEADS * DH],
                                 flat[:, 2048:3072].rearrange("p (t n) -> p t n", n=512), ACT.Copy).then_inc(s["mla_up_set"], 1)
            act.wait_ge(s["mla_up_done"], 3)
            act.wait_ge(s["rope_set"], 2)
            nc.scalar.activation(k_mla[0:NOPE, :, :], flat[0:NOPE, 0:HEADS * N2].rearrange("p (h n) -> p h n", n=N2),
                                 ACT.Copy).then_inc(s["mla_up_set"], 1)
            attention(len(units1), len(units))
            act.wait_ge(s["mixed_set"], len(units))
            norm(8, mixed[:, 0:4, 0:N2], 4, N2)
            act.wait_ge(s["out_norm_half"], 1)
            norm(9, mixed[:, 4:8, 0:N2], 4, N2)
            act.wait_ge(s["proj_evacuated"], R_OUT2 + DC)
            norm(10, resid[:, :, 0:N2], DC, N2)
            add_shift(1, 3 * DC)
            for j in range(N_QUERY):
                r = R_QUERY + j
                evacuate(r, T_QUERY + j, query[:, j, :], bank[r % 4][:, 0:N2])
            for tt in range(2):
                if tt == 0:
                    act.wait_ge(s["keys_scored"], 1)
                else:
                    act.wait_ge(s["weight_used"], N_STREAM)
                nc.scalar.activation(keys_s, flat[:, tt * 2048:(tt + 1) * 2048].rearrange("p (a n) -> p a n", n=P),
                                     ACT.Copy).then_inc(s["keys_evacuated"], 1)
                act.wait_ge(s["topk_set"], 2 * tt + 1)
                nc.scalar.activation(best_e, best_e, ACT.Exp).then_inc(s["act_used"], 1)
                act.wait_ge(s["choice_turned"], tt + 1)
                for k, dst in enumerate((idx1_t, idx2_t, gate_t)):
                    ins = nc.scalar.activation(dst[:, tt * P:(tt + 1) * P], bank[4 * tt + k][:, 0:P], ACT.Copy)
                ins.then_inc(s["choice_t_set"], 1)

            with act.Fori(0, N2 // 8) as i:
                for k in range(2):
                    act.wait_ge(s["gates_done"], i * 2 + k + 1)
                    nc.scalar.activation(gates[:, :, bass.ds((i * 2 + k) * 4, 4)],
                                         bank[k][:, :].rearrange("p (t n) -> p n t", n=P), ACT.Copy).then_inc(s["gates_set"], 1)

            def gelu(e, k):
                act.wait_ge(s["peer_act_done"], e + 1)
                nc.scalar.activation(act_sb[:, k, :], bank[4 + k][:, 0:N2], ACT.Gelu).then_inc(s["peer_gelu_set"], 1)

            for k in range(4):
                gelu(k, k)
            with act.Fori(1, KEYS // 4) as i:
                for k in range(4):
                    act.wait_ge(s["peer_picked"], (i - 1) * 4 + k + 1)
                    gelu(i * 4 + k, k)
            act.wait_ge(s["resid_set"], 3)
            norm(11, resid[:, :, 0:N2], DC, N2)

        @block.tensor
        def _(pe):
            def weight(t):
                pe.wait_ge(weight_landed[t % RING], 16 * (t // RING + 1))
                return ring[:, t % RING, :].rearrange("p (c n) -> p c n", n=P)

            def sum_squares(k, chunks, n):
                pe.wait_ge(s["squared"], k)
                for c in range(chunks):
                    ins = nc.tensor.matmul(bank[7][:, 0:n], ones[:, :], squares[:, c, 0:n], start=(c == 0), stop=(c == chunks - 1))
                ins.then_inc(s["norm_summed"], 1)

            def bank_free(r):
                if r >= 4:
                    pe.wait_ge(s["proj_evacuated"], r - 3)
                return bank[r % 4]

            def linear(r, t, rhs, n):
                b = bank_free(r)
                w = weight(t)
                for c in range(DC):
                    ins = nc.tensor.matmul(b[:, 0:n], w[:, c, :], rhs[:, c, 0:n], start=(c == 0), stop=(c == DC - 1))
                ins.then_inc(s["weight_used"], 1)

            def natural(r, t, lhs, tiles):
                b = bank_free(r)
                w = weight(t)
                for q, (q0, nq) in enumerate(tiles):
                    for c in range(DC):
                        ins = nc.tensor.matmul(b[0:nq, q * P:(q + 1) * P], lhs[:, c, q0:q0 + nq], w[:, c, :],
                                               start=(c == 0), stop=(c == DC - 1))
                ins.then_inc(s["weight_used"], 1)

            pe.wait_ge(s["ones_set"], 2)
            pe.wait_ge(s["consts_landed"], 16 * 8)
            hot = cst("bucket", BUCKETS)
            nc.tensor.matmul(bank[4][0:HEADS, 0:512], rel_sb[0:BUCKETS, :], hot[:, 0:512], start=True, stop=True)
            nc.tensor.matmul(bank[5][0:HEADS, 0:N_BIAS - 512], rel_sb[0:BUCKETS, :], hot[:, 512:N_BIAS],
                             start=True, stop=True).then_inc(s["bias_summed"], 1)
            sum_squares(1, DC, N1)
            pe.wait_ge(s["normed_set"], 1)
            for c in range(DC):
                ins = nc.tensor.matmul(bank[0][0:HEADS, 0:N1], w_f_sb[:, c, :], normed[:, c, :], start=(c == 0), stop=(c == DC - 1))
            ins.then_inc(s["forget_done"], 1)
            for j in range(N_QK1):
                linear(R_QK1 + j, T_QK1 + j, normed, N1)
            for j in range(N_V1):
                natural(R_V1 + j, T_V1 + j, normed, TILE_COLS)
            pe.wait_ge(s["bias_tables_landed"], 16 * 6)
            for n, (src, _, rows, cols) in enumerate(flips):
                if n >= 4:
                    pe.wait_ge(s["bias_taken"], n - 3)
                nc.tensor.matmul(bank[4 + n % 4][0:rows, 0:cols], cst("flip")[0:rows, P - rows:P], src, start=True, stop=True).then_inc(s["bias_flipped"], 1)
            pe.wait_ge(s["bias_taken"], len(flips))
            pe.wait_ge(s["cum_set"], 3)
            for t, (c0, n) in enumerate(TILE_COLS):
                ins = nc.tensor.transpose(bank[4][0:n, t * HEADS:(t + 1) * HEADS], f_work[0:HEADS, 5, c0:c0 + n], ident[0:HEADS, 0:HEADS])
            ins.then_inc(s["cum_turned"], 1)
            sel = cst("select", HEADS).rearrange("p (h n) -> p h n", n=P)
            for h in range(HEADS):
                if h >= 2:
                    pe.wait_ge(s["fox_tables_set"], h - 1)
                nc.tensor.matmul(bank[5 + h % 2][:, 0:N1], sel[:, h, :], f_work[0:HEADS, 5, :], start=True, stop=True).then_inc(s["cum_spread"], 1)
            pe.wait_ge(s["cond_set"], 1)
            with pe.Fori(0, N_ADA // RING) as i:
                for k in range(RING):
                    slot = (T_ADA + k) % RING
                    pe.wait_ge(weight_landed[slot], (i + (T_ADA + k) // RING + 1) * 16)
                    for c in range(DC):
                        ins = nc.tensor.matmul(bank[7][:, bass.ds(i * RING + k, 1)],
                                               ring[:, slot, c * P:(c + 1) * P], cond_act[:, c:c + 1],
                                               start=(c == 0), stop=(c == DC - 1))
                    ins.then_inc(s["weight_used"], 1)

            def scores(u):
                kind, g, _ = units[u]
                k0, nk, q0, nq = shape_of(u)
                if u:
                    pe.wait_ge(s["scores_read"], u)
                for h in range(4):
                    c, half = 2 * g + h // 2, h % 2
                    rows = slice(half * DH, half * DH + DH)
                    if kind == 0:
                        lhs, rhs = qk[rows, c, q0:q0 + nq], qk[rows, 4, k0:k0 + nk]
                    elif kind == 1:
                        lhs, rhs = qk[rows, 5 + c, q0:q0 + nq], qk[rows, 9 + c, k0:k0 + nk]
                    elif kind == 2:
                        lhs, rhs = rope_tmp[rows, c, q0:q0 + nq], rope_tmp[rows, 4, k0:k0 + nk]
                    else:
                        lhs, rhs = q_mla[0:QK, 4 * g + h, q0:q0 + nq], k_mla[0:QK, 4 * g + h, k0:k0 + nk]
                    ins = nc.tensor.matmul(bank[h][0:nq, 0:nk], lhs, rhs, start=True, stop=True)
                ins.then_inc(s["scores_done"], 1)

            def turn_probs(u):
                nq = shape_of(u)[3]
                pe.wait_ge(s["probs_set"], u + 1)
                if u > 0:
                    pe.wait_ge(s["probs_t_set"], u)
                for t, k0, kn in key_blocks(u):
                    for h in range(4):
                        ins = nc.tensor.transpose(bank[4 + t][0:kn, h * P:h * P + nq], score[u % 2][0:nq, h, k0:k0 + kn], ident[0:nq, 0:nq])
                ins.then_inc(s["probs_turned"], 1)

            def attend(u):
                kind, g, _ = units[u]
                nq = shape_of(u)[3]
                pe.wait_ge(s["probs_t_set"], u + 1)
                if u > 0:
                    pe.wait_ge(s["mixed_set"], u)
                blocks = key_blocks(u)
                for h in range(4):
                    c, half = 2 * g + h // 2, h % 2
                    vc = half * DH if kind in (0, 2) else P + (2 * c + half) * DH
                    for n, (t, _, kn) in enumerate(blocks):
                        ins = nc.tensor.matmul(bank[7][half * DH:(half + 1) * DH, (h // 2) * P:(h // 2) * P + nq],
                                               v_nat[0:kn, t, vc:vc + DH], probs_t[u % 2][0:kn, t, h * P:h * P + nq],
                                               start=(n == 0), stop=(n == len(blocks) - 1))
                ins.then_inc(s["attended"], 1)

            def attention(u0, u1):
                for u in range(u0, u1 + 1):
                    if u < u1:
                        scores(u)
                    if u > u0:
                        turn_probs(u - 1)
                        attend(u - 1)

            pe.wait_ge(s["mod_set"], 1)
            pe.wait_ge(s["fox_tables_set"], HEADS)
            pe.wait_ge(s["proj_evacuated"], R_OUT1)
            attention(0, len(units1))
            pe.wait_ge(s["mixed_set"], len(units1))
            for j in range(DC):
                linear(R_OUT1 + j, T_OUT1 + j, mixed, N1)
            sum_squares(2, DC, N1)
            sum_squares(3, DC, N1)
            pe.wait_ge(s["normed_set"], 2)

            def gate_up(tile_round, j, k, first):
                for side in range(2):
                    t = T_FFN + 2 * k + side
                    slot = t % RING
                    pe.wait_ge(weight_landed[slot], (tile_round + t // RING + 1) * 16)
                    if side == 0 and not first:
                        pe.wait_ge(s["ffn_act_set"], j - 3)
                    for c in range(DC):
                        ins = nc.tensor.matmul(bank[2 * k + side][:, 0:N1], ring[:, slot, c * P:(c + 1) * P], normed[:, c, :],
                                               start=(c == 0), stop=(c == DC - 1))
                    ins.then_inc(s["weight_used"], 1)

            for k in range(4):
                gate_up(0, k, k, True)
            with pe.Fori(1, FC // 4) as i:
                for k in range(4):
                    gate_up(i, i * 4 + k, k, False)
            for k in range(FC % 4):
                gate_up(FC // 4, FC // 4 * 4 + k, k, False)
            pe.wait_ge(s["ffn_act_set"], FC)
            for j in range(DC):
                b = bank_free(R_DOWN + j)
                for f in range(FC):
                    n = j * FC + f
                    w = weight(T_DOWN + n // DC)
                    ins = nc.tensor.matmul(b[:, 0:N1], w[:, n % DC, :], ffn_act[:, f, :], start=(f == 0), stop=(f == FC - 1))
                    if n % DC == DC - 1:
                        ins.then_inc(s["weight_used"], 1)
            sum_squares(4, DC, N1)

            sum_squares(5, DC, N2)
            pe.wait_ge(s["normed_set"], 3)
            for j in range(N_QK2):
                linear(R_QK2 + j, T_QK2 + j, normed, N2)
            natural(R_V2, T_V2, normed, TILE_COLS[0:2])
            sum_squares(6, QR_C, N2)
            pe.wait_ge(s["proj_evacuated"], R_OUT2)
            for j in range(5):
                ins = nc.tensor.matmul(flat[:, j * N2:(j + 1) * N2], cst("rot64"), qk[:, j, 0:N2], start=True, stop=True)
            ins.then_inc(s["rot_done"], 1)
            nc.tensor.matmul(bank[4][:, 0:N2], cst("rot32"), qk[:, 8, 0:N2], start=True, stop=True).then_inc(s["rot_done"], 1)
            pe.wait_ge(s["rstd_set"], 6)
            sum_squares(7, 1, N2)
            w_q = small_sb[:, 0:QR_C * HEADS * QK].rearrange("p (c n) -> p c n", c=QR_C)
            w_kv = small_sb[:, QR_C * HEADS * QK:2560].rearrange("p (h n) -> p h n", h=HEADS)
            pe.wait_ge(s["rope_set"], 1)
            pe.wait_ge(s["normed_set"], 4)
            for h in range(HEADS):
                for c in range(QR_C):
                    ins = nc.tensor.matmul(flat[0:QK, h * N2:(h + 1) * N2], w_q[:, c, h * QK:(h + 1) * QK], normed[:, c, 0:N2],
                                           start=(c == 0), stop=(c == QR_C - 1))
            ins.then_inc(s["mla_up_done"], 1)
            pe.wait_ge(s["rope_set"], 2)
            pe.wait_ge(s["normed_set"], 5)
            for t in range(2):
                ins = nc.tensor.matmul(bank[4 + t][:, :], normed[:, 2, t * P:(t + 1) * P], w_kv[:, :, NOPE:NOPE + DH], start=True, stop=True)
            ins.then_inc(s["mla_up_done"], 1)
            pe.wait_ge(s["mla_up_set"], 1)
            for h in range(HEADS):
                ins = nc.tensor.matmul(flat[0:NOPE, h * N2:(h + 1) * N2], w_kv[:, h, 0:NOPE], normed[:, 2, 0:N2], start=True, stop=True)
            ins.then_inc(s["mla_up_done"], 1)
            pe.wait_ge(s["mla_up_set"], 3)
            rot = cst("rot32")[0:QK, 0:QK]
            for h in range(HEADS):
                ins = nc.tensor.matmul(flat[0:QK, h * N2:(h + 1) * N2], rot, q_mla[0:QK, h, :], start=True, stop=True)
            ins.then_inc(s["rot_done"], 1)
            pe.wait_ge(s["rope_set"], 3)
            pe.wait_ge(s["k_rope_set"], 1)
            attention(len(units1), len(units))
            sum_squares(8, 4, N2)
            pe.wait_ge(s["rstd_set"], 8)
            sum_squares(9, 4, N2)
            pe.wait_ge(s["normed_set"], 6)
            for j in range(DC):
                r = R_OUT2 + j
                linear(r, T_OUT2 + j, normed, N2)
            sum_squares(10, DC, N2)
            pe.wait_ge(s["normed_set"], 7)
            for j in range(N_QUERY):
                linear(R_QUERY + j, T_QUERY + j, normed, N2)
            pe.wait_ge(s["proj_evacuated"], R_QUERY + N_QUERY)
            for k in range(N_SUB):
                weight(T_SUB + k)
            for tt in range(2):
                for a in range(16):
                    slot = (T_SUB + a // 8) % RING
                    ins = nc.tensor.matmul(flat[:, tt * 2048 + a * P:tt * 2048 + (a + 1) * P], query[:, a, tt * P:(tt + 1) * P],
                                           ring[:, slot, (a % 8) * P:(a % 8 + 1) * P], start=True, stop=True)
                if tt == 0:
                    ins.then_inc(s["keys_scored"], 1)
                else:
                    ins.then_inc(s["weight_used"], N_SUB)
            pe.wait_ge(s["keys_evacuated"], 1)
            for tt in range(2):
                pe.wait_ge(s["topk_set"], 2 * tt + 2)
                for k in range(3):
                    ins = nc.tensor.transpose(bank[4 * tt + k][:, 0:P], choice[:, k, :], ident[:, :])
                ins.then_inc(s["choice_turned"], 1)
            pe.wait_ge(s["choice_t_set"], 2)
            with pe.Fori(0, N2 // 8) as i:
                for k in range(2):
                    pe.wait_ge(s["hot_set"], i * 2 + k + 1)
                    for q in range(4):
                        ins = nc.tensor.matmul(bank[k][:, q * P:(q + 1) * P], hot2[:, 4 * k + q, :], hot1[:, 4 * k + q, :], start=True, stop=True)
                    ins.then_inc(s["gates_done"], 1)
            pe.wait_ge(s["gates_set"], N2 // 4)
            for b in range(4):
                nc.tensor.matmul(bank[b][:, :], zeros[:, 0:P], zeros[:, :], start=True, stop=True)

            def up(k, landed, picked_at):
                pe.wait_ge(up_landed[k], landed)
                if picked_at is not None:
                    pe.wait_ge(s["peer_gelu_set"], picked_at)
                for c in range(DC):
                    ins = nc.tensor.matmul(bank[4 + k][:, 0:N2], ring[:, k, c * P:(c + 1) * P], normed[:, c, 0:N2],
                                           start=(c == 0), stop=(c == DC - 1))
                ins.then_inc(s["peer_act_done"], 1)

            def down(k, landed, e):
                pe.wait_ge(down_landed[k], landed)
                pe.wait_ge(s["peer_picked"], e + 1)
                for c in range(DC):
                    ins = nc.tensor.matmul(flat[:, c * N2:(c + 1) * N2], ring[:, 4 + k, c * P:(c + 1) * P], picked[:, k, :],
                                           start=False, stop=False, skip_group_check=True)
                ins.then_inc(s["down_used"], 1)

            up(0, 16, None)
            for k in range(3):
                up(k + 1, 16, None)
                down(k, 16, k)
            with pe.Fori(1, KEYS // 4) as i:
                up(0, (i + 1) * 16, i * 4 - 3)
                down(3, i * 16, i * 4 - 1)
                for k in range(3):
                    up(k + 1, (i + 1) * 16, i * 4 + k - 2)
                    down(k, (i + 1) * 16, i * 4 + k)
            down(3, KEYS // 4 * 16, KEYS - 1)
            sum_squares(11, DC, N2)

        @block.vector
        def _(dve):
            steps = [0]

            def step(ins):
                steps[0] += 1
                ins.then_inc(s["vector_step"], 1)

            def settle():
                dve.wait_ge(s["vector_step"], steps[0])

            def normalise(dst, src, gain, chunks, n, done=None):
                for c in range(chunks):
                    ins = nc.vector.scalar_tensor_tensor(out=dst[:, c, 0:n], in0=src[:, c, 0:n], scalar=vcol(gain[0], gain[1] + c),
                                                         in1=rstd[:, 0:n], op0=ALU.mult, op1=ALU.mult)
                    if done is None:
                        step(ins)
                if done is not None:
                    ins.then_inc(s[done], 1)

            dve.wait_ge(s["bias_summed"], 1)
            m = cst("bmask", HEADS)
            nc.vector.tensor_tensor(bias_vec[0:HEADS, 0:512], bank[4][0:HEADS, :], m[:, 0:512], ALU.add).then_inc(s["bias_vec_set"], 1)
            nc.vector.tensor_tensor(bias_vec[0:HEADS, 512:N_BIAS], bank[5][0:HEADS, 0:N_BIAS - 512], m[:, 512:N_BIAS],
                                    ALU.add).then_inc(s["bias_vec_set"], 1)
            dve.wait_ge(s["rstd_set"], 1)
            normalise(normed, resid, ("pre_mix", 0), DC, N1, "normed_set")
            dve.wait_ge(s["proj_evacuated"], 1)
            nc.vector.tensor_scalar(f_work[0:HEADS, 0, :], f_work[0:HEADS, 0, :], bf_sb[0:HEADS, 0:1], None, ALU.add).then_inc(s["forget_set"], 1)
            step(nc.vector.memset(f_work[0:HEADS, 4, :], 1.0))
            dve.wait_ge(s["forget_exp"], 1)
            step(nc.vector.scalar_tensor_tensor(out=f_work[0:HEADS, 3, :], in0=f_work[0:HEADS, 0, :], scalar=0.0,
                                                in1=f_work[0:HEADS, 1, :], op0=ALU.min, op1=ALU.subtract))
            settle()
            before = None
            for t in (2, 1, 0):
                c0, n = TILE_COLS[t]
                if before is not None:
                    dve.wait_ge(s["cum_set"], 2 - t)
                nc.vector.tensor_tensor_scan(f_work[0:HEADS, 5, c0:c0 + n], f_work[0:HEADS, 4, c0:c0 + n], f_work[0:HEADS, 3, c0:c0 + n],
                                             0.0 if before is None else before, ALU.mult, ALU.add).then_inc(s["cum_set"], 1)
                before = f_work[0:HEADS, 5, c0 + n - 1:c0 + n]
            dve.wait_ge(s["cum_turned"], 1)
            step(nc.vector.tensor_copy(cum_q[:, 0:2, :], bank[4][:, 0:2 * HEADS].rearrange("p (t h) -> p t h", h=HEADS)))
            step(nc.vector.tensor_copy(cum_q[0:META, 2, :], bank[4][0:META, 2 * HEADS:3 * HEADS]))
            settle()
            for h in range(HEADS):
                dve.wait_ge(s["cum_spread"], h + 1)
                b = bank[5 + h % 2]
                nc.vector.scalar_tensor_tensor(out=fox1[:, h, :], in0=b[:, 0:N1], scalar=cum_q[:, 0, h:h + 1], in1=cst("causal1"),
                                               op0=ALU.add, op1=ALU.add)
                nc.vector.scalar_tensor_tensor(out=fox0[:, h, :], in0=b[:, P:N1], scalar=cum_q[:, 1, h:h + 1], in1=cst("causal0"),
                                               op0=ALU.add, op1=ALU.add)
                nc.vector.scalar_tensor_tensor(out=foxm[0:META, h, :], in0=b[0:META, 2 * P:N1], scalar=cum_q[0:META, 2, h:h + 1],
                                               in1=cst("causalm", META), op0=ALU.add, op1=ALU.add).then_inc(s["fox_tables_set"], 1)
            dve.wait_ge(s["weight_used"], T_OUT1)
            b0 = VEC["b_ada"][0]
            step(nc.vector.tensor_tensor(modv[:, :], bank[7][:, 0:6 * DC], vec[:, b0:b0 + 6 * DC], ALU.add))
            settle()
            for k in (1, 4):
                ins = nc.vector.tensor_scalar(modv[:, k * DC:(k + 1) * DC], modv[:, k * DC:(k + 1) * DC], 1.0, None, ALU.add)
            ins.then_inc(s["mod_set"], 1)

            def add_bias(u):
                kind, g, qt = units[u]
                _, nk, _, nq = shape_of(u)
                sc = score[u % 2]
                src = psum[0:nq, 0:4, 0:nk]
                dve.wait_ge(s["scores_done"], u + 1)
                if u >= 2:
                    dve.wait_ge(s["probs_turned"], u - 1)
                if kind == 3:
                    ins = nc.vector.tensor_copy(sc[0:nq, :, 0:nk], src)
                else:
                    if kind == 2:
                        table = cst(f"band{1 - qt}").unsqueeze(1).broadcast_to([P, 4, N2])
                    else:
                        table = ((bias1, bias0, biasm), (fox1, fox0, foxm))[kind][qt][0:nq, 4 * g:4 * g + 4, :]
                    ins = nc.vector.tensor_tensor(sc[0:nq, :, 0:nk], src, table, ALU.add)
                ins.then_inc(s["scores_read"], 1)
                dve.wait_ge(s["scores_read"], u + 1)
                if has_sink(u):
                    dve.wait_ge(s["sink_put"], sum(has_sink(v) for v in range(u + 1)))
                n = nk + has_sink(u)
                st = stats[u % 2]
                step(nc.vector.tensor_reduce(st[0:nq, 0:4], sc[0:nq, :, 0:n], AX_X, ALU.max))
                settle()
                nc.vector.tensor_scalar(st[0:nq, 4:8], st[0:nq, 0:4], -1.0, None, ALU.mult).then_inc(s["max_set"], 1)

            def divide(u):
                _, nk, _, nq = shape_of(u)
                st = stats[u % 2]
                dve.wait_ge(s["exp_done"], u + 1)
                step(nc.vector.reciprocal(st[0:nq, 12:16], st[0:nq, 8:12]))
                settle()
                nc.vector.tensor_tensor(score[u % 2][0:nq, :, 0:nk], score[u % 2][0:nq, :, 0:nk],
                                        st[0:nq, 12:16].unsqueeze(2).broadcast_to([nq, 4, nk]), ALU.mult).then_inc(s["probs_set"], 1)

            def take_mixed(u):
                kind, g, _ = units[u]
                _, _, q0, nq = shape_of(u)
                dve.wait_ge(s["attended"], u + 1)
                c = 4 * (kind % 2) + 2 * g
                nc.vector.tensor_copy(mixed[:, c:c + 2, q0:q0 + nq],
                                      bank[7][:, 0:2 * P].rearrange("p (c q) -> p c q", q=P)[:, :, 0:nq]).then_inc(s["mixed_set"], 1)

            def attention(u0, u1):
                for u in range(u0, u1 + 2):
                    if u < u1:
                        add_bias(u)
                    if u0 < u < u1 + 1:
                        divide(u - 1)
                    if u > u0 + 1:
                        take_mixed(u - 2)

            def add_normed(gain):
                normalise(lin_out, lin_out, (gain, 0), DC, N1)
                settle()
                nc.vector.tensor_tensor(resid[:, :, :], resid[:, :, :], lin_out, ALU.add).then_inc(s["resid_set"], 1)

            dve.wait_ge(s["bias_taken"], len(flips))
            attention(0, len(units1))
            dve.wait_ge(s["rstd_set"], 2)
            add_normed("post_mix")
            dve.wait_ge(s["rstd_set"], 3)
            normalise(normed, resid, ("pre_ffn", 0), DC, N1, "normed_set")

            def gate(i, j, k):
                dve.wait_ge(s["silu_set"], j + 1)
                nc.vector.tensor_tensor(ffn_act[:, bass.ds(j, 1), :] if i is not None else ffn_act[:, j:j + 1, :],
                                        silu_sb[:, k:k + 1, :], bank[2 * k + 1][:, 0:N1].unsqueeze(1), ALU.mult).then_inc(s["ffn_act_set"], 1)

            with dve.Fori(0, FC // 4) as i:
                for k in range(4):
                    gate(i, i * 4 + k, k)
            for k in range(FC % 4):
                gate(None, FC // 4 * 4 + k, k)
            dve.wait_ge(s["rstd_set"], 4)
            add_normed("post_ffn")

            def modulate(n, scale_at):
                for c in range(DC):
                    nc.vector.scalar_tensor_tensor(out=normed[:, c, 0:N2], in0=resid[:, c, 0:N2],
                                                   scalar=modv[:, scale_at + c:scale_at + c + 1],
                                                   in1=rstd[:, 0:N2], op0=ALU.mult, op1=ALU.mult).then_inc(s["mixed_scaled"], 1)

            dve.wait_ge(s["rstd_set"], 5)
            modulate(0, DC)
            cos, sin = (cst(n).unsqueeze(1).broadcast_to([P, 5, N2]) for n in ("cos64", "sin64"))
            dve.wait_ge(s["proj_evacuated"], R_QK2 + 5)
            step(nc.vector.tensor_tensor(rope_tmp[:, 0:5, :], qk[:, 0:5, 0:N2], cos, ALU.mult))
            dve.wait_ge(s["rot_done"], 1)
            step(nc.vector.tensor_tensor(rope_tmp2[:, 0:5, :], flat[:, 0:5 * N2].rearrange("p (a n) -> p a n", n=N2), sin, ALU.mult))
            settle()
            nc.vector.tensor_tensor(rope_tmp[:, 0:5, :], rope_tmp[:, 0:5, :], rope_tmp2[:, 0:5, :], ALU.add).then_inc(s["rope_set"], 1)
            dve.wait_ge(s["rope_set"], 1)
            rr = slice(NOPE, QK)
            dve.wait_ge(s["rot_done"], 2)
            step(nc.vector.tensor_tensor(rope_tmp2[rr, 0, :], bank[4][rr, 0:N2], cst("sin32")[rr, :], ALU.mult))
            step(nc.vector.tensor_tensor(rope_tmp2[rr, 1, :], qk[rr, 8, 0:N2], cst("cos32")[rr, :], ALU.mult))
            settle()
            nc.vector.tensor_tensor(rope_tmp2[rr, 5, :], rope_tmp2[rr, 0, :], rope_tmp2[rr, 1, :], ALU.add).then_inc(s["rope_set"], 1)
            dve.wait_ge(s["rope_set"], 2)
            dve.wait_ge(s["rstd_set"], 6)
            normalise(normed, qk[:, 5:7, :], ("q_norm", 0), QR_C, N2, "normed_set")
            dve.wait_ge(s["rstd_set"], 7)
            nc.vector.scalar_tensor_tensor(out=normed[:, 2, 0:N2], in0=qk[:, 7, 0:N2], scalar=vcol("kv_norm"), in1=rstd[:, 0:N2],
                                           op0=ALU.mult, op1=ALU.mult).then_inc(s["normed_set"], 1)
            dve.wait_ge(s["normed_set"], 5)
            nc.vector.tensor_copy(k_mla[rr, :, :], rope_tmp2[rr, 5:6, :].broadcast_to([ROPE, HEADS, N2])).then_inc(s["k_rope_set"], 1)
            cos, sin = (cst(n)[rr, :].unsqueeze(1).broadcast_to([ROPE, HEADS, N2]) for n in ("cos32", "sin32"))
            dve.wait_ge(s["k_rope_set"], 1)
            dve.wait_ge(s["rot_done"], 3)
            step(nc.vector.tensor_tensor(rope_tmp2[rr, :, :], flat[rr, 0:HEADS * N2].rearrange("p (a n) -> p a n", n=N2), sin, ALU.mult))
            step(nc.vector.tensor_tensor(q_mla[rr, :, :], q_mla[rr, :, :], cos, ALU.mult))
            settle()
            nc.vector.tensor_tensor(q_mla[rr, :, :], q_mla[rr, :, :], rope_tmp2[rr, :, :], ALU.add).then_inc(s["rope_set"], 1)
            attention(len(units1), len(units))
            dve.wait_ge(s["rstd_set"], 8)
            normalise(normed, mixed, ("out_norm", 0), 4, N2, "out_norm_half")
            dve.wait_ge(s["rstd_set"], 9)
            normalise(normed[:, 4:8, :], mixed[:, 4:8, :], ("out_norm", 4), 4, N2, "normed_set")
            for j in range(DC):
                r = R_OUT2 + j
                dve.wait_ge(s["weight_used"], T_OUT2 + j + 1)
                ins = nc.vector.scalar_tensor_tensor(out=resid[:, j, 0:N2], in0=bank[r % 4][:, 0:N2], scalar=modv[:, 2 * DC + j:2 * DC + j + 1],
                                                     in1=resid[:, j, 0:N2], op0=ALU.mult, op1=ALU.add)
                ins.then_inc(s["proj_evacuated"], 1)
            dve.wait_ge(s["rstd_set"], 10)
            modulate(1, 4 * DC)

            def top16(src, spare, values, where, n):
                for a in range(n):
                    step(nc.vector.max(values[:, a, 0:8], src[:, a, :]))
                settle()
                for a in range(n):
                    step(nc.vector.max_index(where[:, a, 0:8].bitcast(U32), values[:, a, 0:8], src[:, a, :]))
                for a in range(n):
                    step(nc.vector.match_replace(spare[:, a, :], values[:, a, 0:8], src[:, a, :], LOWEST))
                settle()
                for a in range(n):
                    step(nc.vector.max(values[:, a, 8:16], spare[:, a, :]))
                settle()
                for a in range(n):
                    step(nc.vector.max_index(where[:, a, 8:16].bitcast(U32), values[:, a, 8:16], spare[:, a, :]))
                settle()

            grid = [P, HEADS, TOPK, TOPK]
            iota16 = iota[:, 0:TOPK].unsqueeze(1).unsqueeze(1).broadcast_to(grid)
            for tt in range(2):
                dve.wait_ge(s["keys_evacuated"], tt + 1)
                top16(keys_s, keys_s2, top_v, top_i, 16)
                step(nc.vector.tensor_copy(top_if, top_i.bitcast(U32)))
                tv = top_v.rearrange("p (h a) k -> p h a k", a=2)
                step(nc.vector.tensor_tensor(cand.rearrange("p h (a b) -> p h a b", b=TOPK),
                                             tv[:, :, 0, :].unsqueeze(3).broadcast_to(grid),
                                             tv[:, :, 1, :].unsqueeze(2).broadcast_to(grid), ALU.add))
                settle()
                top16(cand, cand2, best_v, best_i, HEADS)
                nc.vector.tensor_tensor(best_e, best_v, best_v[:, :, 0:1].broadcast_to([P, HEADS, TOPK]),
                                        ALU.subtract).then_inc(s["topk_set"], 1)
                if tt:
                    dve.wait_ge(s["choice_turned"], tt)
                tif = top_if.rearrange("p (h a) k -> p h a k", a=2)
                for a, (op, by) in enumerate(((ALU.logical_shift_right, 4), (ALU.bitwise_and, 15))):
                    step(nc.vector.tensor_scalar(best_a.bitcast(U32), best_i.bitcast(U32), by, None, op))
                    settle()
                    step(nc.vector.tensor_copy(best_f, best_a.bitcast(U32)))
                    settle()
                    h4 = hot16.rearrange("p h (a b) -> p h a b", b=TOPK)
                    step(nc.vector.tensor_tensor(h4, best_f.unsqueeze(3).broadcast_to(grid), iota16, ALU.is_equal))
                    settle()
                    step(nc.vector.tensor_tensor(h4, h4, tif[:, :, a, :].unsqueeze(2).broadcast_to(grid), ALU.mult))
                    settle()
                    step(nc.vector.tensor_reduce(choice[:, a, :].rearrange("p (h k) -> p h k", k=TOPK), h4, AX_X, ALU.add))
                    settle()
                dve.wait_ge(s["act_used"], tt + 1)
                step(nc.vector.tensor_reduce(gate_sum, best_e, AX_X, ALU.add))
                settle()
                step(nc.vector.reciprocal(gate_sum, gate_sum))
                settle()
                nc.vector.tensor_tensor(choice[:, 2, :].rearrange("p (h k) -> p h k", k=TOPK), best_e,
                                        gate_sum.unsqueeze(2).broadcast_to([P, HEADS, TOPK]), ALU.mult).then_inc(s["topk_set"], 1)

            dve.wait_ge(s["choice_t_set"], 2)

            def hots(i, k, again):
                n = i * 2 + k
                for q in range(4):
                    tok = n * 4 + q
                    cols = bass.ds(tok, 1) if again else slice(tok, tok + 1)
                    nc.vector.tensor_scalar(hot1[:, 4 * k + q, :], iota[:, :], idx1_t[:, cols], None, ALU.is_equal)
                    ins = nc.vector.tensor_scalar(hot2[:, 4 * k + q, :], iota[:, :], idx2_t[:, cols], gate_t[:, cols], ALU.is_equal, ALU.mult)
                ins.then_inc(s["hot_set"], 1)

            hots(0, 0, False)
            hots(0, 1, False)
            with dve.Fori(1, N2 // 8) as i:
                for k in range(2):
                    dve.wait_ge(s["gates_set"], i * 2 + k - 1)
                    hots(i, k, True)

            def pick(e, k):
                nc.vector.tensor_tensor(picked[:, k:k + 1, :], act_sb[:, k:k + 1, :], gates[:, bass.ds(e, 1), :], ALU.mult).then_inc(s["peer_picked"], 1)

            for k in range(4):
                dve.wait_ge(s["peer_gelu_set"], k + 1)
                nc.vector.tensor_tensor(picked[:, k, :], act_sb[:, k, :], gates[:, k, :], ALU.mult).then_inc(s["peer_picked"], 1)
            with dve.Fori(1, KEYS // 4) as i:
                for k in range(4):
                    dve.wait_ge(s["peer_gelu_set"], i * 4 + k + 1)
                    dve.wait_ge(s["down_used"], i * 4 + k - 3)
                    pick(i * 4 + k, k)
            dve.wait_ge(s["down_used"], KEYS)
            for c in range(DC):
                ins = nc.vector.scalar_tensor_tensor(out=resid[:, c, 0:N2], in0=flat[:, c * N2:(c + 1) * N2],
                                                     scalar=modv[:, 5 * DC + c:5 * DC + c + 1], in1=resid[:, c, 0:N2],
                                                     op0=ALU.mult, op1=ALU.add)
            ins.then_inc(s["resid_set"], 1)
            dve.wait_ge(s["rstd_set"], 11)
            normalise(lin_out, resid, ("final", 0), DC, N2, "final_set")


def tiles_of(w):
    k, m = w.shape
    return w.reshape(k // P, P, m // P, P).transpose(2, 1, 0, 3).reshape(m // P, P, k)


def column(v):
    return v.reshape(-1, P).T


def kernel(x, meta_tokens, rel_bias, ln_pre_mix, ln_post_mix, ln_pre_ffn, ln_post_ffn, w_in, b_forget,
           sinks, w_out, w_gate_up, w_down, c_2, w_ada_2, b_ada_2, w_in_2, swa_sink_2, mla_q_norm_2,
           w_mla_q_up_2, mla_kv_norm_2, w_mla_kv_up_2, out_norm_swa_2, out_norm_mla_2, w_out_2,
           w_peer_query_2, peer_sub_keys_2, peer_expert_u_2, peer_expert_v_2, final_norm_2):
    import concourse.bacc as bacc
    from concourse.bass_utils import run_bass_kernel_spmd

    cat = np.concatenate
    swa = np.array([h * DH + i for h in SLOT_HEAD for i in range(DH)])

    tokens = cat([x[0, P:], x[0, :P], meta_tokens], 0)
    x_t = np.ascontiguousarray(tokens.T.reshape(DC, P, N1).transpose(1, 0, 2))

    w1 = w_in[0]
    q_a, k_a, v_a, q_b, k_b, v_b, f_b = np.split(w1, [512, 640, 768, 1280, 1792, 2304], axis=1)
    w2 = w_in_2[0]
    q_2, k_2, v_2, q_lat, kv_lat, k_rope = np.split(w2, [512, 640, 768, 1024, 1152], axis=1)
    gate_up = w_gate_up[0].reshape(D, 2, FC, P).transpose(0, 2, 1, 3).reshape(D, 2 * FF)
    down = w_down[0].reshape(FC, P, DC, P).transpose(2, 0, 1, 3).reshape(FC, DC, P, P).transpose(0, 2, 1, 3).reshape(FC, P, D)
    out1 = cat([w_out[0][:512][swa], w_out[0][512:]], 0)
    out2 = cat([w_out_2[0][:512][swa], w_out_2[0][512:]], 0)
    sub = peer_sub_keys_2[0].reshape(2, 8, KEYS, P).transpose(0, 3, 1, 2).reshape(2, P, D)
    weights = cat([
        tiles_of(cat([q_a[:, swa], k_a, q_b, k_b, v_a, v_b], 1)),
        tiles_of(w_ada_2[0]),
        tiles_of(out1), tiles_of(gate_up), down,
        tiles_of(cat([q_2[:, swa], k_2, q_lat, kv_lat, k_rope, k_rope, k_rope, k_rope, v_2], 1)),
        tiles_of(out2), tiles_of(w_peer_query_2[0]), sub,
    ], 0)
    up_experts = peer_expert_u_2[0].reshape(KEYS, KEYS, DC, P).transpose(0, 3, 2, 1).reshape(KEYS, P, D)
    down_experts = peer_expert_v_2[0].reshape(KEYS, KEYS, D)
    small = cat([w_mla_q_up_2[0].reshape(QR_C, P, HEADS * QK).transpose(1, 0, 2).reshape(P, -1), w_mla_kv_up_2[0]], 1)
    slots = np.array(SLOT_HEAD)
    vectors = cat([
        column(ln_pre_mix[0]), column(ln_post_mix[0]), column(ln_pre_ffn[0]), column(ln_post_ffn[0]), column(b_ada_2[0]),
        column(mla_q_norm_2[0]), column(mla_kv_norm_2[0]), column(out_norm_swa_2[0][swa]), column(out_norm_mla_2[0]),
        column(final_norm_2), column(c_2[0]),
        np.broadcast_to(sinks[0][slots], (P, HEADS)), np.broadcast_to(swa_sink_2[0][slots], (P, HEADS)),
    ], 1)
    arrays = {
        "x_t": x_t, "weights": weights, "up_experts": up_experts, "down_experts": down_experts, "small": small,
        "vectors": vectors, "w_f": f_b.reshape(DC, P, HEADS).transpose(1, 0, 2), "b_f": b_forget.reshape(HEADS, 1),
        "rel": rel_bias[:, slots], "const": shape_constants(),
    }
    arrays = {n: np.ascontiguousarray(a) for n, a in arrays.items()}
    nc = bacc.Bacc("TRN2", target_bir_lowering=False, num_devices=1)
    aps = {n: nc.dram_tensor(n, a.shape, F32, kind="ExternalInput").ap() for n, a in arrays.items()}
    scratch = nc.dram_tensor("bias_scratch", [HEADS, N_BIAS], F32, kind="Internal").ap()
    out = nc.dram_tensor("out_t", [P, DC, N2], F32, kind="ExternalOutput").ap()
    build(nc, *[aps[n] for n in ("x_t", "weights", "up_experts", "down_experts", "small", "vectors", "w_f", "b_f", "rel", "const")],
          scratch, out)
    got = run_bass_kernel_spmd(nc, [arrays], core_ids=[0]).results[0]["out_t"]
    got = got.transpose(2, 1, 0).reshape(N2, D)
    return np.ascontiguousarray(cat([got[P:], got[:P]], 0)[None])
```

```python
from contextlib import ExitStack

import numpy as np

import concourse.bass as bass
from concourse import mybir

F32 = mybir.dt.float32
F32R = mybir.dt.float32r
U32 = mybir.dt.uint32
ALU = mybir.AluOpType
ACT = mybir.ActivationFunctionType
AX_X = mybir.AxisListType.X

P = 128
D = 1024
DC = D // P
SEQ = 256
META = 16
N1 = SEQ + META
N2 = SEQ
HEADS = 8
DH = 64
FF = 2816
FC = FF // P
EPS = 1e-6
NEG = -1e30
LOWEST = -3.0e38
WINDOW = 128
BUCKETS = 32
MAX_DISTANCE = 128

NOPE = 64
ROPE = 32
QK = NOPE + ROPE
QR_C = 2
KEYS = 128
TOPK = 16
PAIRS = HEADS * TOPK

TILE_COLS = [(0, P), (P, P), (2 * P, META)]

RING = 8
HIGHS = 4
LEAD = 3
N_QK1, N_V1, N_OUT, N_QK2, N_V2, N_QUERY, N_SUB = 13, 5, DC, 9, 1, 16, 2
N_FFN, N_DOWN, N_ADA = 2 * FC, FC, 6 * DC
T_QK1 = 0
T_V1 = T_QK1 + N_QK1
T_OUT1 = T_V1 + N_V1
T_FFN = T_OUT1 + N_OUT
T_DOWN = T_FFN + N_FFN
T_QK2 = T_DOWN + N_DOWN
T_V2 = T_QK2 + N_QK2
T_OUT2 = T_V2 + N_V2
T_QUERY = T_OUT2 + N_OUT
T_SUB = T_QUERY + N_QUERY
T_UP = T_SUB + N_SUB
T_DOWN_E = T_UP + KEYS
T_END = T_DOWN_E + KEYS
assert T_UP % RING == 0


def split_of(t):
    assert not T_SUB <= t < T_UP
    return t if t < T_SUB else t - N_SUB


def tile_of(n):
    return n if n < T_SUB else n + N_SUB


VEC = {}
_at = 0
for _name, _n in (("pre_mix", DC), ("post_mix", DC), ("pre_ffn", DC), ("post_ffn", DC), ("b_ada", 6 * DC),
                  ("q_norm", QR_C), ("kv_norm", 1), ("out_norm", DC), ("final", DC),
                  ("sinks1", HEADS), ("sinks2", HEADS)):
    VEC[_name] = (_at, _n)
    _at += _n
N_VEC = _at

SLOT_HEAD = [c + 4 * half for c in range(4) for half in range(2)]

BIAS_OWN = (0, 255, 0, -127)
BIAS_PREV = (255, 255, P, -127)
BIAS_META1 = (510, 143, META + P, -127)
BIAS_META0 = (653, 143, META, -127)
BIAS_MM = (796, 31, 0, -15)
N_BIAS = 827

CONST = {}
_at = 0
for _name, _n in (("ident", P), ("iota", P), ("flip", P), ("rot64", P), ("rot32", P), ("cos64", N2), ("sin64", N2),
                  ("cos32", N2), ("sin32", N2), ("causal1", N1), ("causal0", N1 - P), ("causalm", META),
                  ("band1", N2), ("band0", N2), ("select", HEADS * P), ("bucket", N_BIAS), ("bmask", N_BIAS)):
    CONST[_name] = (_at, _n)
    _at += _n
N_CONST = _at


def bucket_of(d):
    n = np.maximum(d, 0)
    exact = BUCKETS // 2
    nf = np.maximum(n, 1).astype(np.float32)
    large = exact + (np.log(nf / np.float32(exact)) / np.float32(np.log(MAX_DISTANCE / exact))
                     * np.float32(BUCKETS - exact)).astype(np.int32)
    return np.where(n < exact, n, np.minimum(large, BUCKETS - 1))


def shape_constants():
    out = np.zeros((P, N_CONST), np.float32)

    def put(name, a):
        at, n = CONST[name]
        assert a.shape[1] == n
        out[:a.shape[0], at:at + n] = a

    row = np.arange(P)
    put("ident", np.eye(P))
    put("iota", np.broadcast_to(row.astype(np.float32), (P, P)))
    put("flip", np.eye(P)[::-1])
    pos = np.concatenate([np.arange(P, 2 * P), np.arange(P)]).astype(np.float32)
    for dim in (64, 32):
        half = dim // 2
        inv = (1.0 / (np.float32(10000.0) ** (np.arange(0, dim, 2, dtype=np.float32) / np.float32(dim)))).astype(np.float32)
        ang = (inv[row % half][:, None] * pos[None, :]).astype(np.float32)
        put(f"cos{dim}", np.cos(ang))
        put(f"sin{dim}", np.sin(ang))
        rot = np.zeros((P, P), np.float32)
        for i in range(P):
            if i % dim < half:
                rot[i + half, i] = -1.0
            else:
                rot[i - half, i] = 1.0
        put(f"rot{dim}", rot)
    q = row[:, None]
    k = row[None, :]
    causal = np.where(k <= q, 0.0, NEG)
    put("causal1", np.concatenate([causal, np.zeros((P, P + META))], 1))
    put("causal0", np.concatenate([causal, np.zeros((P, META))], 1))
    put("causalm", causal[:META, :META])
    both = np.concatenate([k + P, k], 1)
    put("band1", np.where(np.abs(both - (q + P)) <= WINDOW, 0.0, NEG))
    put("band0", np.where(np.abs(both - q) <= WINDOW, 0.0, NEG))
    sel = np.zeros((HEADS, HEADS, P), np.float32)
    for h in range(HEADS):
        sel[h, h] = -1.0
    put("select", sel.reshape(HEADS, HEADS * P))
    hot = np.zeros((BUCKETS, N_BIAS), np.float32)
    mask = np.zeros((HEADS, N_BIAS), np.float32)
    for at, n, d0, u0 in (BIAS_OWN, BIAS_PREV, BIAS_META1, BIAS_META0, BIAS_MM):
        d = d0 - (np.arange(n) + u0)
        hot[bucket_of(d), at + np.arange(n)] = 1.0
        dead = d < 0
        if (at, n, d0, u0) in (BIAS_OWN, BIAS_PREV):
            dead |= d >= WINDOW
        hot[:, at:at + n][:, dead] = 0.0
        mask[:, at:at + n][:, dead] = NEG
    put("bucket", hot)
    put("bmask", mask)
    return out


def build(nc, x_t, weights, w_ada, cond_row, up_experts, down_experts, small, vectors, w_f, b_f, rel, const, scratch, out):
    ctx = ExitStack()
    with ctx:
        base = -(-nc.sbuf_base // 32) * 32
        top = [0]

        def put(name, shape, at=None, dt=F32):
            cols = int(np.prod(shape[1:]))
            if at is None:
                at = top[0]
                top[0] += cols
            return nc.alloc_sbuf_tensor_at(name, shape, dt, offset=base + 4 * at, align_bytes=4).ap()

        ring = put("ring", [P, RING, D])
        ring_low = put("ring_low", [P, RING, D], 0, F32R)
        w_high = put("w_high", [P, HIGHS, D], dt=F32R)
        x_at = top[0]
        x_both = put("x_both", [P, 2 * DC * N1 + P - META], dt=F32R)
        x_high = x_both[:, 0:DC * N1].rearrange("p (c n) -> p c n", n=N1)
        x_low = x_both[:, DC * N1:2 * DC * N1].rearrange("p (c n) -> p c n", n=N1)
        resid = put("resid", [P, DC, N1])
        vec = put("vec", [P, N_VEC])
        modv = put("modv", [P, 6 * DC])
        eps = put("eps", [P, 1])
        ident = put("ident", [P, P])
        iota = put("iota", [P, P])
        ones = put("ones", [P, P])
        choice = put("choice", [P, 3, 2, PAIRS])
        gate_sum = put("gate_sum", [P, 2 * HEADS])
        choice_t = choice[:, :, :, :].rearrange("p k a n -> p k (a n)")

        arena = top[0]
        acts = put("acts", [P, KEYS, N2])
        assert base + 4 * top[0] <= nc.sbuf_usable_end
        end = top[0]
        top[0] = arena
        consts = put("consts", [P, N_CONST])

        def cst(name, rows=P):
            at, n = CONST[name]
            return consts[0:rows, at:at + n]

        squares = put("squares", [P, DC, N1])
        cond = put("cond", [P, D], top[0] - DC * N1)
        rstd = put("rstd", [P, N1])
        small_sb = put("small_sb", [P, QR_C * HEADS * QK + HEADS * (NOPE + DH)])
        w_f_sb = put("w_f_sb", [P, DC, HEADS])
        bf_sb = put("bf_sb", [P, 1])
        rel_sb = put("rel_sb", [P, HEADS])
        cum_q = put("cum_q", [P, 3, HEADS])
        stats = [put(f"stats{i}", [P, 16]) for i in range(2)]
        lin_at = top[0]
        lin_out = put("lin_out", [P, DC, N1])
        ada_slots = put("ada_slots", [P, 2, D], lin_at)
        ffn_at = top[0]
        qk = put("qk", [P, N_QK1, N1])
        k_mla = qk[:, 0:HEADS, 0:N2]
        v_nat = put("v_nat", [P, 3, N_V1 * P])
        score_at = top[0]
        probs_t = [put(f"probs_t{i}", [P, 3, 4 * P]) for i in range(2)]
        score = [put(f"score{i}", [P, 4, N1 + 2]) for i in range(2)]
        rope_tmp2 = put("rope_tmp2", [P, DC, N2], score_at)
        mixed_at = top[0]
        mixed = put("mixed", [P, DC, N1])
        f_work = put("f_work", [P, 6, N1], mixed_at)
        bias_at = top[0]
        bias1 = put("bias1", [P, HEADS, N1])
        bias_vec = put("bias_vec", [P, N_BIAS], top[0])
        bias0, biasm = put("bias0", [P, HEADS, N1 - P]), put("biasm", [P, HEADS, META])
        fox1, fox0, foxm = put("fox1", [P, HEADS, N1]), put("fox0", [P, HEADS, N1 - P]), put("foxm", [P, HEADS, META])
        assert top[0] <= end
        normed = put("normed", [P, DC, N1], bias_at)
        rope_q = put("rope_q", [P, 5, N2], bias_at + DC * N1)
        q_mla = put("q_mla", [P, HEADS, N2], bias_at + DC * N1 + 5 * N2)
        ffn_high = put("ffn_high", [P, FC, N1], ffn_at, F32R)
        ffn_low = put("ffn_low", [P, FC, N1], ffn_at + FC * N1, F32R)
        silu_sb = put("silu_sb", [P, 4, N1], ffn_at + 2 * FC * N1)
        assert ffn_at + 2 * FC * N1 + 4 * N1 <= bias_at + DC * N1 + 5 * N2 + DC * N2 and 2 * FC * N1 <= bias_at - ffn_at
        top[0] = arena + KEYS * N2 // 2
        keys_s = put("keys_s", [P, 2, 16, P])
        query_at = top[0]
        query = put("query", [P, 16, N2])
        spare = put("spare", [P, 16, P], query_at)
        cand = put("cand", [P, HEADS, TOPK * TOPK], query_at + 16 * P)
        cand2 = put("cand2", [P, HEADS, TOPK * TOPK], query_at)
        top_v, top_i, top_if = (put(n, [P, 16, TOPK]) for n in ("top_v", "top_i", "top_if"))
        best_v, best_i, best_a, best_f = (put(n, [P, HEADS, TOPK]) for n in ("best_v", "best_i", "best_a", "best_f"))
        assert top[0] <= end
        hot1 = put("hot1", [P, 2, 8, P], x_at)
        hot2 = put("hot2", [P, 2, 8, P], x_at + 16 * P)
        zeros = put("zeros", [P, 512], x_at + 4 * N1)

        psum = ctx.enter_context(nc.psum_tensor("psum", [P, 8, 512], F32))
        bank = [psum[:, b, :] for b in range(8)]
        flat = psum[:, :, :].rearrange("p b n -> p (b n)")

        names = """
            inputs_landed consts_landed ones_set bias_summed bias_vec_set bias_vec_stored
            bias_tables_landed bias_flipped bias_taken squared norm_summed rstd_set normed_set
            high_set low_set tile_used x_high_set x_low_set proj_evacuated
            forget_done forget_set forget_exp cum_set cum_turned cum_q_set cum_spread fox_tables_set
            cond_set ada_used mod_set
            scores_done scores_read max_set exp_done probs_set probs_turned probs_t_set
            attended mixed_set modulated resid_set silu_set ffn_act_set ffn_high_set ffn_low_set
            rot_done rope_set k_rope_set mla_up_done mla_up_set
            keys_scored keys_evacuated topk_set gate_exp_set gates_ready choice_turned choice_t_set
            hot1_set second_apart hot2_set hot1_scaled gates_done gates_used gelu_set zeros_set
            picked_high_set picked_low_set final_set out_stored vector_step scalar_step
        """.split()
        s = {n: ctx.enter_context(nc.semaphore(n)) for n in names}
        landed = [ctx.enter_context(nc.semaphore(f"landed{i}")) for i in range(RING)]
        ada_landed = [ctx.enter_context(nc.semaphore(f"ada_landed{i}")) for i in range(2)]
        cond_landed = ctx.enter_context(nc.semaphore("cond_landed"))

        def vcol(name, j=0):
            at, n = VEC[name]
            assert j < n
            return vec[:, at + j:at + j + 1]

        R_F, R_QK1, R_V1 = 0, 1, 1 + N_QK1
        R_OUT1 = R_V1 + N_V1
        R_DOWN = R_OUT1 + DC
        R_QK2 = R_DOWN + DC
        R_V2 = R_QK2 + N_QK2
        R_OUT2 = R_V2 + N_V2
        R_QUERY = R_OUT2 + DC

        units1 = [(kind, g, qt) for kind in (0, 1) for g in (0, 1) for qt in (0, 1, 2)]
        units2 = [(kind, g, qt) for kind in (2, 3) for g in (0, 1) for qt in (0, 1)]
        units = units1 + units2

        def shape_of(u):
            kind, _, qt = units[u]
            q0, nq = TILE_COLS[qt]
            if kind >= 2:
                return 0, N2, q0, nq
            return q0, N1 - q0, q0, nq

        def key_blocks(u):
            kind, _, qt = units[u]
            k0 = shape_of(u)[0]
            last = 3 if kind < 2 else 2
            first = qt if kind < 2 else 0
            return [(t, TILE_COLS[t][0] - k0, TILE_COLS[t][1]) for t in range(first, last)]

        flips = []
        for src, dst, rows in ((fox1, bias1, P), (fox0, bias0, P), (foxm, biasm, META)):
            src, dst = (a.rearrange("p h k -> p (h k)") for a in (src, dst))
            for c in range(0, src.shape[1], 512):
                n = min(512, src.shape[1] - c)
                flips.append((src[0:rows, c:c + n], dst[0:rows, c:c + n], rows, n))

        def has_sink(u):
            return units[u][0] in (0, 2)

        block = ctx.enter_context(nc.Block())

        @block.sync
        def _(sp):
            for slot in range(RING):
                sp.dma_start(ring[:, slot, :], weights[slot]).then_inc(landed[slot], 16)
            for first, n, source in ((RING, T_UP, weights), (T_UP, T_DOWN_E, up_experts), (T_DOWN_E, T_END, down_experts)):
                start = 1 if first == RING else 0
                tiles = n - first + start * RING
                with sp.Fori(start, tiles // RING) as i:
                    for slot in range(RING):
                        sp.wait_ge(s["tile_used"], i * RING + (first - start * RING) + slot - RING + 1)
                        sp.dma_start(ring[:, slot, :], source[bass.ds(i * RING + slot, 1)].rearrange("a p n -> p (a n)")).then_inc(landed[slot], 16)
            sp.wait_ge(s["final_set"], 1)
            sp.dma_start(out, lin_out[:, :, 0:N2]).then_inc(s["out_stored"], 16)
            sp.wait_ge(s["out_stored"], 16)

        @block.gpsimd
        def _(pool):
            nc.gpsimd.memset(ones[:, :], 1.0).then_inc(s["ones_set"], 1)
            nc.gpsimd.memset(x_both[:, 2 * DC * N1:2 * DC * N1 + P - META].bitcast(F32), 0.0).then_inc(s["ones_set"], 1)
            nc.gpsimd.memset(eps[:, :], EPS).then_inc(s["ones_set"], 1)
            pool.wait_ge(s["norm_summed"], 1)
            pool.dma_start(cond[:, :], cond_row.partition_broadcast(P)).then_inc(cond_landed, 16)
            for j in range(2):
                pool.dma_start(ada_slots[:, j, :], w_ada[j]).then_inc(ada_landed[j], 16)
            pool.wait_ge(s["bias_vec_set"], 2)
            pool.dma_start(scratch, bias_vec[0:HEADS, :]).then_inc(s["bias_vec_stored"], 16)
            pool.wait_ge(s["bias_vec_stored"], 16)

            def rows(section, nq, nk):
                at, _, _, u0 = section
                return bass.AP(scratch.tensor, scratch.offset + at - u0 - (nq - 1), [[1, nq], [N_BIAS, HEADS], [1, nk]])

            pool.dma_start(fox1[:, :, 0:P], rows(BIAS_OWN, P, P)).then_inc(s["bias_tables_landed"], 16)
            pool.dma_start(fox1[:, :, P:2 * P], rows(BIAS_PREV, P, P)).then_inc(s["bias_tables_landed"], 16)
            pool.dma_start(fox1[:, :, 2 * P:N1], rows(BIAS_META1, P, META)).then_inc(s["bias_tables_landed"], 16)
            pool.dma_start(fox0[:, :, 0:P], rows(BIAS_OWN, P, P)).then_inc(s["bias_tables_landed"], 16)
            pool.dma_start(fox0[:, :, P:N1 - P], rows(BIAS_META0, P, META)).then_inc(s["bias_tables_landed"], 16)
            pool.dma_start(foxm[0:META, :, :], rows(BIAS_MM, META, META)).then_inc(s["bias_tables_landed"], 16)
            pool.wait_ge(s["consts_landed"], 16 * 8)

            with pool.Fori(1, N_ADA // 2) as i:
                for j in range(2):
                    pool.wait_ge(s["ada_used"], i * 2 + j - 1)
                    pool.dma_start(ada_slots[:, j, :], w_ada[bass.ds(i * 2 + j, 1)].rearrange("a p n -> p (a n)")).then_inc(ada_landed[j], 16)
            pool.wait_ge(s["choice_t_set"], 1)

            def second_distance(i, b):
                cols = choice_t[:, 1, bass.ds((i * 2 + b) * 8, 8)].unsqueeze(2).broadcast_to([P, 8, P])
                nc.gpsimd.tensor_tensor(hot2[:, b], iota[:, :].unsqueeze(1).broadcast_to([P, 8, P]), cols, ALU.subtract).then_inc(s["second_apart"], 1)

            for b in range(2):
                second_distance(0, b)
            with pool.Fori(1, N2 // 16) as i:
                for b in range(2):
                    pool.wait_ge(s["gates_done"], i * 2 + b - 1)
                    second_distance(i, b)
            pool.wait_ge(s["gates_done"], N2 // 8)
            nc.gpsimd.memset(zeros[:, :], 0.0).then_inc(s["zeros_set"], 1)

        @block.scalar
        def _(act):
            steps = [0]

            def step(ins):
                steps[0] += 1
                ins.then_inc(s["scalar_step"], 1)

            def settle():
                act.wait_ge(s["scalar_step"], steps[0])

            act.dma_start(resid[:, :, :], x_t).then_inc(s["inputs_landed"], 16)
            act.dma_start(consts, const).then_inc(s["consts_landed"], 16)
            act.dma_start(vec[:, :], vectors).then_inc(s["consts_landed"], 16)
            act.dma_start(ident[:, :], const[:, 0:P]).then_inc(s["consts_landed"], 16)
            act.dma_start(iota[:, :], const[:, P:2 * P]).then_inc(s["consts_landed"], 16)
            act.dma_start(w_f_sb, w_f).then_inc(s["consts_landed"], 16)
            act.dma_start(bf_sb[0:HEADS, :], b_f).then_inc(s["consts_landed"], 16)
            act.dma_start(rel_sb[0:BUCKETS, :], rel).then_inc(s["consts_landed"], 16)
            act.dma_start(small_sb, small).then_inc(s["consts_landed"], 16)

            def norm(k, src, chunks, n):
                nc.scalar.activation(squares[:, 0:chunks, 0:n], src, ACT.Square).then_inc(s["squared"], 1)
                act.wait_ge(s["norm_summed"], k)
                step(nc.scalar.activation(rstd[:, 0:n], bank[7][:, 0:n], ACT.Ln, bias=eps[:, 0:1], scale=1.0 / (chunks * P)))
                settle()
                nc.scalar.activation(rstd[:, 0:n], rstd[:, 0:n], ACT.Exp, scale=-0.5).then_inc(s["rstd_set"], 1)

            def high(t):
                n = split_of(t)
                act.wait_ge(landed[t % RING], 16 * (t // RING + 1))
                if n >= HIGHS:
                    act.wait_ge(s["tile_used"], tile_of(n - HIGHS) + 1)
                nc.scalar.activation(w_high[:, n % HIGHS, :], ring[:, t % RING, :], ACT.Copy).then_inc(s["high_set"], 1)

            next_high = [0]

            def high_to(t):
                while next_high[0] < t:
                    if not T_SUB <= next_high[0] < T_UP:
                        high(next_high[0])
                    next_high[0] += 1

            def x_highs(src, n, ready):
                for half in range(2):
                    ready(half)
                    c = slice(4 * half, 4 * half + 4)
                    nc.scalar.activation(x_high[:, c, 0:n], src[:, c, 0:n], ACT.Copy).then_inc(s["x_high_set"], 1)

            def evacuate(r, t, dst, src, scale=1.0, more=()):
                high_to(min(t + 1 + LEAD, T_SUB))
                act.wait_ge(s["tile_used"], t + 1)
                ins = nc.scalar.activation(dst, src, ACT.Copy, scale=scale)
                for d, f in more:
                    ins = nc.scalar.activation(d, f, ACT.Copy)
                ins.then_inc(s["proj_evacuated"], 1)

            act.wait_ge(s["inputs_landed"], 16)
            act.wait_ge(s["ones_set"], 3)
            high_to(LEAD)
            norm(1, resid[:, :, :], DC, N1)
            x_highs(normed, N1, lambda half: act.wait_ge(s["normed_set"], half + 1))
            act.wait_ge(s["forget_done"], 1)
            nc.scalar.activation(f_work[0:HEADS, 0, :], bank[R_F % 4][0:HEADS, 0:N1], ACT.Copy).then_inc(s["proj_evacuated"], 1)
            act.wait_ge(s["forget_set"], 1)
            step(nc.scalar.activation(f_work[0:HEADS, 1, :], f_work[0:HEADS, 0, :], ACT.Abs))
            settle()
            step(nc.scalar.activation(f_work[0:HEADS, 2, :], f_work[0:HEADS, 1, :], ACT.Exp, scale=-1.0))
            settle()
            nc.scalar.activation(f_work[0:HEADS, 1, :], f_work[0:HEADS, 2, :], ACT.Ln, bias=ones[0:HEADS, 0:1]).then_inc(s["forget_exp"], 1)
            act.wait_ge(cond_landed, 16)
            nc.scalar.activation(cond[:, :], cond[:, :], ACT.Silu).then_inc(s["cond_set"], 1)
            for j in range(N_QK1):
                r = R_QK1 + j
                evacuate(r, T_QK1 + j, qk[:, j, :], bank[r % 4][:, 0:N1], scale=0.125 if j < 4 or 5 <= j < 9 else 1.0)
            for j in range(N_V1):
                r = R_V1 + j
                b = bank[r % 4][:, 0:3 * P].rearrange("p (t n) -> p t n", n=P)
                evacuate(r, T_V1 + j, v_nat[:, 0:2, j * P:(j + 1) * P], b[:, 0:2, :],
                         more=[(v_nat[0:META, 2, j * P:(j + 1) * P], b[0:META, 2, :])])

            for n, (_, dst, rows, cols) in enumerate(flips):
                act.wait_ge(s["bias_flipped"], n + 1)
                nc.scalar.activation(dst, bank[4 + n % 4][0:rows, 0:cols], ACT.Copy).then_inc(s["bias_taken"], 1)

            def exps(u):
                _, nk, _, nq = shape_of(u)
                n = nk + has_sink(u)
                act.wait_ge(s["max_set"], u + 1)
                for h in range(4):
                    ins = nc.scalar.activation(score[u % 2][0:nq, h, 0:n], score[u % 2][0:nq, h, 0:n], ACT.Exp,
                                               bias=stats[u % 2][0:nq, 4 + h:5 + h],
                                               accum_out=stats[u % 2][0:nq, 8 + h:9 + h])
                ins.then_inc(s["exp_done"], 1)

            def take_probs_t(u):
                nq = shape_of(u)[3]
                act.wait_ge(s["probs_turned"], u + 1)
                if u >= 2:
                    act.wait_ge(s["attended"], u - 1)
                for t, _, kn in key_blocks(u):
                    ins = nc.scalar.activation(
                        probs_t[u % 2][0:kn, t, :].rearrange("p (h q) -> p h q", q=P)[:, :, 0:nq],
                        bank[4 + t][0:kn, :].rearrange("p (h q) -> p h q", q=P)[:, :, 0:nq], ACT.Copy)
                ins.then_inc(s["probs_t_set"], 1)

            def attention(u0, u1):
                for u in range(u0, u1 + 1):
                    if u < u1:
                        exps(u)
                    if u > u0:
                        take_probs_t(u - 1)

            attention(0, len(units1))
            act.wait_ge(s["mixed_set"], len(units1))
            x_highs(mixed, N1, lambda half: None)
            for j in range(DC):
                r = R_OUT1 + j
                evacuate(r, T_OUT1 + j, lin_out[:, j, :], bank[r % 4][:, 0:N1])
            act.wait_ge(s["proj_evacuated"], R_OUT1 + DC)
            norm(2, lin_out, DC, N1)
            act.wait_ge(s["resid_set"], 1)
            norm(3, resid[:, :, :], DC, N1)
            x_highs(normed, N1, lambda half: act.wait_ge(s["normed_set"], 3 + half))

            def loop_high(i, t):
                n = split_of(t)
                act.wait_ge(landed[t % RING], (i + t // RING + 1) * 16)
                act.wait_ge(s["tile_used"], i * RING + t - HIGHS + 1)
                nc.scalar.activation(w_high[:, n % HIGHS, :], ring[:, t % RING, :], ACT.Copy).then_inc(s["high_set"], 1)

            def silu(j, k):
                act.wait_ge(s["tile_used"], j * 2 + T_FFN + 2)
                nc.scalar.activation(silu_sb[:, k, :], bank[2 * k][:, 0:N1], ACT.Silu).then_inc(s["silu_set"], 1)

            def ffn_highs(j, at, k):
                act.wait_ge(s["ffn_act_set"], j + 1)
                nc.scalar.activation(ffn_high[:, at, :], silu_sb[:, k:k + 1, :], ACT.Copy).then_inc(s["ffn_high_set"], 1)

            def silu_pair(i, k):
                j = i * 4 + k
                unrolled = isinstance(i, int)
                for d in (0, 1):
                    loop_high(i, T_FFN + 2 * k + LEAD + d)
                if not (unrolled and i == 0):
                    act.wait_ge(s["ffn_low_set"], j - 3)
                silu(j, k)
                if not (unrolled and j == 0):
                    ffn_highs(j - 1, slice(j - 1, j) if unrolled else bass.ds(j - 1, 1), (k - 1) % 4)

            for k in range(4):
                silu_pair(0, k)
            with act.Fori(1, FC // 4) as i:
                for k in range(4):
                    silu_pair(i, k)
            for k in range(FC % 4):
                silu_pair(FC // 4, k)
            ffn_highs(FC - 1, slice(FC - 1, FC), (FC - 1) % 4)
            next_high[0] = T_DOWN + LEAD
            for j in range(DC):
                r = R_DOWN + j
                evacuate(r, T_DOWN + (j * FC + FC - 1) // DC, lin_out[:, j, :], bank[r % 4][:, 0:N1])
            act.wait_ge(s["proj_evacuated"], R_DOWN + DC)
            norm(4, lin_out, DC, N1)

            act.wait_ge(s["resid_set"], 2)
            norm(5, resid[:, :, 0:N2], DC, N2)

            def add_shift(n, at):
                for c in range(DC):
                    act.wait_ge(s["modulated"], n * DC + c + 1)
                    ins = nc.scalar.activation(normed[:, c, 0:N2], normed[:, c, 0:N2], ACT.Identity,
                                               bias=modv[:, at + c:at + c + 1])
                    step(ins)
                settle()
                x_highs(normed, N2, lambda half: None)

            add_shift(0, 0)
            for j in range(N_QK2):
                r = R_QK2 + j
                evacuate(r, T_QK2 + j, qk[:, j, 0:N2], bank[r % 4][:, 0:N2], scale=0.125 if j < 4 else 1.0)
            b = bank[R_V2 % 4][:, 0:2 * P].rearrange("p (t n) -> p t n", n=P)
            evacuate(R_V2, T_V2, v_nat[:, 0:2, 0:P], b)
            act.wait_ge(s["proj_evacuated"], R_QK2 + N_QK2)
            norm(6, qk[:, 5:7, 0:N2], QR_C, N2)
            act.wait_ge(s["normed_set"], 5)
            norm(7, qk[:, 7:8, 0:N2], 1, N2)
            act.wait_ge(s["mla_up_done"], 1)
            nc.scalar.activation(q_mla[0:QK, :, :], flat[0:QK, 0:HEADS * N2].rearrange("p (h n) -> p h n", n=N2),
                                 ACT.Copy, scale=float(QK) ** -0.5).then_inc(s["mla_up_set"], 1)
            act.wait_ge(s["mla_up_done"], 2)
            nc.scalar.activation(v_nat[:, 0:2, P:P + HEADS * DH],
                                 flat[:, 2048:3072].rearrange("p (t n) -> p t n", n=512), ACT.Copy).then_inc(s["mla_up_set"], 1)
            act.wait_ge(s["mla_up_done"], 3)
            act.wait_ge(s["rope_set"], 2)
            nc.scalar.activation(k_mla[0:NOPE, :, :], flat[0:NOPE, 0:HEADS * N2].rearrange("p (h n) -> p h n", n=N2),
                                 ACT.Copy).then_inc(s["mla_up_set"], 1)
            attention(len(units1), len(units))
            act.wait_ge(s["mixed_set"], len(units))
            norm(8, mixed[:, 0:4, 0:N2], 4, N2)
            act.wait_ge(s["normed_set"], 7)
            norm(9, mixed[:, 4:8, 0:N2], 4, N2)
            x_highs(normed, N2, lambda half: act.wait_ge(s["normed_set"], 7 + half))
            for j in range(DC):
                high_to(T_OUT2 + j + 1 + LEAD)
            act.wait_ge(s["proj_evacuated"], R_OUT2 + DC)
            norm(10, resid[:, :, 0:N2], DC, N2)
            add_shift(1, 3 * DC)
            for j in range(N_QUERY):
                r = R_QUERY + j
                evacuate(r, T_QUERY + j, query[:, j, :], bank[r % 4][:, 0:N2])
            for tt in range(2):
                act.wait_ge(s["keys_scored"] if tt == 0 else s["tile_used"], 1 if tt == 0 else T_UP)
                nc.scalar.activation(keys_s[:, tt], flat[:, tt * 2048:(tt + 1) * 2048].rearrange("p (a n) -> p a n", n=P),
                                     ACT.Copy).then_inc(s["keys_evacuated"], 1)

            def gelu(e, at, k):
                act.wait_ge(s["tile_used"], e + T_UP + 1)
                nc.scalar.activation(acts[:, at, :], bank[4 + k][:, 0:N2].unsqueeze(1), ACT.Gelu).then_inc(s["gelu_set"], 1)

            high_to(T_UP + LEAD)
            for e in range(RING):
                high_to(T_UP + e + 1 + LEAD)
                gelu(e, slice(e, e + 1), e % 4)

            def gelus(first, last):
                with act.Fori(first, last) as i:
                    for k in range(RING):
                        loop_high(i, T_UP + k + LEAD)
                        e = i * RING + k
                        gelu(e, bass.ds(e, 1), k % 4)

            gelus(1, KEYS // RING // 2)
            act.wait_ge(s["topk_set"], 1)
            nc.scalar.activation(choice[:, 2], choice[:, 2], ACT.Exp).then_inc(s["gate_exp_set"], 1)
            gelus(KEYS // RING // 2, KEYS // RING)
            next_high[0] = T_DOWN_E + LEAD
            act.wait_ge(s["choice_turned"], 1)
            nc.scalar.activation(choice_t, flat[:, 0:6 * P].rearrange("p (k n) -> p k n", k=3), ACT.Copy).then_inc(s["choice_t_set"], 1)
            act.wait_ge(s["choice_t_set"], 1)
            with act.Fori(0, N2 // 16) as i:
                for b in range(2):
                    act.wait_ge(s["hot1_set"], i * 2 + b + 1)
                    for q in range(8):
                        ins = nc.scalar.activation(hot1[:, b, q, :], hot1[:, b, q, :], ACT.Copy,
                                                   scale=choice_t[:, 2, bass.ds((i * 2 + b) * 8 + q, 1)])
                    ins.then_inc(s["hot1_scaled"], 1)

            def picked_highs(e, at):
                nc.scalar.activation(x_high[:, e % 4:e % 4 + 1, 0:N2] if isinstance(e, int) else e,
                                     acts[:, at, :], ACT.Copy).then_inc(s["picked_high_set"], 1)

            act.wait_ge(s["gates_used"], N2 // 4)
            act.wait_ge(s["zeros_set"], 1)
            for e in range(LEAD):
                picked_highs(e, slice(e, e + 1))
            for k in range(RING):
                high_to(T_DOWN_E + k + 1 + LEAD)
                act.wait_ge(s["tile_used"], T_DOWN_E + k)
                picked_highs(k + LEAD, slice(k + LEAD, k + LEAD + 1))
            with act.Fori(1, KEYS // RING - 1) as i:
                for k in range(RING):
                    loop_high(i, T_DOWN_E + k + LEAD)
                    picked_highs(x_high[:, (k + LEAD) % 4:(k + LEAD) % 4 + 1, 0:N2], bass.ds(i * RING + k + LEAD, 1))
            for e in range(KEYS - RING + LEAD, KEYS):
                act.wait_ge(s["tile_used"], T_DOWN_E + e - LEAD)
                next_high[0] = T_DOWN_E + e
                high_to(T_DOWN_E + e + 1)
                picked_highs(e, slice(e, e + 1))
            act.wait_ge(s["resid_set"], 3)
            norm(11, resid[:, :, 0:N2], DC, N2)

        @block.tensor
        def _(pe):
            def tile(t):
                pe.wait_ge(s["low_set"], split_of(t) + 1)
                return w_high[:, split_of(t) % HIGHS, :], ring_low[:, t % RING, :]

            def three(out, pairs):
                last = len(pairs) - 1
                for n, (wh, wl, xh, xl) in enumerate(pairs):
                    nc.tensor.matmul(out, wh, xh, start=(n == 0), stop=False)
                    nc.tensor.matmul(out, wh, xl, start=False, stop=False)
                    ins = nc.tensor.matmul(out, wl, xh, start=False, stop=(n == last))
                return ins

            def cut_cols(a, c):
                return a[:, c * P:(c + 1) * P]

            def sum_squares(k, chunks, n):
                pe.wait_ge(s["squared"], k)
                for c in range(chunks):
                    ins = nc.tensor.matmul(bank[7][:, 0:n], ones[:, :], squares[:, c, 0:n], start=(c == 0), stop=(c == chunks - 1))
                ins.then_inc(s["norm_summed"], 1)

            def bank_free(r):
                if r >= 4:
                    pe.wait_ge(s["proj_evacuated"], r - 3)
                return bank[r % 4]

            def linear(r, t, n):
                b = bank_free(r)
                high, low = tile(t)
                three(b[:, 0:n], [(cut_cols(high, c), cut_cols(low, c), x_high[:, c, 0:n], x_low[:, c, 0:n])
                                  for c in range(DC)]).then_inc(s["tile_used"], 1)

            def natural(r, t, tiles):
                b = bank_free(r)
                high, low = tile(t)
                for q, (q0, _) in enumerate(tiles):
                    at = [c * N1 + q0 for c in range(DC)]
                    ins = three(b[:, q * P:(q + 1) * P],
                                [(x_both[:, a:a + P], x_both[:, DC * N1 + a:DC * N1 + a + P], cut_cols(high, c), cut_cols(low, c))
                                 for c, a in enumerate(at)])
                ins.then_inc(s["tile_used"], 1)

            pe.wait_ge(s["ones_set"], 2)
            pe.wait_ge(s["consts_landed"], 16 * 8)
            hot = cst("bucket", BUCKETS)
            nc.tensor.matmul(bank[4][0:HEADS, 0:512], rel_sb[0:BUCKETS, :], hot[:, 0:512], start=True, stop=True)
            nc.tensor.matmul(bank[5][0:HEADS, 0:N_BIAS - 512], rel_sb[0:BUCKETS, :], hot[:, 512:N_BIAS],
                             start=True, stop=True).then_inc(s["bias_summed"], 1)
            sum_squares(1, DC, N1)
            pe.wait_ge(s["normed_set"], 2)
            for c in range(DC):
                ins = nc.tensor.matmul(bank[0][0:HEADS, 0:N1], w_f_sb[:, c, :], normed[:, c, :], start=(c == 0), stop=(c == DC - 1))
            ins.then_inc(s["forget_done"], 1)
            pe.wait_ge(s["x_low_set"], 2)
            for j in range(N_QK1):
                linear(R_QK1 + j, T_QK1 + j, N1)
            for j in range(N_V1):
                natural(R_V1 + j, T_V1 + j, TILE_COLS)
            pe.wait_ge(s["bias_tables_landed"], 16 * 6)
            for n, (src, _, rows, cols) in enumerate(flips):
                if n >= 4:
                    pe.wait_ge(s["bias_taken"], n - 3)
                nc.tensor.matmul(bank[4 + n % 4][0:rows, 0:cols], cst("flip")[0:rows, P - rows:P], src, start=True, stop=True).then_inc(s["bias_flipped"], 1)
            pe.wait_ge(s["bias_taken"], len(flips))
            pe.wait_ge(s["cum_set"], 3)
            for t, (c0, n) in enumerate(TILE_COLS):
                ins = nc.tensor.transpose(bank[4][0:n, t * HEADS:(t + 1) * HEADS], f_work[0:HEADS, 5, c0:c0 + n], ident[0:HEADS, 0:HEADS])
            ins.then_inc(s["cum_turned"], 1)
            sel = cst("select", HEADS).rearrange("p (h n) -> p h n", n=P)
            for h in range(HEADS):
                if h >= 2:
                    pe.wait_ge(s["fox_tables_set"], h - 1)
                nc.tensor.matmul(bank[5 + h % 2][:, 0:N1], sel[:, h, :], f_work[0:HEADS, 5, :], start=True, stop=True).then_inc(s["cum_spread"], 1)
            def scores(u):
                kind, g, _ = units[u]
                k0, nk, q0, nq = shape_of(u)
                if u:
                    pe.wait_ge(s["scores_read"], u)
                for h in range(4):
                    c, half = 2 * g + h // 2, h % 2
                    rows = slice(half * DH, half * DH + DH)
                    if kind == 0:
                        lhs, rhs = qk[rows, c, q0:q0 + nq], qk[rows, 4, k0:k0 + nk]
                    elif kind == 1:
                        lhs, rhs = qk[rows, 5 + c, q0:q0 + nq], qk[rows, 9 + c, k0:k0 + nk]
                    elif kind == 2:
                        lhs, rhs = rope_q[rows, c, q0:q0 + nq], rope_q[rows, 4, k0:k0 + nk]
                    else:
                        lhs, rhs = q_mla[0:QK, 4 * g + h, q0:q0 + nq], k_mla[0:QK, 4 * g + h, k0:k0 + nk]
                    ins = nc.tensor.matmul(bank[h][0:nq, 0:nk], lhs, rhs, start=True, stop=True)
                ins.then_inc(s["scores_done"], 1)

            def turn_probs(u):
                nq = shape_of(u)[3]
                pe.wait_ge(s["probs_set"], u + 1)
                if u > 0:
                    pe.wait_ge(s["probs_t_set"], u)
                for t, k0, kn in key_blocks(u):
                    for h in range(4):
                        ins = nc.tensor.transpose(bank[4 + t][0:kn, h * P:h * P + nq], score[u % 2][0:nq, h, k0:k0 + kn], ident[0:nq, 0:nq])
                ins.then_inc(s["probs_turned"], 1)

            def attend(u):
                kind, g, _ = units[u]
                nq = shape_of(u)[3]
                pe.wait_ge(s["probs_t_set"], u + 1)
                if u > 0:
                    pe.wait_ge(s["mixed_set"], u)
                blocks = key_blocks(u)
                for h in range(4):
                    c, half = 2 * g + h // 2, h % 2
                    vc = half * DH if kind in (0, 2) else P + (2 * c + half) * DH
                    for n, (t, _, kn) in enumerate(blocks):
                        ins = nc.tensor.matmul(bank[7][half * DH:(half + 1) * DH, (h // 2) * P:(h // 2) * P + nq],
                                               v_nat[0:kn, t, vc:vc + DH], probs_t[u % 2][0:kn, t, h * P:h * P + nq],
                                               start=(n == 0), stop=(n == len(blocks) - 1))
                ins.then_inc(s["attended"], 1)

            def attention(u0, u1):
                for u in range(u0, u1 + 1):
                    if u < u1:
                        scores(u)
                    if u > u0:
                        turn_probs(u - 1)
                        attend(u - 1)

            pe.wait_ge(s["fox_tables_set"], HEADS)
            pe.wait_ge(s["proj_evacuated"], R_OUT1)
            attention(0, len(units1))
            pe.wait_ge(s["x_low_set"], 4)
            for j in range(DC):
                linear(R_OUT1 + j, T_OUT1 + j, N1)
            sum_squares(2, DC, N1)
            sum_squares(3, DC, N1)
            pe.wait_ge(s["x_low_set"], 6)

            def gate_up(i, k):
                for side in range(2):
                    t = T_FFN + 2 * k + side
                    pe.wait_ge(s["low_set"], i * RING + t + 1)
                    if side == 0 and not (isinstance(i, int) and i == 0):
                        pe.wait_ge(s["ffn_act_set"], i * 4 + k - 3)
                    three(bank[2 * k + side][:, 0:N1],
                          [(cut_cols(w_high[:, t % HIGHS, :], c), cut_cols(ring_low[:, t % RING, :], c), x_high[:, c, :], x_low[:, c, :])
                           for c in range(DC)]).then_inc(s["tile_used"], 1)

            for k in range(4):
                gate_up(0, k)
            with pe.Fori(1, FC // 4) as i:
                for k in range(4):
                    gate_up(i, k)
            for k in range(FC % 4):
                gate_up(FC // 4, k)
            pe.wait_ge(s["ffn_low_set"], FC)
            for j in range(DC):
                b = bank_free(R_DOWN + j)
                for f in range(FC):
                    n = j * FC + f
                    high, low = (cut_cols(a, n % DC) for a in tile(T_DOWN + n // DC))
                    nc.tensor.matmul(b[:, 0:N1], high, ffn_high[:, f, :], start=(f == 0), stop=False)
                    nc.tensor.matmul(b[:, 0:N1], high, ffn_low[:, f, :], start=False, stop=False)
                    ins = nc.tensor.matmul(b[:, 0:N1], low, ffn_high[:, f, :], start=False, stop=(f == FC - 1))
                    if n % DC == DC - 1:
                        ins.then_inc(s["tile_used"], 1)
            sum_squares(4, DC, N1)

            sum_squares(5, DC, N2)
            pe.wait_ge(s["x_low_set"], 8)
            for j in range(N_QK2):
                linear(R_QK2 + j, T_QK2 + j, N2)
            natural(R_V2, T_V2, TILE_COLS[0:2])
            sum_squares(6, QR_C, N2)
            pe.wait_ge(s["proj_evacuated"], R_OUT2)
            for j in range(5):
                ins = nc.tensor.matmul(flat[:, j * N2:(j + 1) * N2], cst("rot64"), qk[:, j, 0:N2], start=True, stop=True)
            ins.then_inc(s["rot_done"], 1)
            nc.tensor.matmul(bank[4][:, 0:N2], cst("rot32"), qk[:, 8, 0:N2], start=True, stop=True).then_inc(s["rot_done"], 1)
            pe.wait_ge(s["rstd_set"], 6)
            sum_squares(7, 1, N2)
            w_q = small_sb[:, 0:QR_C * HEADS * QK].rearrange("p (c n) -> p c n", c=QR_C)
            w_kv = small_sb[:, QR_C * HEADS * QK:2560].rearrange("p (h n) -> p h n", h=HEADS)
            pe.wait_ge(s["rope_set"], 1)
            pe.wait_ge(s["normed_set"], 5)
            for h in range(HEADS):
                for c in range(QR_C):
                    ins = nc.tensor.matmul(flat[0:QK, h * N2:(h + 1) * N2], w_q[:, c, h * QK:(h + 1) * QK], normed[:, c, 0:N2],
                                           start=(c == 0), stop=(c == QR_C - 1))
            ins.then_inc(s["mla_up_done"], 1)
            pe.wait_ge(s["rope_set"], 2)
            pe.wait_ge(s["normed_set"], 6)
            for t in range(2):
                ins = nc.tensor.matmul(bank[4 + t][:, :], normed[:, 2, t * P:(t + 1) * P], w_kv[:, :, NOPE:NOPE + DH], start=True, stop=True)
            ins.then_inc(s["mla_up_done"], 1)
            pe.wait_ge(s["mla_up_set"], 1)
            for h in range(HEADS):
                ins = nc.tensor.matmul(flat[0:NOPE, h * N2:(h + 1) * N2], w_kv[:, h, 0:NOPE], normed[:, 2, 0:N2], start=True, stop=True)
            ins.then_inc(s["mla_up_done"], 1)
            pe.wait_ge(s["mla_up_set"], 3)
            rot = cst("rot32")[0:QK, 0:QK]
            for h in range(HEADS):
                ins = nc.tensor.matmul(flat[0:QK, h * N2:(h + 1) * N2], rot, q_mla[0:QK, h, :], start=True, stop=True)
            ins.then_inc(s["rot_done"], 1)
            pe.wait_ge(s["rope_set"], 3)
            pe.wait_ge(s["k_rope_set"], 1)
            attention(len(units1), len(units))
            sum_squares(8, 4, N2)
            pe.wait_ge(s["rstd_set"], 8)
            sum_squares(9, 4, N2)
            pe.wait_ge(s["x_low_set"], 10)
            for j in range(DC):
                linear(R_OUT2 + j, T_OUT2 + j, N2)
            sum_squares(10, DC, N2)
            pe.wait_ge(s["x_low_set"], 12)
            for j in range(N_QUERY):
                linear(R_QUERY + j, T_QUERY + j, N2)
            pe.wait_ge(s["proj_evacuated"], R_QUERY + N_QUERY)
            for k in range(N_SUB):
                t = T_SUB + k
                pe.wait_ge(landed[t % RING], 16 * (t // RING + 1))
            for tt in range(2):
                for a in range(16):
                    ins = nc.tensor.matmul(flat[:, tt * 2048 + a * P:tt * 2048 + (a + 1) * P], query[:, a, tt * P:(tt + 1) * P],
                                           cut_cols(ring[:, (T_SUB + a // 8) % RING, :], a % 8), start=True, stop=True)
                if tt == 0:
                    ins.then_inc(s["keys_scored"], 1)
                else:
                    ins.then_inc(s["tile_used"], N_SUB)
            pe.wait_ge(s["keys_evacuated"], 2)

            def up(i, k):
                t = T_UP + k
                pe.wait_ge(s["low_set"], i * RING + split_of(t) + 1)
                if k >= 4 or not isinstance(i, int):
                    pe.wait_ge(s["gelu_set"], i * RING + k - 3)
                high, low = w_high[:, split_of(t) % HIGHS, :], ring_low[:, t % RING, :]
                three(bank[4 + k % 4][:, 0:N2], [(cut_cols(high, c), cut_cols(low, c), x_high[:, c, 0:N2], x_low[:, c, 0:N2])
                                                 for c in range(DC)]).then_inc(s["tile_used"], 1)

            for k in range(RING):
                up(0, k)
            with pe.Fori(1, KEYS // RING) as i:
                for k in range(RING):
                    up(i, k)
            pe.wait_ge(s["gates_ready"], 1)
            for k in range(3):
                for tt in range(2):
                    ins = nc.tensor.transpose(flat[:, (2 * k + tt) * P:(2 * k + tt + 1) * P], choice[:, k, tt, :], ident[:, :])
            ins.then_inc(s["choice_turned"], 1)
            pe.wait_ge(s["choice_t_set"], 1)
            def gate_matrices(i, b):
                pe.wait_ge(s["hot2_set"], i * 2 + b + 1)
                pe.wait_ge(s["hot1_scaled"], i * 2 + b + 1)
                if not isinstance(i, int):
                    pe.wait_ge(s["gates_used"], (i - 1) * 4 + b * 2 + 2)
                for q in range(8):
                    ins = nc.tensor.matmul(flat[:, b * 1024 + q * P:b * 1024 + (q + 1) * P], hot2[:, b, q, :], hot1[:, b, q, :], start=True, stop=True)
                ins.then_inc(s["gates_done"], 1)

            for b in range(2):
                gate_matrices(0, b)
            with pe.Fori(1, N2 // 16) as i:
                for b in range(2):
                    gate_matrices(i, b)
            pe.wait_ge(s["gates_used"], N2 // 4)
            pe.wait_ge(s["zeros_set"], 1)
            for b in range(4):
                nc.tensor.matmul(bank[b][:, :], zeros[:, 0:P], zeros[:, :], start=True, stop=True)

            def down(i, k):
                t = T_DOWN_E + k
                pe.wait_ge(s["low_set"], i * RING + split_of(t) + 1)
                pe.wait_ge(s["picked_low_set"], i * RING + k + 1)
                high, low = w_high[:, split_of(t) % HIGHS, :], ring_low[:, t % RING, :]
                xh, xl = x_high[:, k % 4, 0:N2], x_low[:, k % 4, 0:N2]
                for c in range(DC):
                    for w, x in ((high, xh), (high, xl), (low, xh)):
                        ins = nc.tensor.matmul(flat[:, c * N2:(c + 1) * N2], cut_cols(w, c), x, start=False, stop=False, skip_group_check=True)
                ins.then_inc(s["tile_used"], 1)

            with pe.Fori(0, KEYS // RING) as i:
                for k in range(RING):
                    down(i, k)
            sum_squares(11, DC, N2)

        @block.vector
        def _(dve):
            steps = [0]

            def step(ins):
                steps[0] += 1
                ins.then_inc(s["vector_step"], 1)

            def settle():
                dve.wait_ge(s["vector_step"], steps[0])

            def normalise(dst, src, gain, chunks, n, done=None, per=DC):
                for c in range(chunks):
                    ins = nc.vector.scalar_tensor_tensor(out=dst[:, c, 0:n], in0=src[:, c, 0:n], scalar=vcol(gain[0], gain[1] + c),
                                                         in1=rstd[:, 0:n], op0=ALU.mult, op1=ALU.mult)
                    if done is None:
                        step(ins)
                    elif c % per == per - 1:
                        ins.then_inc(s[done], 1)

            next_low = [0]

            def low(t):
                n = split_of(t)
                dve.wait_ge(s["high_set"], n + 1)
                nc.vector.tensor_tensor(ring_low[:, t % RING, :], ring[:, t % RING, :], w_high[:, n % HIGHS, :].bitcast(F32),
                                        ALU.subtract).then_inc(s["low_set"], 1)

            def low_to(t):
                while next_low[0] < t:
                    if not T_SUB <= next_low[0] < T_UP:
                        low(next_low[0])
                    next_low[0] += 1

            def loop_low(i, t):
                n = split_of(t)
                dve.wait_ge(s["high_set"], i * RING + n + 1)
                nc.vector.tensor_tensor(ring_low[:, t % RING, :], ring[:, t % RING, :], w_high[:, n % HIGHS, :].bitcast(F32),
                                        ALU.subtract).then_inc(s["low_set"], 1)

            def x_lows(k, src, n):
                for half in range(2):
                    dve.wait_ge(s["x_high_set"], 2 * k + half + 1)
                    c = slice(4 * half, 4 * half + 4)
                    nc.vector.tensor_tensor(x_low[:, c, 0:n], src[:, c, 0:n], x_high[:, c, 0:n].bitcast(F32), ALU.subtract).then_inc(s["x_low_set"], 1)

            next_ada = [0]

            def modulation(n):
                for j in range(next_ada[0], min(next_ada[0] + n, N_ADA)):
                    if j == 0:
                        dve.wait_ge(s["cond_set"], 1)
                    dve.wait_ge(ada_landed[j % 2], 16 * (j // 2 + 1))
                    w = ada_slots[:, j % 2, :]
                    nc.vector.tensor_tensor_reduce(w, w, cond[:, :], 1.0, 0.0, ALU.mult, ALU.add, modv[:, j:j + 1]).then_inc(s["ada_used"], 1)
                next_ada[0] = min(next_ada[0] + n, N_ADA)

            dve.wait_ge(s["bias_summed"], 1)
            m = cst("bmask", HEADS)
            nc.vector.tensor_tensor(bias_vec[0:HEADS, 0:512], bank[4][0:HEADS, :], m[:, 0:512], ALU.add).then_inc(s["bias_vec_set"], 1)
            nc.vector.tensor_tensor(bias_vec[0:HEADS, 512:N_BIAS], bank[5][0:HEADS, 0:N_BIAS - 512], m[:, 512:N_BIAS],
                                    ALU.add).then_inc(s["bias_vec_set"], 1)
            dve.wait_ge(s["rstd_set"], 1)
            low_to(LEAD)
            normalise(normed, resid, ("pre_mix", 0), DC, N1, "normed_set", 4)
            x_lows(0, normed, N1)
            dve.wait_ge(s["proj_evacuated"], 1)
            nc.vector.tensor_scalar(f_work[0:HEADS, 0, :], f_work[0:HEADS, 0, :], bf_sb[0:HEADS, 0:1], None, ALU.add).then_inc(s["forget_set"], 1)
            step(nc.vector.memset(f_work[0:HEADS, 4, :], 1.0))
            dve.wait_ge(s["forget_exp"], 1)
            step(nc.vector.scalar_tensor_tensor(out=f_work[0:HEADS, 3, :], in0=f_work[0:HEADS, 0, :], scalar=0.0,
                                                in1=f_work[0:HEADS, 1, :], op0=ALU.min, op1=ALU.subtract))
            settle()
            before = None
            for t in (2, 1, 0):
                c0, n = TILE_COLS[t]
                if before is not None:
                    dve.wait_ge(s["cum_set"], 2 - t)
                nc.vector.tensor_tensor_scan(f_work[0:HEADS, 5, c0:c0 + n], f_work[0:HEADS, 4, c0:c0 + n], f_work[0:HEADS, 3, c0:c0 + n],
                                             0.0 if before is None else before, ALU.mult, ALU.add).then_inc(s["cum_set"], 1)
                before = f_work[0:HEADS, 5, c0 + n - 1:c0 + n]
            while next_low[0] < T_OUT1:
                low_to(next_low[0] + 1)
                modulation(1)
            dve.wait_ge(s["cum_turned"], 1)
            step(nc.vector.tensor_copy(cum_q[:, 0:2, :], bank[4][:, 0:2 * HEADS].rearrange("p (t h) -> p t h", h=HEADS)))
            step(nc.vector.tensor_copy(cum_q[0:META, 2, :], bank[4][0:META, 2 * HEADS:3 * HEADS]))
            settle()
            for h in range(HEADS):
                dve.wait_ge(s["cum_spread"], h + 1)
                b = bank[5 + h % 2]
                nc.vector.scalar_tensor_tensor(out=fox1[:, h, :], in0=b[:, 0:N1], scalar=cum_q[:, 0, h:h + 1], in1=cst("causal1"),
                                               op0=ALU.add, op1=ALU.add)
                nc.vector.scalar_tensor_tensor(out=fox0[:, h, :], in0=b[:, P:N1], scalar=cum_q[:, 1, h:h + 1], in1=cst("causal0"),
                                               op0=ALU.add, op1=ALU.add)
                nc.vector.scalar_tensor_tensor(out=foxm[0:META, h, :], in0=b[0:META, 2 * P:N1], scalar=cum_q[0:META, 2, h:h + 1],
                                               in1=cst("causalm", META), op0=ALU.add, op1=ALU.add).then_inc(s["fox_tables_set"], 1)
            def add_bias(u):
                kind, g, qt = units[u]
                _, nk, _, nq = shape_of(u)
                sc = score[u % 2]
                src = psum[0:nq, 0:4, 0:nk]
                dve.wait_ge(s["scores_done"], u + 1)
                if u >= 2:
                    dve.wait_ge(s["probs_turned"], u - 1)
                if has_sink(u):
                    at = VEC["sinks1" if kind == 0 else "sinks2"][0] + 4 * g
                    step(nc.vector.tensor_copy(sc[0:nq, :, nk:nk + 1], vec[0:nq, at:at + 4].unsqueeze(2)))
                    settle()
                if kind == 3:
                    ins = nc.vector.tensor_copy(sc[0:nq, :, 0:nk], src)
                else:
                    if kind == 2:
                        table = cst(f"band{1 - qt}").unsqueeze(1).broadcast_to([P, 4, N2])
                    else:
                        table = ((bias1, bias0, biasm), (fox1, fox0, foxm))[kind][qt][0:nq, 4 * g:4 * g + 4, :]
                    ins = nc.vector.tensor_tensor(sc[0:nq, :, 0:nk], src, table, ALU.add)
                ins.then_inc(s["scores_read"], 1)
                dve.wait_ge(s["scores_read"], u + 1)
                n = nk + has_sink(u)
                st = stats[u % 2]
                step(nc.vector.tensor_reduce(st[0:nq, 0:4], sc[0:nq, :, 0:n], AX_X, ALU.max))
                settle()
                nc.vector.tensor_scalar(st[0:nq, 4:8], st[0:nq, 0:4], -1.0, None, ALU.mult).then_inc(s["max_set"], 1)

            def divide(u):
                _, nk, _, nq = shape_of(u)
                st = stats[u % 2]
                dve.wait_ge(s["exp_done"], u + 1)
                step(nc.vector.reciprocal(st[0:nq, 12:16], st[0:nq, 8:12]))
                settle()
                nc.vector.tensor_tensor(score[u % 2][0:nq, :, 0:nk], score[u % 2][0:nq, :, 0:nk],
                                        st[0:nq, 12:16].unsqueeze(2).broadcast_to([nq, 4, nk]), ALU.mult).then_inc(s["probs_set"], 1)

            def take_mixed(u):
                kind, g, _ = units[u]
                _, _, q0, nq = shape_of(u)
                dve.wait_ge(s["attended"], u + 1)
                c = 4 * (kind % 2) + 2 * g
                nc.vector.tensor_copy(mixed[:, c:c + 2, q0:q0 + nq],
                                      bank[7][:, 0:2 * P].rearrange("p (c q) -> p c q", q=P)[:, :, 0:nq]).then_inc(s["mixed_set"], 1)

            def attention(u0, u1):
                for u in range(u0, u1 + 2):
                    if u < u1:
                        add_bias(u)
                        modulation(1)
                    if u0 < u < u1 + 1:
                        divide(u - 1)
                        modulation(2)
                    if u > u0 + 1:
                        take_mixed(u - 2)

            def add_normed(gain):
                normalise(lin_out, lin_out, (gain, 0), DC, N1)
                settle()
                nc.vector.tensor_tensor(resid[:, :, :], resid[:, :, :], lin_out, ALU.add).then_inc(s["resid_set"], 1)

            dve.wait_ge(s["bias_taken"], len(flips))
            low_to(T_OUT1 + LEAD)
            attention(0, len(units1))
            modulation(N_ADA)
            x_lows(1, mixed, N1)
            low_to(T_FFN + LEAD)
            b0 = VEC["b_ada"][0]
            dve.wait_ge(s["ada_used"], N_ADA)
            step(nc.vector.tensor_tensor(modv[:, :], modv[:, :], vec[:, b0:b0 + 6 * DC], ALU.add))
            settle()
            for k in (1, 4):
                ins = nc.vector.tensor_scalar(modv[:, k * DC:(k + 1) * DC], modv[:, k * DC:(k + 1) * DC], 1.0, None, ALU.add)
            ins.then_inc(s["mod_set"], 1)
            dve.wait_ge(s["rstd_set"], 2)
            add_normed("post_mix")
            dve.wait_ge(s["rstd_set"], 3)
            normalise(normed, resid, ("pre_ffn", 0), DC, N1, "normed_set", 4)
            x_lows(2, normed, N1)

            def ffn_lows(j, at, k):
                dve.wait_ge(s["ffn_high_set"], j + 1)
                nc.vector.tensor_tensor(ffn_low[:, at, :], silu_sb[:, k:k + 1, :], ffn_high[:, at, :].bitcast(F32), ALU.subtract).then_inc(s["ffn_low_set"], 1)

            def gate_pair(i, k):
                j = i * 4 + k
                unrolled = isinstance(i, int)
                for d in (0, 1):
                    loop_low(i, T_FFN + 2 * k + LEAD + d)
                dve.wait_ge(s["silu_set"], j + 1)
                nc.vector.tensor_tensor(silu_sb[:, k, :], silu_sb[:, k, :], bank[2 * k + 1][:, 0:N1], ALU.mult).then_inc(s["ffn_act_set"], 1)
                if not (unrolled and j == 0):
                    ffn_lows(j - 1, slice(j - 1, j) if unrolled else bass.ds(j - 1, 1), (k - 1) % 4)

            for k in range(4):
                gate_pair(0, k)
            with dve.Fori(1, FC // 4) as i:
                for k in range(4):
                    gate_pair(i, k)
            for k in range(FC % 4):
                gate_pair(FC // 4, k)
            ffn_lows(FC - 1, slice(FC - 1, FC), (FC - 1) % 4)
            next_low[0] = T_DOWN + LEAD
            low_to(T_QK2 + LEAD)
            dve.wait_ge(s["rstd_set"], 4)
            add_normed("post_ffn")

            def modulate(n, scale_at):
                for c in range(DC):
                    nc.vector.scalar_tensor_tensor(out=normed[:, c, 0:N2], in0=resid[:, c, 0:N2],
                                                   scalar=modv[:, scale_at + c:scale_at + c + 1],
                                                   in1=rstd[:, 0:N2], op0=ALU.mult, op1=ALU.mult).then_inc(s["modulated"], 1)

            dve.wait_ge(s["rstd_set"], 5)
            modulate(0, DC)
            x_lows(3, normed, N2)
            low_to(T_OUT2 + LEAD)
            cos, sin = (cst(n).unsqueeze(1).broadcast_to([P, 5, N2]) for n in ("cos64", "sin64"))
            dve.wait_ge(s["proj_evacuated"], R_QK2 + 5)
            step(nc.vector.tensor_tensor(rope_q[:, 0:5, :], qk[:, 0:5, 0:N2], cos, ALU.mult))
            dve.wait_ge(s["rot_done"], 1)
            step(nc.vector.tensor_tensor(rope_tmp2[:, 0:5, :], flat[:, 0:5 * N2].rearrange("p (a n) -> p a n", n=N2), sin, ALU.mult))
            settle()
            nc.vector.tensor_tensor(rope_q[:, 0:5, :], rope_q[:, 0:5, :], rope_tmp2[:, 0:5, :], ALU.add).then_inc(s["rope_set"], 1)
            dve.wait_ge(s["rope_set"], 1)
            rr = slice(NOPE, QK)
            dve.wait_ge(s["rot_done"], 2)
            step(nc.vector.tensor_tensor(rope_tmp2[rr, 0, :], bank[4][rr, 0:N2], cst("sin32")[rr, :], ALU.mult))
            step(nc.vector.tensor_tensor(rope_tmp2[rr, 1, :], qk[rr, 8, 0:N2], cst("cos32")[rr, :], ALU.mult))
            settle()
            nc.vector.tensor_tensor(rope_tmp2[rr, 5, :], rope_tmp2[rr, 0, :], rope_tmp2[rr, 1, :], ALU.add).then_inc(s["rope_set"], 1)
            dve.wait_ge(s["rope_set"], 2)
            dve.wait_ge(s["rstd_set"], 6)
            normalise(normed, qk[:, 5:7, :], ("q_norm", 0), QR_C, N2, "normed_set", QR_C)
            dve.wait_ge(s["rstd_set"], 7)
            nc.vector.scalar_tensor_tensor(out=normed[:, 2, 0:N2], in0=qk[:, 7, 0:N2], scalar=vcol("kv_norm"), in1=rstd[:, 0:N2],
                                           op0=ALU.mult, op1=ALU.mult).then_inc(s["normed_set"], 1)
            dve.wait_ge(s["normed_set"], 6)
            nc.vector.tensor_copy(k_mla[rr, :, :], rope_tmp2[rr, 5:6, :].broadcast_to([ROPE, HEADS, N2])).then_inc(s["k_rope_set"], 1)
            cos, sin = (cst(n)[rr, :].unsqueeze(1).broadcast_to([ROPE, HEADS, N2]) for n in ("cos32", "sin32"))
            dve.wait_ge(s["k_rope_set"], 1)
            dve.wait_ge(s["rot_done"], 3)
            step(nc.vector.tensor_tensor(rope_tmp2[rr, :, :], flat[rr, 0:HEADS * N2].rearrange("p (a n) -> p a n", n=N2), sin, ALU.mult))
            step(nc.vector.tensor_tensor(q_mla[rr, :, :], q_mla[rr, :, :], cos, ALU.mult))
            settle()
            nc.vector.tensor_tensor(q_mla[rr, :, :], q_mla[rr, :, :], rope_tmp2[rr, :, :], ALU.add).then_inc(s["rope_set"], 1)
            attention(len(units1), len(units))
            dve.wait_ge(s["rstd_set"], 8)
            normalise(normed, mixed, ("out_norm", 0), 4, N2, "normed_set", 4)
            dve.wait_ge(s["rstd_set"], 9)
            normalise(normed[:, 4:8, :], mixed[:, 4:8, :], ("out_norm", 4), 4, N2, "normed_set", 4)
            x_lows(4, normed, N2)
            for j in range(DC):
                r = R_OUT2 + j
                low_to(T_OUT2 + j + 1 + LEAD)
                dve.wait_ge(s["tile_used"], T_OUT2 + j + 1)
                ins = nc.vector.scalar_tensor_tensor(out=resid[:, j, 0:N2], in0=bank[r % 4][:, 0:N2], scalar=modv[:, 2 * DC + j:2 * DC + j + 1],
                                                     in1=resid[:, j, 0:N2], op0=ALU.mult, op1=ALU.add)
                ins.then_inc(s["proj_evacuated"], 1)
            dve.wait_ge(s["rstd_set"], 10)
            modulate(1, 4 * DC)
            x_lows(5, normed, N2)
            low_to(T_UP + LEAD)

            since = [0]

            def relief():
                since[0] += 1
                if since[0] % 5 == 0 and next_low[0] < T_UP + KEYS // 2:
                    low_to(next_low[0] + 1)

            def top16(src, other, values, where, n):
                for a in range(n):
                    step(nc.vector.max(values[:, a, 0:8], src[:, a, :]))
                    relief()
                settle()
                for a in range(n):
                    step(nc.vector.max_index(where[:, a, 0:8].bitcast(U32), values[:, a, 0:8], src[:, a, :]))
                    relief()
                for a in range(n):
                    step(nc.vector.match_replace(other[:, a, :], values[:, a, 0:8], src[:, a, :], LOWEST))
                    relief()
                settle()
                for a in range(n):
                    step(nc.vector.max(values[:, a, 8:16], other[:, a, :]))
                    relief()
                settle()
                for a in range(n):
                    step(nc.vector.max_index(where[:, a, 8:16].bitcast(U32), values[:, a, 8:16], other[:, a, :]))
                    relief()
                settle()

            grid = [P, HEADS, TOPK, TOPK]
            iota16 = iota[:, 0:TOPK].unsqueeze(1).unsqueeze(1).broadcast_to(grid)
            dve.wait_ge(s["keys_evacuated"], 2)
            for tt in range(2):
                top16(keys_s[:, tt], spare, top_v, top_i, 16)
                step(nc.vector.tensor_copy(top_if[:, :, :], top_i[:, :, :].bitcast(U32)))
                tv = top_v[:, :, :].rearrange("p (h a) k -> p h a k", a=2)
                step(nc.vector.tensor_tensor(cand[:, :, :].rearrange("p h (a b) -> p h a b", b=TOPK),
                                             tv[:, :, 0, :].unsqueeze(3).broadcast_to(grid),
                                             tv[:, :, 1, :].unsqueeze(2).broadcast_to(grid), ALU.add))
                settle()
                top16(cand, cand2, best_v, best_i, HEADS)

                def pairs(k):
                    return choice[:, k, tt, :].rearrange("p (h k) -> p h k", k=TOPK)

                step(nc.vector.tensor_tensor(pairs(2), best_v[:, :, :], best_v[:, :, 0:1].broadcast_to([P, HEADS, TOPK]), ALU.subtract))
                tif = top_if[:, :, :].rearrange("p (h a) k -> p h a k", a=2)
                h4 = cand2[:, :, :].rearrange("p h (a b) -> p h a b", b=TOPK)
                for a, (op, by) in enumerate(((ALU.logical_shift_right, 4), (ALU.bitwise_and, 15))):
                    step(nc.vector.tensor_scalar(best_a[:, :, :].bitcast(U32), best_i[:, :, :].bitcast(U32), by, None, op))
                    settle()
                    step(nc.vector.tensor_copy(best_f[:, :, :], best_a[:, :, :].bitcast(U32)))
                    settle()
                    step(nc.vector.tensor_tensor(h4, best_f[:, :, :].unsqueeze(3).broadcast_to(grid), iota16, ALU.is_equal))
                    settle()
                    low_to(next_low[0] + 1)
                    step(nc.vector.tensor_tensor(h4, h4, tif[:, :, a, :].unsqueeze(2).broadcast_to(grid), ALU.mult))
                    settle()
                    low_to(next_low[0] + 1)
                    step(nc.vector.tensor_reduce(pairs(a), h4, AX_X, ALU.add))
                    settle()
                    low_to(next_low[0] + 1)
            nc.vector.tensor_copy(best_f[:, 0, 0:1], choice[:, 2, 0, 0:1]).then_inc(s["topk_set"], 1)
            while next_low[0] % RING:
                low_to(next_low[0] + 1)
            with dve.Fori((next_low[0] - T_UP) // RING, KEYS // RING) as i:
                for k in range(RING):
                    loop_low(i, T_UP + k)
            next_low[0] = T_DOWN_E
            dve.wait_ge(s["gate_exp_set"], 1)
            exps = choice[:, 2].rearrange("p a (h k) -> p (a h) k", k=TOPK)
            step(nc.vector.tensor_reduce(gate_sum[:, :], exps, AX_X, ALU.add))
            settle()
            step(nc.vector.reciprocal(gate_sum[:, :], gate_sum[:, :]))
            settle()
            nc.vector.tensor_tensor(exps, exps, gate_sum[:, :].unsqueeze(2).broadcast_to([P, 2 * HEADS, TOPK]), ALU.mult).then_inc(s["gates_ready"], 1)
            low_to(T_DOWN_E + LEAD)

            dve.wait_ge(s["choice_t_set"], 1)
            dve.wait_ge(s["gelu_set"], KEYS)

            def hot_rows(i, b):
                cols = choice_t[:, 0, bass.ds((i * 2 + b) * 8, 8)].unsqueeze(2).broadcast_to([P, 8, P])
                nc.vector.tensor_tensor(hot1[:, b], iota[:, :].unsqueeze(1).broadcast_to([P, 8, P]), cols, ALU.is_equal).then_inc(s["hot1_set"], 1)
                dve.wait_ge(s["second_apart"], i * 2 + b + 1)
                nc.vector.tensor_scalar(hot2[:, b], hot2[:, b], 0.0, None, ALU.is_equal).then_inc(s["hot2_set"], 1)

            def apply_gates(i, b):
                dve.wait_ge(s["gates_done"], i * 2 + b + 1)
                for half in range(2):
                    a = acts[:, :, bass.ds((i * 2 + b) * 8 + half * 4, 4)]
                    nc.vector.tensor_tensor(a, a, bank[2 * b + half].rearrange("p (t n) -> p n t", n=P), ALU.mult).then_inc(s["gates_used"], 1)

            for b in range(2):
                hot_rows(0, b)
            with dve.Fori(1, N2 // 16) as i:
                for b in range(2):
                    apply_gates(i - 1, b)
                    hot_rows(i, b)
            for b in range(2):
                apply_gates(N2 // 16 - 1, b)

            def picked_lows(e, at, k):
                dve.wait_ge(s["picked_high_set"], e + 1)
                nc.vector.tensor_tensor(x_low[:, k:k + 1, 0:N2], acts[:, at, :], x_high[:, k:k + 1, 0:N2].bitcast(F32),
                                        ALU.subtract).then_inc(s["picked_low_set"], 1)

            for e in range(LEAD):
                picked_lows(e, slice(e, e + 1), e % 4)
            for k in range(RING):
                low_to(T_DOWN_E + k + LEAD + 1)
                picked_lows(k + LEAD, slice(k + LEAD, k + LEAD + 1), (k + LEAD) % 4)
            with dve.Fori(1, KEYS // RING - 1) as i:
                for k in range(RING):
                    loop_low(i, T_DOWN_E + k + LEAD)
                    e = i * RING + k + LEAD
                    picked_lows(e, bass.ds(e, 1), (k + LEAD) % 4)
            for e in range(KEYS - RING + LEAD, KEYS):
                next_low[0] = T_DOWN_E + e
                low_to(T_DOWN_E + e + 1)
                picked_lows(e, slice(e, e + 1), e % 4)
            dve.wait_ge(s["tile_used"], T_END)
            for c in range(DC):
                ins = nc.vector.scalar_tensor_tensor(out=resid[:, c, 0:N2], in0=flat[:, c * N2:(c + 1) * N2],
                                                     scalar=modv[:, 5 * DC + c:5 * DC + c + 1], in1=resid[:, c, 0:N2],
                                                     op0=ALU.mult, op1=ALU.add)
            ins.then_inc(s["resid_set"], 1)
            dve.wait_ge(s["rstd_set"], 11)
            normalise(lin_out, resid, ("final", 0), DC, N2, "final_set")


def tiles_of(w):
    k, m = w.shape
    return w.reshape(k // P, P, m // P, P).transpose(2, 1, 0, 3).reshape(m // P, P, k)


def column(v):
    return v.reshape(-1, P).T


def kernel(x, meta_tokens, rel_bias, ln_pre_mix, ln_post_mix, ln_pre_ffn, ln_post_ffn, w_in, b_forget,
           sinks, w_out, w_gate_up, w_down, c_2, w_ada_2, b_ada_2, w_in_2, swa_sink_2, mla_q_norm_2,
           w_mla_q_up_2, mla_kv_norm_2, w_mla_kv_up_2, out_norm_swa_2, out_norm_mla_2, w_out_2,
           w_peer_query_2, peer_sub_keys_2, peer_expert_u_2, peer_expert_v_2, final_norm_2):
    import concourse.bacc as bacc
    from concourse.bass_utils import run_bass_kernel_spmd

    cat = np.concatenate
    swa = np.array([h * DH + i for h in SLOT_HEAD for i in range(DH)])

    tokens = cat([x[0, P:], x[0, :P], meta_tokens], 0)
    x_t = np.ascontiguousarray(tokens.T.reshape(DC, P, N1).transpose(1, 0, 2))

    w1 = w_in[0]
    q_a, k_a, v_a, q_b, k_b, v_b, f_b = np.split(w1, [512, 640, 768, 1280, 1792, 2304], axis=1)
    w2 = w_in_2[0]
    q_2, k_2, v_2, q_lat, kv_lat, k_rope = np.split(w2, [512, 640, 768, 1024, 1152], axis=1)
    gate_up = w_gate_up[0].reshape(D, 2, FC, P).transpose(0, 2, 1, 3).reshape(D, 2 * FF)
    down = w_down[0].reshape(FC, P, DC, P).transpose(2, 0, 1, 3).reshape(FC, DC, P, P).transpose(0, 2, 1, 3).reshape(FC, P, D)
    out1 = cat([w_out[0][:512][swa], w_out[0][512:]], 0)
    out2 = cat([w_out_2[0][:512][swa], w_out_2[0][512:]], 0)
    sub = peer_sub_keys_2[0].reshape(2, 8, KEYS, P).transpose(0, 3, 1, 2).reshape(2, P, D)
    weights = cat([
        tiles_of(cat([q_a[:, swa], k_a, q_b, k_b, v_a, v_b], 1)),
        tiles_of(out1), tiles_of(gate_up), down,
        tiles_of(cat([q_2[:, swa], k_2, q_lat, kv_lat, k_rope, k_rope, k_rope, k_rope, v_2], 1)),
        tiles_of(out2), tiles_of(w_peer_query_2[0]), sub,
    ], 0)
    up_experts = peer_expert_u_2[0].reshape(KEYS, KEYS, DC, P).transpose(0, 3, 2, 1).reshape(KEYS, P, D)
    down_experts = peer_expert_v_2[0].reshape(KEYS, KEYS, D)
    small = cat([w_mla_q_up_2[0].reshape(QR_C, P, HEADS * QK).transpose(1, 0, 2).reshape(P, -1), w_mla_kv_up_2[0]], 1)
    slots = np.array(SLOT_HEAD)
    vectors = cat([
        column(ln_pre_mix[0]), column(ln_post_mix[0]), column(ln_pre_ffn[0]), column(ln_post_ffn[0]), column(b_ada_2[0]),
        column(mla_q_norm_2[0]), column(mla_kv_norm_2[0]), column(out_norm_swa_2[0][swa]), column(out_norm_mla_2[0]),
        column(final_norm_2),
        np.broadcast_to(sinks[0][slots], (P, HEADS)), np.broadcast_to(swa_sink_2[0][slots], (P, HEADS)),
    ], 1)
    arrays = {
        "x_t": x_t, "weights": weights, "w_ada": w_ada_2[0].T.reshape(N_ADA, P, D), "cond_row": c_2[0], "up_experts": up_experts, "down_experts": down_experts, "small": small,
        "vectors": vectors, "w_f": f_b.reshape(DC, P, HEADS).transpose(1, 0, 2), "b_f": b_forget.reshape(HEADS, 1),
        "rel": rel_bias[:, slots], "const": shape_constants(),
    }
    arrays = {n: np.ascontiguousarray(a) for n, a in arrays.items()}
    nc = bacc.Bacc("TRN2", target_bir_lowering=False, num_devices=1)
    aps = {n: nc.dram_tensor(n, a.shape, F32, kind="ExternalInput").ap() for n, a in arrays.items()}
    scratch = nc.dram_tensor("bias_scratch", [HEADS, N_BIAS], F32, kind="Internal").ap()
    out = nc.dram_tensor("out_t", [P, DC, N2], F32, kind="ExternalOutput").ap()
    build(nc, *[aps[n] for n in ("x_t", "weights", "w_ada", "cond_row", "up_experts", "down_experts", "small", "vectors", "w_f", "b_f", "rel", "const")],
          scratch, out)
    got = run_bass_kernel_spmd(nc, [arrays], core_ids=[0]).results[0]["out_t"]
    got = got.transpose(2, 1, 0).reshape(N2, D)
    return np.ascontiguousarray(cat([got[P:], got[:P]], 0)[None])
```

```python
from contextlib import ExitStack

import numpy as np

import concourse.bass as bass
from concourse import mybir

F32 = mybir.dt.float32
F32R = mybir.dt.float32r
BF16 = mybir.dt.bfloat16
U32 = mybir.dt.uint32
ALU = mybir.AluOpType
ACT = mybir.ActivationFunctionType
AX_X = mybir.AxisListType.X

P = 128
D = 1024
DC = D // P
SEQ = 256
META = 16
N1 = SEQ + META
N2 = SEQ
HEADS = 8
DH = 64
FF = 2816
FC = FF // P
EPS = 1e-6
NEG = -1e30
LOWEST = -3.0e38
WINDOW = 128
BUCKETS = 32
MAX_DISTANCE = 128

NOPE = 64
ROPE = 32
QK = NOPE + ROPE
QR_C = 2
KEYS = 128
TOPK = 16
PAIRS = HEADS * TOPK

TILE_COLS = [(0, P), (P, P), (2 * P, META)]

RING = 8
HIGHS = 4
LEAD = 3
ADA_FIRST = 24
N_QK1, N_V1, N_OUT, N_QK2, N_V2, N_QUERY, N_SUB = 13, 5, DC, 9, 1, 16, 2
N_FFN, N_DOWN, N_ADA = 2 * FC, FC, 6 * DC
T_QK1 = 0
T_V1 = T_QK1 + N_QK1
T_OUT1 = T_V1 + N_V1
T_FFN = T_OUT1 + N_OUT
T_DOWN = T_FFN + N_FFN
T_QK2 = T_DOWN + N_DOWN
T_V2 = T_QK2 + N_QK2
T_OUT2 = T_V2 + N_V2
T_QUERY = T_OUT2 + N_OUT
T_SUB = T_QUERY + N_QUERY
T_UP = T_SUB + N_SUB
T_DOWN_E = T_UP + KEYS
T_END = T_DOWN_E + KEYS
assert T_UP % RING == 0


WHOLE = [*range(T_V1, T_V1 + N_V1), *range(T_V2, T_V2 + N_V2), *range(T_SUB, T_SUB + N_SUB)]


def split_of(t):
    assert t not in WHOLE
    return t - sum(w < t for w in WHOLE)


def tile_of(n):
    return next(t for t in range(n, n + len(WHOLE) + 1) if t not in WHOLE and split_of(t) == n)


def by_pool(t):
    if t < T_UP:
        return False
    return t % 4 != 3 if t < T_UP + KEYS // 2 + LEAD else t % 4 == 3


def lows_until(t):
    return sum(by_pool(u) == by_pool(t) for u in range(t + 1) if u not in WHOLE)


GROUP = 4
GROUPS = SEQ // GROUP
HALF = KEYS // 2


VEC = {}
_at = 0
for _name, _n in (("pre_mix", DC), ("post_mix", DC), ("pre_ffn", DC), ("post_ffn", DC), ("b_ada", 6 * DC),
                  ("q_norm", QR_C), ("kv_norm", 1), ("out_norm", DC), ("final", DC),
                  ("sinks1", HEADS), ("sinks2", HEADS)):
    VEC[_name] = (_at, _n)
    _at += _n
N_VEC = _at

SLOT_HEAD = [c + 4 * half for c in range(4) for half in range(2)]

BIAS_OWN = (0, 255, 0, -127)
BIAS_PREV = (255, 255, P, -127)
BIAS_META1 = (510, 143, META + P, -127)
BIAS_META0 = (653, 143, META, -127)
BIAS_MM = (796, 31, 0, -15)
N_BIAS = 827

CONST = {}
_at = 0
for _name, _n in (("ident", P), ("iota", P), ("flip", P), ("causal1", N1), ("causal0", N1 - P), ("causalm", META),
                  ("rot64", P), ("rot32", P), ("cos64", N2), ("sin64", N2), ("cos32", N2), ("sin32", N2), ("band1", N2), ("band0", N2), ("select", HEADS * P), ("bucket", N_BIAS), ("bmask", N_BIAS)):
    CONST[_name] = (_at, _n)
    _at += _n
N_CONST = _at
SECOND_BLOCK = CONST["rot64"][0]
FEW_ROWS = CONST["select"][0]


def bucket_of(d):
    n = np.maximum(d, 0)
    exact = BUCKETS // 2
    nf = np.maximum(n, 1).astype(np.float32)
    large = exact + (np.log(nf / np.float32(exact)) / np.float32(np.log(MAX_DISTANCE / exact))
                     * np.float32(BUCKETS - exact)).astype(np.int32)
    return np.where(n < exact, n, np.minimum(large, BUCKETS - 1))


def shape_constants():
    out = np.zeros((P, N_CONST), np.float32)

    def put(name, a):
        at, n = CONST[name]
        assert a.shape[1] == n
        out[:a.shape[0], at:at + n] = a

    row = np.arange(P)
    put("ident", np.eye(P))
    put("iota", np.broadcast_to(row.astype(np.float32), (P, P)))
    put("flip", np.eye(P)[::-1])
    pos = np.concatenate([np.arange(P, 2 * P), np.arange(P)]).astype(np.float32)
    for dim in (64, 32):
        half = dim // 2
        inv = (1.0 / (np.float32(10000.0) ** (np.arange(0, dim, 2, dtype=np.float32) / np.float32(dim)))).astype(np.float32)
        ang = (inv[row % half][:, None] * pos[None, :]).astype(np.float32)
        put(f"cos{dim}", np.cos(ang))
        put(f"sin{dim}", np.sin(ang))
        rot = np.zeros((P, P), np.float32)
        for i in range(P):
            if i % dim < half:
                rot[i + half, i] = -1.0
            else:
                rot[i - half, i] = 1.0
        put(f"rot{dim}", rot)
    q = row[:, None]
    k = row[None, :]
    causal = np.where(k <= q, 0.0, NEG)
    put("causal1", np.concatenate([causal, np.zeros((P, P + META))], 1))
    put("causal0", np.concatenate([causal, np.zeros((P, META))], 1))
    put("causalm", causal[:META, :META])
    both = np.concatenate([k + P, k], 1)
    put("band1", np.where(np.abs(both - (q + P)) <= WINDOW, 0.0, NEG))
    put("band0", np.where(np.abs(both - q) <= WINDOW, 0.0, NEG))
    sel = np.zeros((HEADS, HEADS, P), np.float32)
    for h in range(HEADS):
        sel[h, h] = -1.0
    put("select", sel.reshape(HEADS, HEADS * P))
    hot = np.zeros((BUCKETS, N_BIAS), np.float32)
    mask = np.zeros((HEADS, N_BIAS), np.float32)
    for at, n, d0, u0 in (BIAS_OWN, BIAS_PREV, BIAS_META1, BIAS_META0, BIAS_MM):
        d = d0 - (np.arange(n) + u0)
        hot[bucket_of(d), at + np.arange(n)] = 1.0
        dead = d < 0
        if (at, n, d0, u0) in (BIAS_OWN, BIAS_PREV):
            dead |= d >= WINDOW
        hot[:, at:at + n][:, dead] = 0.0
        mask[:, at:at + n][:, dead] = NEG
    put("bucket", hot)
    put("bmask", mask)
    return out


def build(nc, x_t, weights, w_ada, cond_row, up_experts, down_experts, small, vectors, w_f, b_f, rel, const, scratch, out):
    ctx = ExitStack()
    with ctx:
        base = -(-nc.sbuf_base // 32) * 32
        top = [0]

        def put(name, shape, at=None, dt=F32):
            cols = int(np.prod(shape[1:]))
            if at is None:
                at = top[0]
                top[0] += cols
            return nc.alloc_sbuf_tensor_at(name, shape, dt, offset=base + 4 * at, align_bytes=4).ap()

        ring = put("ring", [P, RING, D])
        ring_low = put("ring_low", [P, RING, D], 0, F32R)
        w_high = put("w_high", [P, HIGHS, D], dt=F32R)
        x_at = top[0]
        x_high = put("x_high", [P, DC, N1], dt=F32R)
        x_low = put("x_low", [P, DC, N1], dt=F32R)
        resid = put("resid", [P, DC, N1])
        vec = put("vec", [P, N_VEC])
        modv = put("modv", [P, 6 * DC])
        eps = put("eps", [P, 1])
        gate_parts = put("gate_parts", [P, 3, N2], top[0], BF16)
        top[0] += P
        ident = put("ident", [P, P])
        ones = put("ones", [P, P])
        iota = put("iota", [P, P])
        choice = put("choice", [P, 3, 2, PAIRS])
        gate_sum = put("gate_sum", [P, 2 * HEADS])
        choice_t = choice[:, :, :, :].rearrange("p k a n -> p k (a n)")

        arena = top[0]
        acts = put("acts", [P, KEYS, N2])
        assert base + 4 * top[0] <= nc.sbuf_usable_end
        end = top[0]
        top[0] = arena
        consts = put("consts", [P, N_CONST - 2 * P])

        def cst(name, rows=P):
            at, n = CONST[name]
            return consts[0:rows, at - 2 * P:at - 2 * P + n]

        squares_at = top[0]
        squares = put("squares", [P, DC, N1])
        cond = put("cond", [P, D], top[0] - D)
        rstds = [put(f"rstd{i}", [P, N1]) for i in range(2)]
        rstd = rstds[0]
        small_sb = put("small_sb", [P, QR_C * HEADS * QK + HEADS * (NOPE + DH)])
        w_f_sb = put("w_f_sb", [P, DC, HEADS])
        bf_sb = put("bf_sb", [P, 1])
        rel_sb = put("rel_sb", [P, HEADS])
        cum_q = put("cum_q", [P, 3, HEADS])
        stats = [put(f"stats{i}", [P, 16]) for i in range(2)]
        lin_at = top[0]
        lin_out = put("lin_out", [P, DC, N1])
        ffn_at = top[0]
        qk = put("qk", [P, N_QK1, N1])
        k_mla = qk[:, 0:HEADS, 0:N2]
        v_nat = put("v_nat", [P, 3, N_V1 * P])
        score_at = top[0]
        probs_t = [put(f"probs_t{i}", [P, 3, 4 * P]) for i in range(2)]
        score = [put("score0", [P, 4, N1 + 2]), put("score1", [P, 4, N1 + 2]), put("score2", [P, 4, N1 + 2], squares_at)]
        normed1 = put("normed1", [P, DC, N1], score_at)
        rope_tmp2 = put("rope_tmp2", [P, DC, N2], score_at)
        mixed_at = top[0]
        mixed = put("mixed", [P, DC, N1])
        f_work = put("f_work", [P, 6, N1], mixed_at)
        bias_at = top[0]
        bias1 = put("bias1", [P, HEADS, N1])
        bias_vec = put("bias_vec", [P, N_BIAS], top[0])
        bias0, biasm = put("bias0", [P, HEADS, N1 - P]), put("biasm", [P, HEADS, META])
        fox1, fox0, foxm = put("fox1", [P, HEADS, N1]), put("fox0", [P, HEADS, N1 - P]), put("foxm", [P, HEADS, META])
        assert top[0] <= end
        normed = put("normed", [P, DC, N1], bias_at)
        rope_q = put("rope_q", [P, 5, N2], bias_at + DC * N1)
        q_mla = put("q_mla", [P, HEADS, N2], bias_at + DC * N1 + 5 * N2)
        ada_slots = [put("ada_slots0", [P, 2, D], lin_at), put("ada_slots1", [P, 2, D], end - 2 * D)]
        conds = [cond, put("cond1", [P, D], end - 3 * D)]
        ffn_high = put("ffn_high", [P, FC, N1], ffn_at, F32R)
        ffn_low = put("ffn_low", [P, FC, N1], ffn_at + FC * N1, F32R)
        silu_sb = put("silu_sb", [P, 4, N1], ffn_at + 2 * FC * N1)
        assert ffn_at + 2 * FC * N1 + 4 * N1 <= end - 3 * D and 2 * FC * N1 <= bias_at - ffn_at
        top[0] = arena + KEYS * N2 // 2
        keys_s = put("keys_s", [P, 2, 16, P])
        query_at = top[0]
        query = put("query", [P, 16, N2])
        spare = put("spare", [P, 16, P], query_at)
        cand = put("cand", [P, HEADS, TOPK * TOPK], query_at + 16 * P)
        cand2 = put("cand2", [P, HEADS, TOPK * TOPK], query_at)
        top_v, top_i, top_if = (put(n, [P, 16, TOPK]) for n in ("top_v", "top_i", "top_if"))
        best_v, best_i, best_a, best_f = (put(n, [P, HEADS, TOPK]) for n in ("best_v", "best_i", "best_a", "best_f"))
        assert top[0] <= end
        last_keys = arena + (KEYS - RING) * N2
        late1, late2 = x_at + (DC + 4) * N1, x_at + 4 * N1
        hot1 = [put(f"hot1_{at}", [P, 2, GROUP, HALF], at, BF16) for at in (last_keys, late1)]
        gated1 = [put(f"gated1_{at}", [P, 2, 3, GROUP, HALF], at + GROUP * HALF, BF16) for at in (last_keys, late1)]
        hot2 = [put(f"hot2_{at}", [P, 2, GROUP, KEYS], at, BF16) for at in (last_keys + 4 * GROUP * HALF, late2)]
        zeros = put("zeros", [P, 512], late2 + GROUP * KEYS, BF16)
        assert GROUP * (4 * HALF + KEYS) <= RING * N2 and 4 * GROUP * HALF <= 4 * N1 and GROUP * KEYS + 256 <= 4 * N1

        psum = ctx.enter_context(nc.psum_tensor("psum", [P, 8, 512], F32))
        bank = [psum[:, b, :] for b in range(8)]
        flat = psum[:, :, :].rearrange("p b n -> p (b n)")

        names = """
            first_landed consts_landed second_block_landed ones_set bias_summed bias_vec_set bias_vec_stored
            bias_tables_landed bias_flipped bias_taken squared norm_summed rstd_set normed_set
            high_set low_set pool_low_set tile_used x_high_set x_low_set proj_evacuated
            forget_done forget_set forget_exp cum_set cum_turned cum_spread fox_tables_set
            cond_set cond_moved ada_used
            scores_done scores_read max_set exp_done probs_set probs_turned probs_t_set
            attended mixed_set modulated resid_set silu_set ffn_act_set ffn_high_set ffn_low_set
            shifted_set rot_done rope_set k_rope_set mla_up_done mla_up_set
            keys_scored keys_evacuated topk_set gate_exp_set gates_ready choice_turned choice_t_set
            gate_parts_set hot1_set hot2_set hot1_gated ones_restored gates_done gates_used gelu_set zeros_set
            picked_high_set picked_low_set final_set out_stored vector_step scalar_step
        """.split()
        s = {n: ctx.enter_context(nc.semaphore(n)) for n in names}
        x_landed = [ctx.enter_context(nc.semaphore(f"x_landed{i}")) for i in range(4)]
        landed = [ctx.enter_context(nc.semaphore(f"landed{i}")) for i in range(RING)]
        ada_landed = [ctx.enter_context(nc.semaphore(f"ada_landed{i}")) for i in range(2)]
        cond_landed = ctx.enter_context(nc.semaphore("cond_landed"))

        def vcol(name, j=0):
            at, n = VEC[name]
            assert j < n
            return vec[:, at + j:at + j + 1]

        R_F, R_QK1, R_V1 = 0, 1, 1 + N_QK1
        R_OUT1 = R_V1 + N_V1
        R_DOWN = R_OUT1 + DC
        R_QK2 = R_DOWN + DC
        R_V2 = R_QK2 + N_QK2
        R_OUT2 = R_V2 + N_V2
        R_QUERY = R_OUT2 + DC

        units1 = [(kind, g, qt) for qt in (0, 1, 2) for kind in (0, 1) for g in (0, 1)]
        units2 = [(kind, g, qt) for qt in (0, 1) for kind in (2, 3) for g in (0, 1)]
        units = units1 + units2

        def shape_of(u):
            kind, _, qt = units[u]
            q0, nq = TILE_COLS[qt]
            if kind >= 2:
                return 0, N2, q0, nq
            return q0, N1 - q0, q0, nq

        def key_blocks(u):
            kind, _, qt = units[u]
            k0 = shape_of(u)[0]
            last = 3 if kind < 2 else 2
            first = qt if kind < 2 else 0
            return [(t, TILE_COLS[t][0] - k0, TILE_COLS[t][1]) for t in range(first, last)]

        flips = []
        for src, dst, rows in ((fox1, bias1, P), (fox0, bias0, P), (foxm, biasm, META)):
            src, dst = (a.rearrange("p h k -> p (h k)") for a in (src, dst))
            for c in range(0, src.shape[1], 512):
                n = min(512, src.shape[1] - c)
                flips.append((src[0:rows, c:c + n], dst[0:rows, c:c + n], rows, n))

        def has_sink(u):
            return units[u][0] in (0, 2)

        block = ctx.enter_context(nc.Block())

        @block.sync
        def _(sp):
            for q in range(4):
                sp.dma_start(resid[:, 2 * q:2 * q + 2, :], x_t[:, 2 * q:2 * q + 2, :]).then_inc(x_landed[q], 16)
            for slot in range(RING):
                sp.dma_start(ring[:, slot, :], weights[slot]).then_inc(landed[slot], 16)
            sp.dma_start(consts[:, 0:SECOND_BLOCK - 2 * P], const[:, 2 * P:SECOND_BLOCK]).then_inc(s["consts_landed"], 16)
            sp.dma_start(ident[:, :], const[:, 0:P]).then_inc(s["consts_landed"], 16)
            sp.dma_start(iota[:, :], const[:, P:2 * P]).then_inc(s["consts_landed"], 16)
            for first, n, source in ((RING, T_UP, weights), (T_UP, T_DOWN_E, up_experts), (T_DOWN_E, T_END, down_experts)):
                start = 1 if first == RING else 0
                tiles = n - first + start * RING
                with sp.Fori(start, tiles // RING) as i:
                    for slot in range(RING):
                        sp.wait_ge(s["tile_used"], i * RING + (first - start * RING) + slot - RING + 1)
                        sp.dma_start(ring[:, slot, :], source[bass.ds(i * RING + slot, 1)].rearrange("a p n -> p (a n)")).then_inc(landed[slot], 16)
            for q in range(4):
                sp.wait_ge(s["final_set"], q + 1)
                sp.dma_start(out[:, 2 * q:2 * q + 2, :], lin_out[:, 2 * q:2 * q + 2, 0:N2]).then_inc(s["out_stored"], 16)
            sp.wait_ge(s["out_stored"], 4 * 16)

        @block.gpsimd
        def _(pool):
            nc.gpsimd.memset(ones[:, :], 1.0).then_inc(s["ones_set"], 1)
            nc.gpsimd.memset(eps[:, :], EPS).then_inc(s["ones_set"], 1)
            pool.wait_ge(s["norm_summed"], 1)
            pool.dma_start(cond[:, :], cond_row.partition_broadcast(P)).then_inc(cond_landed, 16)
            for j in range(2):
                pool.dma_start(ada_slots[0][:, j, :], w_ada[j]).then_inc(ada_landed[j], 16)
            pool.wait_ge(s["bias_vec_set"], 2)
            pool.dma_start(scratch, bias_vec[0:HEADS, :]).then_inc(s["bias_vec_stored"], 16)
            pool.wait_ge(s["bias_vec_stored"], 16)

            def rows(section, nq, nk):
                at, _, _, u0 = section
                return bass.AP(scratch.tensor, scratch.offset + at - u0 - (nq - 1), [[1, nq], [N_BIAS, HEADS], [1, nk]])

            pool.dma_start(fox1[:, :, 0:P], rows(BIAS_OWN, P, P)).then_inc(s["bias_tables_landed"], 16)
            pool.dma_start(fox1[:, :, P:2 * P], rows(BIAS_PREV, P, P)).then_inc(s["bias_tables_landed"], 16)
            pool.dma_start(fox1[:, :, 2 * P:N1], rows(BIAS_META1, P, META)).then_inc(s["bias_tables_landed"], 16)
            pool.dma_start(fox0[:, :, 0:P], rows(BIAS_OWN, P, P)).then_inc(s["bias_tables_landed"], 16)
            pool.dma_start(fox0[:, :, P:N1 - P], rows(BIAS_META0, P, META)).then_inc(s["bias_tables_landed"], 16)
            pool.dma_start(foxm[0:META, :, :], rows(BIAS_MM, META, META)).then_inc(s["bias_tables_landed"], 16)


            def ada_tiles(first, last, slots):
                with pool.Fori(first, last) as i:
                    for j in range(2):
                        pool.wait_ge(s["ada_used"], i * 2 + j - 1)
                        pool.dma_start(slots[:, j, :], w_ada[bass.ds(i * 2 + j, 1)].rearrange("a p n -> p (a n)")).then_inc(ada_landed[j], 16)

            ada_tiles(1, ADA_FIRST // 2, ada_slots[0])
            pool.dma_start(consts[:, SECOND_BLOCK - 2 * P:FEW_ROWS - 2 * P], const[:, SECOND_BLOCK:FEW_ROWS]).then_inc(s["second_block_landed"], 16)
            pool.dma_start(small_sb, small).then_inc(s["second_block_landed"], 16)
            pool.wait_ge(s["mixed_set"], len(units1))
            nc.gpsimd.tensor_copy(conds[1][:, :], conds[0][:, :]).then_inc(s["cond_moved"], 1)
            for j in range(2):
                pool.dma_start(ada_slots[1][:, j, :], w_ada[ADA_FIRST + j]).then_inc(ada_landed[j], 16)
            ada_tiles(ADA_FIRST // 2 + 1, N_ADA // 2, ada_slots[1])

            def pool_low(t, i=0):
                n = split_of(t)
                pool.wait_ge(s["high_set"], i * RING + n + 1)
                nc.gpsimd.tensor_tensor(ring_low[:, t % RING, :], ring[:, t % RING, :], w_high[:, n % HIGHS, :].bitcast(F32),
                                        ALU.subtract).then_inc(s["pool_low_set"], 1)

            def pool_lows(t, i=0):
                if by_pool(t + LEAD):
                    pool_low(t + LEAD, i)

            def gate_rows(n, g, b, place):
                shape = [P, 3, GROUP, HALF]
                gates = gate_parts[:, :, bass.ds(g * GROUP, GROUP)].unsqueeze(3).broadcast_to(shape)
                pool.wait_ge(s["hot1_set"], n + 1)
                nc.gpsimd.tensor_tensor(gated1[place][:, b], hot1[place][:, b].unsqueeze(1).broadcast_to(shape), gates,
                                        ALU.mult).then_inc(s["hot1_gated"], 1)

            for t in range(T_UP, T_UP + LEAD):
                if by_pool(t):
                    pool_low(t)
            with pool.Fori(0, HALF // RING) as i:
                for k in range(RING):
                    pool_lows(T_UP + k, i)
            pool.wait_ge(s["gate_parts_set"], 1)
            with pool.Fori(0, HALF // RING) as i:
                for k in range(RING):
                    pool_lows(T_UP + HALF + k, i)
                    gate_rows(i * RING + k, i * RING + k, k % 2, 0)
            pool.wait_ge(s["tile_used"], T_DOWN_E)
            nc.gpsimd.memset(zeros[:, :], 0.0).then_inc(s["zeros_set"], 1)
            with pool.Fori(0, HALF // RING) as i:
                for k in range(RING):
                    pool_lows(T_DOWN_E + k, i)
                    gate_rows(i * RING + k + GROUPS, i * RING + k, k % 2, 1)
            with pool.Fori(HALF // RING, KEYS // RING - 1) as i:
                for k in range(RING):
                    pool_lows(T_DOWN_E + k, i)
            for t in range(T_END - RING, T_END - LEAD):
                pool_lows(t)
            pool.wait_ge(s["hot1_gated"], 2 * GROUPS)
            nc.gpsimd.memset(ones[:, :], 1.0).then_inc(s["ones_restored"], 1)

        @block.scalar
        def _(act):
            steps = [0]

            def step(ins):
                steps[0] += 1
                ins.then_inc(s["scalar_step"], 1)

            def settle():
                act.wait_ge(s["scalar_step"], steps[0])

            act.dma_start(vec[:, :], vectors).then_inc(s["first_landed"], 16)
            act.dma_start(w_f_sb, w_f).then_inc(s["first_landed"], 16)
            act.dma_start(bf_sb[0:HEADS, :], b_f).then_inc(s["first_landed"], 16)
            act.dma_start(rel_sb[0:BUCKETS, :], rel).then_inc(s["first_landed"], 16)
            act.dma_start(consts[0:BUCKETS, FEW_ROWS - 2 * P:], const[0:BUCKETS, FEW_ROWS:]).then_inc(s["first_landed"], 16)

            def square(src, at, n):
                chunks = src.shape[1]
                nc.scalar.activation(squares[:, at:at + chunks, 0:n], src, ACT.Square).then_inc(s["squared"], 1)

            norms = [0]

            def factors(n, *sizes):
                act.wait_ge(s["norm_summed"], norms[0] + len(sizes))
                for m, chunks in enumerate(sizes):
                    step(nc.scalar.activation(rstds[m][:, 0:n], bank[7][:, m * N2:m * N2 + n], ACT.Ln, bias=eps[:, 0:1], scale=1.0 / (chunks * P)))
                settle()
                for m in range(len(sizes)):
                    nc.scalar.activation(rstds[m][:, 0:n], rstds[m][:, 0:n], ACT.Exp, scale=-0.5).then_inc(s["rstd_set"], 1)
                norms[0] += len(sizes)

            def high(t):
                n = split_of(t)
                act.wait_ge(landed[t % RING], 16 * (t // RING + 1))
                if n >= HIGHS:
                    act.wait_ge(s["tile_used"], tile_of(n - HIGHS) + 1)
                nc.scalar.activation(w_high[:, n % HIGHS, :], ring[:, t % RING, :], ACT.Copy).then_inc(s["high_set"], 1)

            next_high = [0]

            def high_to(t):
                while next_high[0] < t:
                    if next_high[0] not in WHOLE:
                        high(next_high[0])
                    next_high[0] += 1

            def x_high_pair(src, q, n):
                c = slice(2 * q, 2 * q + 2)
                nc.scalar.activation(x_high[:, c, 0:n], src[:, c, 0:n], ACT.Copy).then_inc(s["x_high_set"], 1)

            def x_highs(src, n, first_normed):
                for q in range(4):
                    if first_normed is not None:
                        act.wait_ge(s["normed_set"], first_normed + q + 1)
                    x_high_pair(src, q, n)

            def evacuate(r, t, dst, src, scale=1.0, more=()):
                high_to(min(t + 1 + LEAD, T_SUB))
                act.wait_ge(s["tile_used"], t + 1)
                ins = nc.scalar.activation(dst, src, ACT.Copy, scale=scale)
                for d, f in more:
                    ins = nc.scalar.activation(d, f, ACT.Copy)
                ins.then_inc(s["proj_evacuated"], 1)

            act.wait_ge(s["ones_set"], 2)
            for q in range(4):
                act.wait_ge(x_landed[q], 16)
                square(resid[:, 2 * q:2 * q + 2, :], 2 * q, N1)
            high_to(LEAD)
            factors(N1, DC)
            x_highs(normed1, N1, 0)
            act.wait_ge(s["forget_done"], 1)
            nc.scalar.activation(f_work[0:HEADS, 0, :], bank[R_F % 4][0:HEADS, 0:N1], ACT.Copy).then_inc(s["proj_evacuated"], 1)
            act.wait_ge(s["forget_set"], 1)
            step(nc.scalar.activation(f_work[0:HEADS, 1, :], f_work[0:HEADS, 0, :], ACT.Abs))
            settle()
            step(nc.scalar.activation(f_work[0:HEADS, 2, :], f_work[0:HEADS, 1, :], ACT.Exp, scale=-1.0))
            settle()
            nc.scalar.activation(f_work[0:HEADS, 1, :], f_work[0:HEADS, 2, :], ACT.Ln, bias=ones[0:HEADS, 0:1]).then_inc(s["forget_exp"], 1)
            act.wait_ge(cond_landed, 16)
            nc.scalar.activation(cond[:, :], cond[:, :], ACT.Silu).then_inc(s["cond_set"], 1)
            for j in range(N_QK1):
                r = R_QK1 + j
                evacuate(r, T_QK1 + j, qk[:, j, :], bank[r % 4][:, 0:N1], scale=0.125 if j < 4 or 5 <= j < 9 else 1.0)
            for n, (_, dst, rows, cols) in enumerate(flips):
                act.wait_ge(s["bias_flipped"], n + 1)
                nc.scalar.activation(dst, bank[4 + n % 4][0:rows, 0:cols], ACT.Copy).then_inc(s["bias_taken"], 1)
            for j in range(N_V1):
                r = R_V1 + j
                b = bank[r % 4][:, 0:3 * P].rearrange("p (t n) -> p t n", n=P)
                evacuate(r, T_V1 + j, v_nat[:, 0:2, j * P:(j + 1) * P], b[:, 0:2, :],
                         more=[(v_nat[0:META, 2, j * P:(j + 1) * P], b[0:META, 2, :])])

            def exps(u):
                _, nk, _, nq = shape_of(u)
                n = nk + has_sink(u)
                act.wait_ge(s["max_set"], u + 1)
                for h in range(4):
                    ins = nc.scalar.activation(score[u % 3][0:nq, h, 0:n], score[u % 3][0:nq, h, 0:n], ACT.Exp,
                                               bias=stats[u % 2][0:nq, 4 + h:5 + h],
                                               accum_out=stats[u % 2][0:nq, 8 + h:9 + h])
                ins.then_inc(s["exp_done"], 1)

            def take_probs_t(u):
                nq = shape_of(u)[3]
                act.wait_ge(s["probs_turned"], u + 1)
                if u >= 2:
                    act.wait_ge(s["attended"], u - 1)
                for t, _, kn in key_blocks(u):
                    ins = nc.scalar.activation(
                        probs_t[u % 2][0:kn, t, :].rearrange("p (h q) -> p h q", q=P)[:, :, 0:nq],
                        bank[4 + t][0:kn, :].rearrange("p (h q) -> p h q", q=P)[:, :, 0:nq], ACT.Copy)
                ins.then_inc(s["probs_t_set"], 1)

            def attention(u0, u1):
                for u in range(u0, u1 + 1):
                    if u < u1:
                        exps(u)
                    if u > u0:
                        take_probs_t(u - 1)

            attention(0, len(units1))
            act.wait_ge(s["mixed_set"], len(units1))
            x_highs(mixed, N1, None)

            def take_outputs(r0, last_tile):
                for j in range(DC):
                    evacuate(r0 + j, last_tile(j), lin_out[:, j, :], bank[(r0 + j) % 4][:, 0:N1])
                    if j % 2:
                        act.wait_ge(s["proj_evacuated"], r0 + j + 1)
                        square(lin_out[:, j - 1:j + 1, :], j - 1, N1)

            def resid_squares(n, before):
                for q in range(4):
                    act.wait_ge(s["resid_set"], before + q + 1)
                    square(resid[:, 2 * q:2 * q + 2, 0:n], 2 * q, n)

            act.wait_ge(s["cond_moved"], 1)
            take_outputs(R_OUT1, lambda j: T_OUT1 + j)
            factors(N1, DC)
            resid_squares(N1, 0)
            factors(N1, DC)
            x_highs(normed, N1, 4)

            def loop_high(i, t):
                n = split_of(t)
                act.wait_ge(landed[t % RING], (i + t // RING + 1) * 16)
                act.wait_ge(s["tile_used"], i * RING + t - HIGHS + 1)
                nc.scalar.activation(w_high[:, n % HIGHS, :], ring[:, t % RING, :], ACT.Copy).then_inc(s["high_set"], 1)

            def silu(j, k):
                act.wait_ge(s["tile_used"], j * 2 + T_FFN + 2)
                nc.scalar.activation(silu_sb[:, k, :], bank[2 * k][:, 0:N1], ACT.Silu).then_inc(s["silu_set"], 1)

            def ffn_highs(j, at, k):
                act.wait_ge(s["ffn_act_set"], j + 1)
                nc.scalar.activation(ffn_high[:, at, :], silu_sb[:, k:k + 1, :], ACT.Copy).then_inc(s["ffn_high_set"], 1)

            def silu_pair(i, k):
                j = i * 4 + k
                unrolled = isinstance(i, int)
                for d in (0, 1):
                    loop_high(i, T_FFN + 2 * k + LEAD + d)
                if not (unrolled and i == 0):
                    act.wait_ge(s["ffn_low_set"], j - 3)
                silu(j, k)
                if not (unrolled and j == 0):
                    ffn_highs(j - 1, slice(j - 1, j) if unrolled else bass.ds(j - 1, 1), (k - 1) % 4)

            for k in range(4):
                silu_pair(0, k)
            with act.Fori(1, FC // 4) as i:
                for k in range(4):
                    silu_pair(i, k)
            for k in range(FC % 4):
                silu_pair(FC // 4, k)
            ffn_highs(FC - 1, slice(FC - 1, FC), (FC - 1) % 4)
            next_high[0] = T_DOWN + LEAD
            take_outputs(R_DOWN, lambda j: T_DOWN + (j * FC + FC - 1) // DC)
            factors(N1, DC)

            resid_squares(N2, 4)
            factors(N2, DC)

            def shifted(dst, c, at):
                return nc.scalar.activation(dst, normed[:, c, 0:N2], ACT.Identity, bias=modv[:, at + c:at + c + 1])

            def shifted_highs(n, at):
                for c in range(DC):
                    act.wait_ge(s["modulated"], n * DC + c + 1)
                    ins = shifted(x_high[:, c, 0:N2], c, at)
                    if c % 2:
                        ins.then_inc(s["x_high_set"], 1)

            shifted_highs(0, 0)
            for j in range(N_QK2):
                r = R_QK2 + j
                evacuate(r, T_QK2 + j, qk[:, j, 0:N2], bank[r % 4][:, 0:N2], scale=0.125 if j < 4 else 1.0)
                if j < DC:
                    shifted(lin_out[:, j, 0:N2], j, 0).then_inc(s["shifted_set"], 1)
                if j == 6:
                    act.wait_ge(s["proj_evacuated"], r + 1)
                    square(qk[:, 5:7, 0:N2], 0, N2)
                if j == 7:
                    act.wait_ge(s["proj_evacuated"], r + 1)
                    square(qk[:, 7:8, 0:N2], 2, N2)
            factors(N2, QR_C, 1)
            b = bank[R_V2 % 4][:, 0:2 * P].rearrange("p (t n) -> p t n", n=P)
            evacuate(R_V2, T_V2, v_nat[:, 0:2, 0:P], b)
            def heads(half):
                return slice(4 * half, 4 * half + 4), flat[:, 1024 * half:1024 * (half + 1)].rearrange("p (h n) -> p h n", n=N2)

            for half in range(2):
                h, src = heads(half)
                act.wait_ge(s["mla_up_done"], half + 1)
                nc.scalar.activation(q_mla[0:QK, h, :], src[0:QK], ACT.Copy, scale=float(QK) ** -0.5).then_inc(s["mla_up_set"], 1)
            act.wait_ge(s["mla_up_done"], 3)
            nc.scalar.activation(v_nat[:, 0:2, P:P + HEADS * DH],
                                 flat[:, 2048:3072].rearrange("p (t n) -> p t n", n=512), ACT.Copy).then_inc(s["mla_up_set"], 1)
            act.wait_ge(s["rope_set"], 2)
            for half in range(2):
                h, src = heads(half)
                act.wait_ge(s["mla_up_done"], half + 4)
                nc.scalar.activation(k_mla[0:NOPE, h, :], src[0:NOPE], ACT.Copy).then_inc(s["mla_up_set"], 1)
            attention(len(units1), len(units))
            act.wait_ge(s["mixed_set"], len(units))
            for q in range(4):
                square(mixed[:, 2 * q:2 * q + 2, 0:N2], 2 * q, N2)
            factors(N2, 4, 4)
            x_highs(normed, N2, 10)
            for j in range(DC):
                high_to(T_OUT2 + j + 1 + LEAD)
                if j % 2:
                    act.wait_ge(s["proj_evacuated"], R_OUT2 + j + 1)
                    square(resid[:, j - 1:j + 1, 0:N2], j - 1, N2)
            factors(N2, DC)
            shifted_highs(1, 3 * DC)
            for j in range(N_QUERY):
                r = R_QUERY + j
                evacuate(r, T_QUERY + j, query[:, j, :], bank[r % 4][:, 0:N2])
            high_to(T_UP + LEAD)
            for tt in range(2):
                act.wait_ge(s["keys_scored"] if tt == 0 else s["tile_used"], 1 if tt == 0 else T_UP)
                nc.scalar.activation(keys_s[:, tt], flat[:, (1 - tt) * 2048:(2 - tt) * 2048].rearrange("p (a n) -> p a n", n=P),
                                     ACT.Copy).then_inc(s["keys_evacuated"], 1)

            def gelu(e, at, k):
                act.wait_ge(s["tile_used"], e + T_UP + 1)
                nc.scalar.activation(acts[:, at, :], bank[4 + k][:, 0:N2].unsqueeze(1), ACT.Gelu).then_inc(s["gelu_set"], 1)

            for e in range(RING):
                high_to(T_UP + e + 1 + LEAD)
                gelu(e, slice(e, e + 1), e % 4)

            def gelus(first, last):
                with act.Fori(first, last) as i:
                    for k in range(RING):
                        loop_high(i, T_UP + k + LEAD)
                        e = i * RING + k
                        gelu(e, bass.ds(e, 1), k % 4)

            gelus(1, HALF // RING - 1)
            act.wait_ge(s["topk_set"], 1)
            nc.scalar.activation(choice[:, 2], choice[:, 2], ACT.Exp).then_inc(s["gate_exp_set"], 1)
            gelus(HALF // RING - 1, HALF // RING)
            act.wait_ge(s["choice_turned"], 1)
            nc.scalar.activation(choice_t, flat[:, 0:6 * P].rearrange("p (k n) -> p k n", k=3), ACT.Copy).then_inc(s["choice_t_set"], 1)
            gelus(HALF // RING, KEYS // RING - 1)
            for k in range(RING):
                loop_high(KEYS // RING - 1, T_UP + k + LEAD)

            def picked_high(at, k):
                nc.scalar.activation(x_high[:, k:k + 1, 0:N2], acts[:, at, :], ACT.Copy).then_inc(s["picked_high_set"], 1)

            def down_operands(first, last):
                with act.Fori(first, last) as i:
                    for k in range(RING):
                        loop_high(i, T_DOWN_E + k + LEAD)
                        picked_high(bass.ds(i * RING + k + LEAD, 1), (k + LEAD) % 4)

            act.wait_ge(s["tile_used"], T_DOWN_E)
            act.wait_ge(s["gates_used"], GROUPS)
            for e in range(LEAD):
                picked_high(slice(e, e + 1), e % 4)
            for k in range(RING):
                nc.scalar.activation(acts[:, KEYS - RING + k, :], bank[4 + k % 4][:, k // 4 * N2:(k // 4 + 1) * N2],
                                     ACT.Gelu).then_inc(s["gelu_set"], 1)
            down_operands(0, HALF // RING - 1)
            for e in range(HALF - RING, HALF):
                loop_high(0, T_DOWN_E + e + LEAD)
                if e + LEAD < HALF:
                    picked_high(slice(e + LEAD, e + LEAD + 1), (e + LEAD) % 4)
            act.wait_ge(s["gates_used"], 2 * GROUPS)
            for e in range(HALF, HALF + LEAD):
                picked_high(slice(e, e + 1), e % 4)
            down_operands(HALF // RING, KEYS // RING - 1)
            for e in range(KEYS - RING + LEAD, KEYS):
                loop_high(0, T_DOWN_E + e)
                picked_high(slice(e, e + 1), e % 4)
            resid_squares(N2, 8)
            factors(N2, DC)

        @block.tensor
        def _(pe):
            def wait_low(t, i=0):
                a_round = RING if t < T_UP else lows_until(t + RING) - lows_until(t)
                pe.wait_ge(s["pool_low_set" if by_pool(t) else "low_set"], i * a_round + lows_until(t))

            def tile(t):
                wait_low(t)
                return w_high[:, split_of(t) % HIGHS, :], ring_low[:, t % RING, :]

            def cut_cols(a, c):
                return a[:, c * P:(c + 1) * P]

            squared = [0]

            def sum_pair(at, of, n, col=0, width=2):
                squared[0] += 1
                pe.wait_ge(s["squared"], squared[0])
                for c in range(at, at + width):
                    ins = nc.tensor.matmul(bank[7][:, col:col + n], ones[:, :], squares[:, c, 0:n], start=(c == of[0]), stop=(c == of[-1]))
                if c == of[-1]:
                    ins.then_inc(s["norm_summed"], 1)

            def sum_squares(n):
                for q in range(4):
                    sum_pair(2 * q, range(DC), n)

            def bank_free(r):
                if r >= 4:
                    pe.wait_ge(s["proj_evacuated"], r - 3)
                return bank[r % 4]

            def layer(b, parts, n, new_input=None):
                high, low = parts
                for c in range(DC):
                    if new_input is not None and c % 2 == 0:
                        pe.wait_ge(s["x_low_set"], 4 * new_input + c // 2 + 1)
                    xh, xl = x_high[:, c, 0:n], x_low[:, c, 0:n]
                    nc.tensor.matmul(b[:, 0:n], cut_cols(high, c), xh, start=(c == 0), stop=False)
                    nc.tensor.matmul(b[:, 0:n], cut_cols(high, c), xl, start=False, stop=False)
                    ins = nc.tensor.matmul(b[:, 0:n], cut_cols(low, c), xh, start=False, stop=(c == DC - 1))
                ins.then_inc(s["tile_used"], 1)

            def linear(r, t, n, new_input=None):
                layer(bank_free(r), tile(t), n, new_input)

            def natural(r, t, tiles, src):
                b = bank_free(r)
                pe.wait_ge(landed[t % RING], 16 * (t // RING + 1))
                for q, (q0, nq) in enumerate(tiles):
                    for c in range(DC):
                        ins = nc.tensor.matmul(b[0:nq, q * P:(q + 1) * P], src[:, c, q0:q0 + nq], cut_cols(ring[:, t % RING, :], c),
                                               start=(c == 0), stop=(c == DC - 1))
                ins.then_inc(s["tile_used"], 1)

            pe.wait_ge(s["ones_set"], 1)
            sum_squares(N1)
            pe.wait_ge(s["first_landed"], 16 * 5)
            hot = cst("bucket", BUCKETS)
            nc.tensor.matmul(bank[4][0:HEADS, 0:512], rel_sb[0:BUCKETS, :], hot[:, 0:512], start=True, stop=True)
            nc.tensor.matmul(bank[5][0:HEADS, 0:N_BIAS - 512], rel_sb[0:BUCKETS, :], hot[:, 512:N_BIAS],
                             start=True, stop=True).then_inc(s["bias_summed"], 1)
            for c in range(DC):
                if c % 2 == 0:
                    pe.wait_ge(s["normed_set"], c // 2 + 1)
                ins = nc.tensor.matmul(bank[0][0:HEADS, 0:N1], w_f_sb[:, c, :], normed1[:, c, :], start=(c == 0), stop=(c == DC - 1))
            ins.then_inc(s["forget_done"], 1)
            for j in range(N_QK1):
                linear(R_QK1 + j, T_QK1 + j, N1, 0 if j == 0 else None)
            pe.wait_ge(s["consts_landed"], 16 * 3)
            pe.wait_ge(s["bias_tables_landed"], 16 * 6)
            for n, (src, _, rows, cols) in enumerate(flips):
                if n >= 4:
                    pe.wait_ge(s["bias_taken"], n - 3)
                nc.tensor.matmul(bank[4 + n % 4][0:rows, 0:cols], cst("flip")[0:rows, P - rows:P], src, start=True, stop=True).then_inc(s["bias_flipped"], 1)
            def spread(h):
                if h >= 2:
                    pe.wait_ge(s["fox_tables_set"], h - 1)
                sel = cst("select", HEADS).rearrange("p (h n) -> p h n", n=P)
                nc.tensor.matmul(bank[5 + h % 2][:, 0:N1], sel[:, h, :], f_work[0:HEADS, 5, :], start=True, stop=True).then_inc(s["cum_spread"], 1)

            natural(R_V1, T_V1, TILE_COLS, normed1)
            pe.wait_ge(s["bias_taken"], len(flips))
            pe.wait_ge(s["cum_set"], 3)
            for t, (c0, n) in enumerate(TILE_COLS):
                ins = nc.tensor.transpose(bank[4][0:n, t * HEADS:(t + 1) * HEADS], f_work[0:HEADS, 5, c0:c0 + n], ident[0:HEADS, 0:HEADS])
            ins.then_inc(s["cum_turned"], 1)
            spread(0)
            spread(1)
            for j in range(1, N_V1):
                natural(R_V1 + j, T_V1 + j, TILE_COLS, normed1)
                for h in (2 * j, 2 * j + 1):
                    if h < HEADS:
                        spread(h)

            def scores(u):
                kind, g, _ = units[u]
                k0, nk, q0, nq = shape_of(u)
                if u not in (0, len(units1)):
                    pe.wait_ge(s["scores_read"], u)
                for h in range(4):
                    c, half = 2 * g + h // 2, h % 2
                    rows = slice(half * DH, half * DH + DH)
                    if kind == 0:
                        lhs, rhs = qk[rows, c, q0:q0 + nq], qk[rows, 4, k0:k0 + nk]
                    elif kind == 1:
                        lhs, rhs = qk[rows, 5 + c, q0:q0 + nq], qk[rows, 9 + c, k0:k0 + nk]
                    elif kind == 2:
                        lhs, rhs = rope_q[rows, c, q0:q0 + nq], rope_q[rows, 4, k0:k0 + nk]
                    else:
                        lhs, rhs = q_mla[0:QK, 4 * g + h, q0:q0 + nq], k_mla[0:QK, 4 * g + h, k0:k0 + nk]
                    ins = nc.tensor.matmul(bank[h][0:nq, 0:nk], lhs, rhs, start=True, stop=True)
                ins.then_inc(s["scores_done"], 1)

            def turn_probs(u):
                nq = shape_of(u)[3]
                pe.wait_ge(s["probs_set"], u + 1)
                if u > 0:
                    pe.wait_ge(s["probs_t_set"], u)
                for t, k0, kn in key_blocks(u):
                    for h in range(4):
                        ins = nc.tensor.transpose(bank[4 + t][0:kn, h * P:h * P + nq], score[u % 3][0:nq, h, k0:k0 + kn], ident[0:nq, 0:nq])
                ins.then_inc(s["probs_turned"], 1)

            def attend(u):
                kind, g, _ = units[u]
                nq = shape_of(u)[3]
                pe.wait_ge(s["probs_t_set"], u + 1)
                if u > 0:
                    pe.wait_ge(s["mixed_set"], u)
                blocks = key_blocks(u)
                for h in range(4):
                    c, half = 2 * g + h // 2, h % 2
                    vc = half * DH if kind in (0, 2) else P + (2 * c + half) * DH
                    for n, (t, _, kn) in enumerate(blocks):
                        ins = nc.tensor.matmul(bank[7][half * DH:(half + 1) * DH, (h // 2) * P:(h // 2) * P + nq],
                                               v_nat[0:kn, t, vc:vc + DH], probs_t[u % 2][0:kn, t, h * P:h * P + nq],
                                               start=(n == 0), stop=(n == len(blocks) - 1))
                ins.then_inc(s["attended"], 1)

            def attention(u0, u1):
                scores(u0)
                for u in range(u0, u1 + 2):
                    if u + 1 < u1:
                        scores(u + 1)
                    if u0 < u <= u1:
                        turn_probs(u - 1)
                    if u > u0 + 1:
                        attend(u - 2)

            pe.wait_ge(s["fox_tables_set"], HEADS)
            pe.wait_ge(s["proj_evacuated"], R_OUT1)
            attention(0, len(units1))
            for j in range(DC):
                linear(R_OUT1 + j, T_OUT1 + j, N1, 1 if j == 0 else None)
                if j in (3, 5, 7):
                    sum_pair(j - 3, range(DC), N1)
            sum_pair(DC - 2, range(DC), N1)
            sum_squares(N1)

            def gate_up(i, k):
                for side in range(2):
                    t = T_FFN + 2 * k + side
                    wait_low(t, i)
                    if side == 0 and not (isinstance(i, int) and i == 0):
                        pe.wait_ge(s["ffn_act_set"], i * 4 + k - 3)
                    layer(bank[2 * k + side], (w_high[:, split_of(t) % HIGHS, :], ring_low[:, t % RING, :]), N1,
                          2 if isinstance(i, int) and i + k + side == 0 else None)

            for k in range(4):
                gate_up(0, k)
            with pe.Fori(1, FC // 4) as i:
                for k in range(4):
                    gate_up(i, k)
            for k in range(FC % 4):
                gate_up(FC // 4, k)
            pe.wait_ge(s["ffn_act_set"], FC)
            for j in range(DC):
                b = bank_free(R_DOWN + j)
                for f in range(FC):
                    if j == 0:
                        pe.wait_ge(s["ffn_low_set"], f + 1)
                    n = j * FC + f
                    high, low = (cut_cols(a, n % DC) for a in tile(T_DOWN + n // DC))
                    nc.tensor.matmul(b[:, 0:N1], high, ffn_high[:, f, :], start=(f == 0), stop=False)
                    nc.tensor.matmul(b[:, 0:N1], high, ffn_low[:, f, :], start=False, stop=False)
                    ins = nc.tensor.matmul(b[:, 0:N1], low, ffn_high[:, f, :], start=False, stop=(f == FC - 1))
                    if n % DC == DC - 1:
                        ins.then_inc(s["tile_used"], 1)
                if j in (3, 5, 7):
                    sum_pair(j - 3, range(DC), N1)
            sum_pair(DC - 2, range(DC), N1)

            sum_squares(N2)
            for j in range(N_QK2):
                linear(R_QK2 + j, T_QK2 + j, N2, 3 if j == 0 else None)
                if j == 6:
                    pe.wait_ge(s["second_block_landed"], 2 * 16)
                    pe.wait_ge(s["proj_evacuated"], R_QK2 + 5)
                    for c in range(5):
                        ins = nc.tensor.matmul(flat[:, 2048 + c * N2:2048 + (c + 1) * N2], cst("rot64"), qk[:, c, 0:N2], start=True, stop=True)
                    ins.then_inc(s["rot_done"], 1)
            sum_pair(0, range(QR_C), N2)
            sum_pair(2, range(2, 3), N2, N2, 1)
            pe.wait_ge(s["shifted_set"], DC)
            natural(R_V2, T_V2, TILE_COLS[0:2], lin_out)
            pe.wait_ge(s["proj_evacuated"], R_V2)
            pe.wait_ge(s["rope_set"], 1)
            nc.tensor.matmul(bank[6][:, N2:2 * N2], cst("rot32"), qk[:, 8, 0:N2], start=True, stop=True).then_inc(s["rot_done"], 1)
            w_q = small_sb[:, 0:QR_C * HEADS * QK].rearrange("p (c n) -> p c n", c=QR_C)
            w_kv = small_sb[:, QR_C * HEADS * QK:2560].rearrange("p (h n) -> p h n", h=HEADS)
            pe.wait_ge(s["proj_evacuated"], R_OUT2)
            pe.wait_ge(s["normed_set"], 9)
            for half in range(2):
                for h in range(4 * half, 4 * half + 4):
                    for c in range(QR_C):
                        ins = nc.tensor.matmul(flat[0:QK, h * N2:(h + 1) * N2], w_q[:, c, h * QK:(h + 1) * QK], normed[:, c, 0:N2],
                                               start=(c == 0), stop=(c == QR_C - 1))
                ins.then_inc(s["mla_up_done"], 1)
            pe.wait_ge(s["normed_set"], 10)
            for t in range(2):
                ins = nc.tensor.matmul(bank[4 + t][:, :], normed[:, 2, t * P:(t + 1) * P], w_kv[:, :, NOPE:NOPE + DH], start=True, stop=True)
            ins.then_inc(s["mla_up_done"], 1)
            for half in range(2):
                pe.wait_ge(s["mla_up_set"], half + 1)
                for h in range(4 * half, 4 * half + 4):
                    ins = nc.tensor.matmul(flat[0:NOPE, h * N2:(h + 1) * N2], w_kv[:, h, 0:NOPE], normed[:, 2, 0:N2], start=True, stop=True)
                ins.then_inc(s["mla_up_done"], 1)
            rot = cst("rot32")[0:QK, 0:QK]
            for half in range(2):
                pe.wait_ge(s["mla_up_set"], half + 3)
                for h in range(4):
                    at = 2048 * (1 - half) + h * N2
                    ins = nc.tensor.matmul(flat[0:QK, at:at + N2], rot, q_mla[0:QK, 4 * half + h, :], start=True, stop=True)
                ins.then_inc(s["rot_done"], 1)
            pe.wait_ge(s["mla_up_set"], 5)
            pe.wait_ge(s["rope_set"], 4)
            pe.wait_ge(s["k_rope_set"], 1)
            attention(len(units1), len(units))
            for q in range(4):
                sum_pair(2 * q, range(0, 4) if q < 2 else range(4, 8), N2, 0 if q < 2 else N2)
            for j in range(DC):
                linear(R_OUT2 + j, T_OUT2 + j, N2, 4 if j == 0 else None)
                if j in (3, 5, 7):
                    sum_pair(j - 3, range(DC), N2)
            sum_pair(DC - 2, range(DC), N2)
            for j in range(N_QUERY):
                linear(R_QUERY + j, T_QUERY + j, N2, 5 if j == 0 else None)
            pe.wait_ge(s["proj_evacuated"], R_QUERY + N_QUERY)
            for k in range(N_SUB):
                t = T_SUB + k
                pe.wait_ge(landed[t % RING], 16 * (t // RING + 1))
            for tt in range(2):
                for a in range(16):
                    ins = nc.tensor.matmul(flat[:, (1 - tt) * 2048 + a * P:(1 - tt) * 2048 + (a + 1) * P], query[:, a, tt * P:(tt + 1) * P],
                                           cut_cols(ring[:, (T_SUB + a // 8) % RING, :], a % 8), start=True, stop=True)
                if tt == 0:
                    ins.then_inc(s["keys_scored"], 1)
                else:
                    ins.then_inc(s["tile_used"], N_SUB)
            pe.wait_ge(s["keys_evacuated"], 1)

            def up(i, k, base=0, last=False):
                t = T_UP + base * RING + k
                wait_low(t, i)
                col = N2 * (k // 4) if last else 0
                if (t >= T_UP + 4 or not isinstance(i, int)) and col == 0:
                    pe.wait_ge(s["gelu_set"], i * RING + base * RING + k - 3)
                layer(bank[4 + k % 4][:, col:col + N2], (w_high[:, split_of(t) % HIGHS, :], ring_low[:, t % RING, :]), N2)

            def gate_matrices(n, b, place, late=False):
                pe.wait_ge(s["hot2_set"], n + 1)
                pe.wait_ge(s["hot1_gated"], n + 1)
                if not isinstance(n, int) or n >= 2:
                    pe.wait_ge(s["gates_used"], n - 1)
                for q in range(GROUP):
                    for part in range(3):
                        ins = nc.tensor.matmul(bank[(4 if late else 0) + b][:, q * HALF:(q + 1) * HALF], hot2[place][:, b, q, :],
                                               gated1[place][:, b, part, q, :], start=(part == 0), stop=(part == 2))
                ins.then_inc(s["gates_done"], 1)

            for k in range(RING):
                up(0, k)
            with pe.Fori(1, HALF // RING) as i:
                for k in range(RING):
                    up(i, k)
            pe.wait_ge(s["gates_ready"], 1)
            for k in range(3):
                for tt in range(2):
                    ins = nc.tensor.transpose(flat[:, (2 * k + tt) * P:(2 * k + tt + 1) * P], choice[:, k, tt, :], ident[:, :])
            ins.then_inc(s["choice_turned"], 1)
            for k in range(RING):
                up(0, k, HALF // RING)
                if k == 0:
                    pe.wait_ge(s["choice_t_set"], 1)
                else:
                    gate_matrices(k - 1, (k - 1) % 2, 0)
            with pe.Fori(1, HALF // RING - 1) as i:
                for k in range(RING):
                    up(i - 1, k, HALF // RING + 1)
                    gate_matrices(i * RING + (k - 1), (k - 1) % 2, 0)
            for k in range(RING):
                up(0, k, KEYS // RING - 1, True)
                gate_matrices(GROUPS - RING + k - 1, (k - 1) % 2, 0)
            gate_matrices(GROUPS - 1, 1, 0)
            pe.wait_ge(s["gates_used"], GROUPS)
            pe.wait_ge(s["zeros_set"], 1)
            for b in range(4):
                nc.tensor.matmul(bank[b][:, :], zeros[:, 0:P], zeros[:, :], start=True, stop=True)

            def down(i, k):
                t = T_DOWN_E + k
                wait_low(t, i)
                pe.wait_ge(s["picked_low_set"], i * RING + k + 1)
                high, low = w_high[:, split_of(t) % HIGHS, :], ring_low[:, t % RING, :]
                xh, xl = x_high[:, k % 4, 0:N2], x_low[:, k % 4, 0:N2]
                for c in range(DC):
                    for w, x in ((high, xh), (high, xl), (low, xh)):
                        ins = nc.tensor.matmul(flat[:, c * N2:(c + 1) * N2], cut_cols(w, c), x, start=False, stop=False, skip_group_check=True)
                ins.then_inc(s["tile_used"], 1)

            for k in range(RING):
                down(0, k)
                if k == 0:
                    pe.wait_ge(s["gelu_set"], KEYS)
                else:
                    gate_matrices(GROUPS + k - 1, (k - 1) % 2, 1, True)
            with pe.Fori(1, HALF // RING) as i:
                for k in range(RING):
                    down(i, k)
                    gate_matrices(i * RING + (GROUPS + k - 1), (k - 1) % 2, 1, True)
            gate_matrices(2 * GROUPS - 1, 1, 1, True)
            with pe.Fori(HALF // RING, KEYS // RING) as i:
                for k in range(RING):
                    down(i, k)
            pe.wait_ge(s["ones_restored"], 1)
            sum_squares(N2)

        @block.vector
        def _(dve):
            steps = [0]

            def step(ins):
                steps[0] += 1
                ins.then_inc(s["vector_step"], 1)

            def settle():
                dve.wait_ge(s["vector_step"], steps[0])

            def normalise(dst, src, gain, chunks, n, factor=rstd):
                for c in chunks:
                    ins = nc.vector.scalar_tensor_tensor(out=dst[:, c, 0:n], in0=src[:, c, 0:n], scalar=vcol(gain[0], gain[1] + c),
                                                         in1=factor[:, 0:n], op0=ALU.mult, op1=ALU.mult)
                return ins

            next_low = [0]

            def low(t):
                n = split_of(t)
                dve.wait_ge(s["high_set"], n + 1)
                nc.vector.tensor_tensor(ring_low[:, t % RING, :], ring[:, t % RING, :], w_high[:, n % HIGHS, :].bitcast(F32),
                                        ALU.subtract).then_inc(s["low_set"], 1)

            def low_to(t):
                while next_low[0] < t:
                    if not (next_low[0] in WHOLE or by_pool(next_low[0])):
                        low(next_low[0])
                    next_low[0] += 1

            def loop_low(i, t):
                if by_pool(t):
                    return
                n = split_of(t)
                dve.wait_ge(s["high_set"], i * RING + n + 1)
                nc.vector.tensor_tensor(ring_low[:, t % RING, :], ring[:, t % RING, :], w_high[:, n % HIGHS, :].bitcast(F32),
                                        ALU.subtract).then_inc(s["low_set"], 1)

            def x_low_pair(k, q, src, n):
                dve.wait_ge(s["x_high_set"], 4 * k + q + 1)
                c = slice(2 * q, 2 * q + 2)
                nc.vector.tensor_tensor(x_low[:, c, 0:n], src[:, c, 0:n], x_high[:, c, 0:n].bitcast(F32), ALU.subtract).then_inc(s["x_low_set"], 1)

            def x_lows(k, src, n):
                for q in range(4):
                    x_low_pair(k, q, src, n)

            def layer_input(k, chunk_pair, dst=normed):
                n = N1 if k < 3 else N2
                for q in range(5):
                    if q < 4:
                        chunk_pair(q).then_inc(s["normed_set"], 1)
                    if q:
                        x_low_pair(k, q - 1, dst, n)

            def pair(q):
                return range(2 * q, 2 * q + 2)

            next_ada = [0]

            def modulation(n):
                for j in range(next_ada[0], min(next_ada[0] + n, N_ADA)):
                    if j == 0:
                        dve.wait_ge(s["cond_set"], 1)
                    dve.wait_ge(ada_landed[j % 2], 16 * (j // 2 + 1))
                    w = ada_slots[j >= ADA_FIRST][:, j % 2, :]
                    if j == ADA_FIRST:
                        dve.wait_ge(s["cond_moved"], 1)
                    nc.vector.tensor_tensor_reduce(w, w, conds[j >= ADA_FIRST][:, :], 1.0, 0.0, ALU.mult, ALU.add, modv[:, j:j + 1]).then_inc(s["ada_used"], 1)
                next_ada[0] = min(next_ada[0] + n, N_ADA)

            dve.wait_ge(s["first_landed"], 16 * 5)
            low_to(LEAD)
            dve.wait_ge(s["rstd_set"], 1)
            layer_input(0, lambda q: normalise(normed1, resid, ("pre_mix", 0), pair(q), N1), normed1)
            dve.wait_ge(s["bias_summed"], 1)
            m = cst("bmask", HEADS)
            nc.vector.tensor_tensor(bias_vec[0:HEADS, 0:512], bank[4][0:HEADS, :], m[:, 0:512], ALU.add).then_inc(s["bias_vec_set"], 1)
            nc.vector.tensor_tensor(bias_vec[0:HEADS, 512:N_BIAS], bank[5][0:HEADS, 0:N_BIAS - 512], m[:, 512:N_BIAS],
                                    ALU.add).then_inc(s["bias_vec_set"], 1)
            dve.wait_ge(s["proj_evacuated"], 1)
            nc.vector.tensor_scalar(f_work[0:HEADS, 0, :], f_work[0:HEADS, 0, :], bf_sb[0:HEADS, 0:1], None, ALU.add).then_inc(s["forget_set"], 1)
            step(nc.vector.memset(f_work[0:HEADS, 4, :], 1.0))
            dve.wait_ge(s["forget_exp"], 1)
            step(nc.vector.scalar_tensor_tensor(out=f_work[0:HEADS, 3, :], in0=f_work[0:HEADS, 0, :], scalar=0.0,
                                                in1=f_work[0:HEADS, 1, :], op0=ALU.min, op1=ALU.subtract))
            settle()
            before = None
            for t in (2, 1, 0):
                c0, n = TILE_COLS[t]
                if before is not None:
                    dve.wait_ge(s["cum_set"], 2 - t)
                nc.vector.tensor_tensor_scan(f_work[0:HEADS, 5, c0:c0 + n], f_work[0:HEADS, 4, c0:c0 + n], f_work[0:HEADS, 3, c0:c0 + n],
                                             0.0 if before is None else before, ALU.mult, ALU.add).then_inc(s["cum_set"], 1)
                before = f_work[0:HEADS, 5, c0 + n - 1:c0 + n]
            low_to(2 * LEAD)
            while next_low[0] < T_V1:
                low_to(next_low[0] + 1)
                modulation(1)
            modulation(5)
            dve.wait_ge(s["bias_taken"], len(flips))
            dve.wait_ge(s["cum_turned"], 1)
            step(nc.vector.tensor_copy(cum_q[:, 0:2, :], bank[4][:, 0:2 * HEADS].rearrange("p (t h) -> p t h", h=HEADS)))
            step(nc.vector.tensor_copy(cum_q[0:META, 2, :], bank[4][0:META, 2 * HEADS:3 * HEADS]))
            settle()
            for h in range(HEADS):
                dve.wait_ge(s["cum_spread"], h + 1)
                b = bank[5 + h % 2]
                nc.vector.scalar_tensor_tensor(out=fox1[:, h, :], in0=b[:, 0:N1], scalar=cum_q[:, 0, h:h + 1], in1=cst("causal1"),
                                               op0=ALU.add, op1=ALU.add)
                nc.vector.scalar_tensor_tensor(out=fox0[:, h, :], in0=b[:, P:N1], scalar=cum_q[:, 1, h:h + 1], in1=cst("causal0"),
                                               op0=ALU.add, op1=ALU.add)
                nc.vector.scalar_tensor_tensor(out=foxm[0:META, h, :], in0=b[0:META, 2 * P:N1], scalar=cum_q[0:META, 2, h:h + 1],
                                               in1=cst("causalm", META), op0=ALU.add, op1=ALU.add).then_inc(s["fox_tables_set"], 1)
                if h % 2:
                    modulation(2)
            def add_bias(u):
                kind, g, qt = units[u]
                _, nk, _, nq = shape_of(u)
                sc = score[u % 3]
                src = psum[0:nq, 0:4, 0:nk]
                dve.wait_ge(s["scores_done"], u + 1)
                if u >= 3:
                    dve.wait_ge(s["probs_turned"], u - 2)
                if has_sink(u):
                    at = VEC["sinks1" if kind == 0 else "sinks2"][0] + 4 * g
                    step(nc.vector.tensor_copy(sc[0:nq, :, nk:nk + 1], vec[0:nq, at:at + 4].unsqueeze(2)))
                    settle()
                if kind == 3:
                    ins = nc.vector.tensor_copy(sc[0:nq, :, 0:nk], src)
                else:
                    if kind == 2:
                        table = cst(f"band{1 - qt}").unsqueeze(1).broadcast_to([P, 4, N2])
                    else:
                        table = ((bias1, bias0, biasm), (fox1, fox0, foxm))[kind][qt][0:nq, 4 * g:4 * g + 4, :]
                    ins = nc.vector.tensor_tensor(sc[0:nq, :, 0:nk], src, table, ALU.add)
                ins.then_inc(s["scores_read"], 1)
                dve.wait_ge(s["scores_read"], u + 1)
                n = nk + has_sink(u)
                st = stats[u % 2]
                step(nc.vector.tensor_reduce(st[0:nq, 0:4], sc[0:nq, :, 0:n], AX_X, ALU.max))
                settle()
                nc.vector.tensor_scalar(st[0:nq, 4:8], st[0:nq, 0:4], -1.0, None, ALU.mult).then_inc(s["max_set"], 1)

            def divide(u):
                _, nk, _, nq = shape_of(u)
                st = stats[u % 2]
                dve.wait_ge(s["exp_done"], u + 1)
                step(nc.vector.reciprocal(st[0:nq, 12:16], st[0:nq, 8:12]))
                settle()
                nc.vector.tensor_tensor(score[u % 3][0:nq, :, 0:nk], score[u % 3][0:nq, :, 0:nk],
                                        st[0:nq, 12:16].unsqueeze(2).broadcast_to([nq, 4, nk]), ALU.mult).then_inc(s["probs_set"], 1)

            def take_mixed(u):
                kind, g, _ = units[u]
                _, _, q0, nq = shape_of(u)
                dve.wait_ge(s["attended"], u + 1)
                c = 4 * (kind % 2) + 2 * g
                nc.vector.tensor_copy(mixed[:, c:c + 2, q0:q0 + nq],
                                      bank[7][:, 0:2 * P].rearrange("p (c q) -> p c q", q=P)[:, :, 0:nq]).then_inc(s["mixed_set"], 1)

            def attention(u0, u1):
                for u in range(u0, u1 + 3):
                    if u < u1:
                        add_bias(u)
                    if u0 < u < u1 + 1:
                        divide(u - 1)
                        if next_ada[0] < ADA_FIRST:
                            modulation(1)
                    if u > u0 + 2:
                        take_mixed(u - 3)

            def add_normed(gain):
                for q in range(5):
                    if q < 4:
                        step(normalise(lin_out, lin_out, (gain, 0), pair(q), N1))
                    if q:
                        dve.wait_ge(s["vector_step"], steps[0] - (q < 4))
                        c = slice(2 * q - 2, 2 * q)
                        nc.vector.tensor_tensor(resid[:, c, :], resid[:, c, :], lin_out[:, c, :], ALU.add).then_inc(s["resid_set"], 1)

            low_to(T_OUT1 + LEAD)
            attention(0, len(units1))
            x_lows(1, mixed, N1)
            low_to(T_FFN + LEAD)
            dve.wait_ge(s["rstd_set"], 2)
            add_normed("post_mix")
            dve.wait_ge(s["rstd_set"], 3)
            layer_input(2, lambda q: normalise(normed, resid, ("pre_ffn", 0), pair(q), N1))

            def ffn_lows(j, at, k):
                dve.wait_ge(s["ffn_high_set"], j + 1)
                nc.vector.tensor_tensor(ffn_low[:, at, :], silu_sb[:, k:k + 1, :], ffn_high[:, at, :].bitcast(F32), ALU.subtract).then_inc(s["ffn_low_set"], 1)

            def gate_pair(i, k):
                j = i * 4 + k
                unrolled = isinstance(i, int)
                for d in (0, 1):
                    loop_low(i, T_FFN + 2 * k + LEAD + d)
                dve.wait_ge(s["silu_set"], j + 1)
                nc.vector.tensor_tensor(silu_sb[:, k, :], silu_sb[:, k, :], bank[2 * k + 1][:, 0:N1], ALU.mult).then_inc(s["ffn_act_set"], 1)
                if not (unrolled and j == 0):
                    ffn_lows(j - 1, slice(j - 1, j) if unrolled else bass.ds(j - 1, 1), (k - 1) % 4)

            for k in range(4):
                gate_pair(0, k)
                modulation(1)
            with dve.Fori(1, FC // 4) as i:
                for k in range(4):
                    gate_pair(i, k)
            for k in range(FC % 4):
                gate_pair(FC // 4, k)
                modulation(1)
            ffn_lows(FC - 1, slice(FC - 1, FC), (FC - 1) % 4)
            next_low[0] = T_DOWN + LEAD
            while next_low[0] < T_QK2 + LEAD:
                low_to(next_low[0] + 1)
                modulation(1)
            b0 = VEC["b_ada"][0]
            dve.wait_ge(s["ada_used"], N_ADA)
            step(nc.vector.tensor_tensor(modv[:, :], modv[:, :], vec[:, b0:b0 + 6 * DC], ALU.add))
            settle()
            for k in (1, 4):
                ins = nc.vector.tensor_scalar(modv[:, k * DC:(k + 1) * DC], modv[:, k * DC:(k + 1) * DC], 1.0, None, ALU.add)
            step(ins)
            dve.wait_ge(s["rstd_set"], 4)
            add_normed("post_ffn")

            def modulate(n, k, scale_at, shift_at):
                for q in range(5):
                    if q < 4:
                        for c in pair(q):
                            nc.vector.scalar_tensor_tensor(out=normed[:, c, 0:N2], in0=resid[:, c, 0:N2],
                                                           scalar=modv[:, scale_at + c:scale_at + c + 1],
                                                           in1=rstd[:, 0:N2], op0=ALU.mult, op1=ALU.mult).then_inc(s["modulated"], 1)
                    if q:
                        dve.wait_ge(s["x_high_set"], 4 * k + q)
                        for c in pair(q - 1):
                            ins = nc.vector.scalar_tensor_tensor(out=x_low[:, c, 0:N2], in0=normed[:, c, 0:N2],
                                                                 scalar=modv[:, shift_at + c:shift_at + c + 1],
                                                                 in1=x_high[:, c, 0:N2].bitcast(F32), op0=ALU.add, op1=ALU.subtract)
                        ins.then_inc(s["x_low_set"], 1)

            dve.wait_ge(s["rstd_set"], 5)
            modulate(0, 3, DC, 0)
            low_to(T_QK2 + 7)
            cos, sin = (cst(n).unsqueeze(1).broadcast_to([P, 5, N2]) for n in ("cos64", "sin64"))
            dve.wait_ge(s["second_block_landed"], 2 * 16)
            dve.wait_ge(s["proj_evacuated"], R_QK2 + 5)
            step(nc.vector.tensor_tensor(rope_q[:, 0:5, :], qk[:, 0:5, 0:N2], cos, ALU.mult))
            low_to(T_QK2 + 8)
            dve.wait_ge(s["rot_done"], 1)
            step(nc.vector.tensor_tensor(rope_tmp2[:, 0:5, :], flat[:, 2048:2048 + 5 * N2].rearrange("p (a n) -> p a n", n=N2), sin, ALU.mult))
            low_to(T_QK2 + N_QK2)
            settle()
            nc.vector.tensor_tensor(rope_q[:, 0:5, :], rope_q[:, 0:5, :], rope_tmp2[:, 0:5, :], ALU.add).then_inc(s["rope_set"], 1)
            dve.wait_ge(s["rstd_set"], 6)
            normalise(normed, qk[:, 5:7, :], ("q_norm", 0), range(QR_C), N2).then_inc(s["normed_set"], 1)
            dve.wait_ge(s["rstd_set"], 7)
            nc.vector.scalar_tensor_tensor(out=normed[:, 2, 0:N2], in0=qk[:, 7, 0:N2], scalar=vcol("kv_norm"), in1=rstds[1][:, 0:N2],
                                           op0=ALU.mult, op1=ALU.mult).then_inc(s["normed_set"], 1)
            dve.wait_ge(s["rope_set"], 1)
            rr = slice(NOPE, QK)
            dve.wait_ge(s["rot_done"], 2)
            step(nc.vector.tensor_tensor(rope_tmp2[rr, 0, :], bank[6][rr, N2:2 * N2], cst("sin32")[rr, :], ALU.mult))
            step(nc.vector.tensor_tensor(rope_tmp2[rr, 1, :], qk[rr, 8, 0:N2], cst("cos32")[rr, :], ALU.mult))
            settle()
            nc.vector.tensor_tensor(rope_tmp2[rr, 5, :], rope_tmp2[rr, 0, :], rope_tmp2[rr, 1, :], ALU.add).then_inc(s["rope_set"], 1)
            dve.wait_ge(s["rope_set"], 2)
            dve.wait_ge(s["normed_set"], 10)
            nc.vector.tensor_copy(k_mla[rr, :, :], rope_tmp2[rr, 5:6, :].broadcast_to([ROPE, HEADS, N2])).then_inc(s["k_rope_set"], 1)
            cos, sin = (cst(n)[rr, :].unsqueeze(1).broadcast_to([ROPE, 4, N2]) for n in ("cos32", "sin32"))
            for half in range(2):
                h = slice(4 * half, 4 * half + 4)
                dve.wait_ge(s["mla_up_set"], half + 1)
                step(nc.vector.tensor_tensor(lin_out[rr, h, 0:N2], q_mla[rr, h, :], cos, ALU.mult))
            dve.wait_ge(s["k_rope_set"], 1)
            for half in range(2):
                h = slice(4 * half, 4 * half + 4)
                dve.wait_ge(s["rot_done"], half + 3)
                src = flat[rr, 2048 * (1 - half):2048 * (1 - half) + 1024].rearrange("p (a n) -> p a n", n=N2)
                step(nc.vector.tensor_tensor(rope_tmp2[rr, h, :], src, sin, ALU.mult))
                settle()
                nc.vector.tensor_tensor(q_mla[rr, h, :], lin_out[rr, h, 0:N2], rope_tmp2[rr, h, :], ALU.add).then_inc(s["rope_set"], 1)
            low_to(T_OUT2 + LEAD)
            attention(len(units1), len(units))
            dve.wait_ge(s["rstd_set"], 9)
            layer_input(4, lambda q: normalise(normed, mixed, ("out_norm", 0), pair(q), N2, rstds[q // 2]))
            for j in range(DC):
                r = R_OUT2 + j
                low_to(T_OUT2 + j + 1 + LEAD)
                dve.wait_ge(s["tile_used"], T_OUT2 + j + 1)
                ins = nc.vector.scalar_tensor_tensor(out=resid[:, j, 0:N2], in0=bank[r % 4][:, 0:N2], scalar=modv[:, 2 * DC + j:2 * DC + j + 1],
                                                     in1=resid[:, j, 0:N2], op0=ALU.mult, op1=ALU.add)
                ins.then_inc(s["proj_evacuated"], 1)
            dve.wait_ge(s["rstd_set"], 10)
            modulate(1, 5, 4 * DC, 3 * DC)
            low_to(T_UP + LEAD)

            since = [0]
            PACE = 1700
            before_gates = T_UP + HALF - RING + LEAD

            def relief(columns):
                since[0] += columns + 60
                if since[0] > PACE and next_low[0] < before_gates:
                    since[0] -= PACE
                    low_to(next_low[0] + 1)

            def top16(src, other, values, where, n):
                for a in range(n):
                    step(nc.vector.max(values[:, a, 0:8], src[:, a, :]))
                    relief(src.shape[2])
                settle()
                for a in range(n):
                    step(nc.vector.max_index(where[:, a, 0:8].bitcast(U32), values[:, a, 0:8], src[:, a, :]))
                    relief(src.shape[2])
                for a in range(n):
                    step(nc.vector.match_replace(other[:, a, :], values[:, a, 0:8], src[:, a, :], LOWEST))
                    relief(src.shape[2])
                settle()
                for a in range(n):
                    step(nc.vector.max(values[:, a, 8:16], other[:, a, :]))
                    relief(src.shape[2])
                settle()
                for a in range(n):
                    step(nc.vector.max_index(where[:, a, 8:16].bitcast(U32), values[:, a, 8:16], other[:, a, :]))
                    relief(src.shape[2])
                settle()

            grid = [P, HEADS, TOPK, TOPK]
            iota16 = iota[:, 0:TOPK].unsqueeze(1).unsqueeze(1).broadcast_to(grid)
            dve.wait_ge(s["keys_evacuated"], 2)
            for tt in range(2):
                top16(keys_s[:, tt], spare, top_v, top_i, 16)
                step(nc.vector.tensor_copy(top_if[:, :, :], top_i[:, :, :].bitcast(U32)))
                tv = top_v[:, :, :].rearrange("p (h a) k -> p h a k", a=2)
                step(nc.vector.tensor_tensor(cand[:, :, :].rearrange("p h (a b) -> p h a b", b=TOPK),
                                             tv[:, :, 0, :].unsqueeze(3).broadcast_to(grid),
                                             tv[:, :, 1, :].unsqueeze(2).broadcast_to(grid), ALU.add))
                settle()
                top16(cand, cand2, best_v, best_i, HEADS)

                def pairs(k):
                    return choice[:, k, tt, :].rearrange("p (h k) -> p h k", k=TOPK)

                step(nc.vector.tensor_tensor(pairs(2), best_v[:, :, :], best_v[:, :, 0:1].broadcast_to([P, HEADS, TOPK]), ALU.subtract))
                tif = top_if[:, :, :].rearrange("p (h a) k -> p h a k", a=2)
                h4 = cand2[:, :, :].rearrange("p h (a b) -> p h a b", b=TOPK)
                for a, (op, by) in enumerate(((ALU.logical_shift_right, 4), (ALU.bitwise_and, 15))):
                    step(nc.vector.tensor_scalar(best_a[:, :, :].bitcast(U32), best_i[:, :, :].bitcast(U32), by, None, op))
                    settle()
                    step(nc.vector.tensor_copy(best_f[:, :, :], best_a[:, :, :].bitcast(U32)))
                    settle()
                    step(nc.vector.tensor_tensor(h4, best_f[:, :, :].unsqueeze(3).broadcast_to(grid), iota16, ALU.is_equal))
                    settle()
                    relief(HEADS * TOPK * TOPK)
                    step(nc.vector.tensor_tensor(h4, h4, tif[:, :, a, :].unsqueeze(2).broadcast_to(grid), ALU.mult))
                    settle()
                    relief(HEADS * TOPK * TOPK)
                    ins = nc.vector.tensor_reduce(pairs(a), h4, AX_X, ALU.add)
                    if (tt, a) == (1, 1):
                        ins.then_inc(s["topk_set"], 1)
                        break
                    step(ins)
                    settle()
                    relief(HEADS * TOPK * TOPK)
            low_to(before_gates)
            dve.wait_ge(s["gate_exp_set"], 1)
            exps = choice[:, 2].rearrange("p a (h k) -> p (a h) k", k=TOPK)
            step(nc.vector.tensor_reduce(gate_sum[:, :], exps, AX_X, ALU.add))
            settle()
            step(nc.vector.reciprocal(gate_sum[:, :], gate_sum[:, :]))
            settle()
            nc.vector.tensor_tensor(exps, exps, gate_sum[:, :].unsqueeze(2).broadcast_to([P, 2 * HEADS, TOPK]), ALU.mult).then_inc(s["gates_ready"], 1)
            low_to(T_UP + HALF + LEAD)

            dve.wait_ge(s["choice_t_set"], 1)
            gates = choice_t[:, 2, :]
            for part in range(3):
                ins = nc.vector.tensor_copy(gate_parts[:, part, :], gates)
                if part < 2:
                    step(ins)
                    settle()
                    step(nc.vector.tensor_tensor(gates, gates, gate_parts[:, part, :], ALU.subtract))
                    settle()
            ins.then_inc(s["gate_parts_set"], 1)

            def hot_rows(n, g, b, place, first=0):
                def chosen(kind, width):
                    return choice_t[:, kind, bass.ds(g * GROUP, GROUP)].unsqueeze(2).broadcast_to([P, GROUP, width])

                if not isinstance(n, int) or n >= 2:
                    dve.wait_ge(s["gates_done"], n - 1)
                nc.vector.tensor_tensor(hot1[place][:, b], iota[:, first:first + HALF].unsqueeze(1).broadcast_to([P, GROUP, HALF]),
                                        chosen(0, HALF), ALU.is_equal).then_inc(s["hot1_set"], 1)
                nc.vector.tensor_tensor(hot2[place][:, b], iota[:, :].unsqueeze(1).broadcast_to([P, GROUP, KEYS]), chosen(1, KEYS),
                                        ALU.is_equal).then_inc(s["hot2_set"], 1)

            def apply_gates(n, g, b, first, late=0):
                dve.wait_ge(s["gates_done"], n + 1)
                a = acts[:, first:first + HALF, bass.ds(g * GROUP, GROUP)]
                nc.vector.tensor_tensor(a, a, bank[4 * late + b][:, 0:GROUP * HALF].rearrange("p (t n) -> p n t", n=HALF), ALU.mult).then_inc(s["gates_used"], 1)

            for k in range(RING):
                loop_low(0, T_UP + HALF + k + LEAD)
                hot_rows(k, k, k % 2, 0)
                if k >= 2:
                    apply_gates(k - 2, k - 2, k % 2, 0)
            with dve.Fori(1, HALF // RING) as i:
                for k in range(RING):
                    loop_low(i - 1, T_UP + HALF + RING + k + LEAD)
                    hot_rows(i * RING + k, i * RING + k, k % 2, 0)
                    apply_gates(i * RING + (k - 2), i * RING + (k - 2), k % 2, 0)
            for n in range(GROUPS - 2, GROUPS):
                apply_gates(n, n, n % 2, 0)

            def picked_low(e, at, k):
                dve.wait_ge(s["picked_high_set"], e + 1)
                nc.vector.tensor_tensor(x_low[:, k:k + 1, 0:N2], acts[:, at, :], x_high[:, k:k + 1, 0:N2].bitcast(F32),
                                        ALU.subtract).then_inc(s["picked_low_set"], 1)

            for e in range(LEAD):
                picked_low(e, slice(e, e + 1), e % 4)
            dve.wait_ge(s["gelu_set"], KEYS)
            for k in range(RING):
                loop_low(0, T_DOWN_E + k + LEAD)
                picked_low(k + LEAD, slice(k + LEAD, k + LEAD + 1), (k + LEAD) % 4)
                hot_rows(GROUPS + k, k, k % 2, 1, HALF)
                if k >= 2:
                    apply_gates(GROUPS + k - 2, k - 2, k % 2, HALF, 1)
            with dve.Fori(1, HALF // RING - 1) as i:
                for k in range(RING):
                    loop_low(i, T_DOWN_E + k + LEAD)
                    e = i * RING + k + LEAD
                    picked_low(e, bass.ds(e, 1), (k + LEAD) % 4)
                    hot_rows(i * RING + (GROUPS + k), i * RING + k, k % 2, 1, HALF)
                    apply_gates(i * RING + (GROUPS + k - 2), i * RING + (k - 2), k % 2, HALF, 1)
            for e in range(HALF - RING, HALF):
                loop_low(0, T_DOWN_E + e + LEAD)
                if e + LEAD < HALF:
                    picked_low(e + LEAD, slice(e + LEAD, e + LEAD + 1), (e + LEAD) % 4)
                hot_rows(GROUPS + e, e, e % 2, 1, HALF)
                apply_gates(GROUPS + e - 2, e - 2, e % 2, HALF, 1)
            for n in range(GROUPS - 2, GROUPS):
                apply_gates(GROUPS + n, n, n % 2, HALF, 1)
            for e in range(HALF, HALF + LEAD):
                picked_low(e, slice(e, e + 1), e % 4)
            with dve.Fori(HALF // RING, KEYS // RING - 1) as i:
                for k in range(RING):
                    loop_low(i, T_DOWN_E + k + LEAD)
                    e = i * RING + k + LEAD
                    picked_low(e, bass.ds(e, 1), (k + LEAD) % 4)
            for e in range(KEYS - RING + LEAD, KEYS):
                loop_low(0, T_DOWN_E + e)
                picked_low(e, slice(e, e + 1), e % 4)
            dve.wait_ge(s["tile_used"], T_END)
            for c in range(DC):
                ins = nc.vector.scalar_tensor_tensor(out=resid[:, c, 0:N2], in0=flat[:, c * N2:(c + 1) * N2],
                                                     scalar=modv[:, 5 * DC + c:5 * DC + c + 1], in1=resid[:, c, 0:N2],
                                                     op0=ALU.mult, op1=ALU.add)
                if c % 2:
                    ins.then_inc(s["resid_set"], 1)
            dve.wait_ge(s["rstd_set"], 11)
            for q in range(4):
                normalise(lin_out, resid, ("final", 0), pair(q), N2).then_inc(s["final_set"], 1)


def tiles_of(w):
    k, m = w.shape
    return w.reshape(k // P, P, m // P, P).transpose(2, 1, 0, 3).reshape(m // P, P, k)


def column(v):
    return v.reshape(-1, P).T


def kernel(x, meta_tokens, rel_bias, ln_pre_mix, ln_post_mix, ln_pre_ffn, ln_post_ffn, w_in, b_forget,
           sinks, w_out, w_gate_up, w_down, c_2, w_ada_2, b_ada_2, w_in_2, swa_sink_2, mla_q_norm_2,
           w_mla_q_up_2, mla_kv_norm_2, w_mla_kv_up_2, out_norm_swa_2, out_norm_mla_2, w_out_2,
           w_peer_query_2, peer_sub_keys_2, peer_expert_u_2, peer_expert_v_2, final_norm_2):
    import concourse.bacc as bacc
    from concourse.bass_utils import run_bass_kernel_spmd

    cat = np.concatenate
    swa = np.array([h * DH + i for h in SLOT_HEAD for i in range(DH)])

    tokens = cat([x[0, P:], x[0, :P], meta_tokens], 0)
    x_t = np.ascontiguousarray(tokens.T.reshape(DC, P, N1).transpose(1, 0, 2))

    w1 = w_in[0]
    q_a, k_a, v_a, q_b, k_b, v_b, f_b = np.split(w1, [512, 640, 768, 1280, 1792, 2304], axis=1)
    w2 = w_in_2[0]
    q_2, k_2, v_2, q_lat, kv_lat, k_rope = np.split(w2, [512, 640, 768, 1024, 1152], axis=1)
    gate_up = w_gate_up[0].reshape(D, 2, FC, P).transpose(0, 2, 1, 3).reshape(D, 2 * FF)
    down = w_down[0].reshape(FC, P, DC, P).transpose(2, 0, 1, 3).reshape(FC, DC, P, P).transpose(0, 2, 1, 3).reshape(FC, P, D)
    out1 = cat([w_out[0][:512][swa], w_out[0][512:]], 0)
    out2 = cat([w_out_2[0][:512][swa], w_out_2[0][512:]], 0)
    sub = peer_sub_keys_2[0].reshape(2, 8, KEYS, P).transpose(0, 3, 1, 2).reshape(2, P, D)
    weights = cat([
        tiles_of(cat([q_a[:, swa], k_a, q_b, k_b, v_a, v_b], 1)),
        tiles_of(out1), tiles_of(gate_up), down,
        tiles_of(cat([q_2[:, swa], k_2, q_lat, kv_lat, k_rope, k_rope, k_rope, k_rope, v_2], 1)),
        tiles_of(out2), tiles_of(w_peer_query_2[0]), sub,
    ], 0)
    up_experts = peer_expert_u_2[0].reshape(KEYS, KEYS, DC, P).transpose(0, 3, 2, 1).reshape(KEYS, P, D)
    down_experts = peer_expert_v_2[0].reshape(KEYS, KEYS, D)
    small = cat([w_mla_q_up_2[0].reshape(QR_C, P, HEADS * QK).transpose(1, 0, 2).reshape(P, -1), w_mla_kv_up_2[0]], 1)
    slots = np.array(SLOT_HEAD)
    vectors = cat([
        column(ln_pre_mix[0]), column(ln_post_mix[0]), column(ln_pre_ffn[0]), column(ln_post_ffn[0]), column(b_ada_2[0]),
        column(mla_q_norm_2[0]), column(mla_kv_norm_2[0]), column(out_norm_swa_2[0][swa]), column(out_norm_mla_2[0]),
        column(final_norm_2),
        np.broadcast_to(sinks[0][slots], (P, HEADS)), np.broadcast_to(swa_sink_2[0][slots], (P, HEADS)),
    ], 1)
    arrays = {
        "x_t": x_t, "weights": weights, "w_ada": w_ada_2[0].T.reshape(N_ADA, P, D), "cond_row": c_2[0], "up_experts": up_experts, "down_experts": down_experts, "small": small,
        "vectors": vectors, "w_f": f_b.reshape(DC, P, HEADS).transpose(1, 0, 2), "b_f": b_forget.reshape(HEADS, 1),
        "rel": rel_bias[:, slots], "const": shape_constants(),
    }
    arrays = {n: np.ascontiguousarray(a) for n, a in arrays.items()}
    nc = bacc.Bacc("TRN2", target_bir_lowering=False, num_devices=1)
    aps = {n: nc.dram_tensor(n, a.shape, F32, kind="ExternalInput").ap() for n, a in arrays.items()}
    scratch = nc.dram_tensor("bias_scratch", [HEADS, N_BIAS], F32, kind="Internal").ap()
    out = nc.dram_tensor("out_t", [P, DC, N2], F32, kind="ExternalOutput").ap()
    build(nc, *[aps[n] for n in ("x_t", "weights", "w_ada", "cond_row", "up_experts", "down_experts", "small", "vectors", "w_f", "b_f", "rel", "const")],
          scratch, out)
    got = run_bass_kernel_spmd(nc, [arrays], core_ids=[0]).results[0]["out_t"]
    got = got.transpose(2, 1, 0).reshape(N2, D)
    return np.ascontiguousarray(cat([got[P:], got[:P]], 0)[None])
```
